# Optimizing a Trainium2 kernel written in Bass

```python
import numpy as np
import jax
import jax.numpy as jnp
from jax import lax

D_MODEL = 1024
BATCH = 1
SEQ = 512
DEPTH = 2

N_MEM = 256
EPS = 1e-6
ROPE_THETA = 10000.0
QB = 128

NSA_HEADS = 8
NSA_KV = 2
NSA_HPG = NSA_HEADS // NSA_KV
HEAD_DIM = 64
CMP_LEN = 32
CMP_STRIDE = 16
SLC_LEN = 64
SLC_TOPN = 8
WINDOW = 256
FORCE_BONUS = 1000.0

GLA_HEADS = 4
GLA_DK = 64
GLA_DV = 128
GLA_RANK = 16
GLA_TAU = 16.0
GLA_CHUNK = 64

SG_CHUNK = 128
SG_GROUPS = 8
SG_WIDTH = 2 * D_MODEL
SG_GW = SG_WIDTH // SG_GROUPS

X_HEADS = 4
X_HD = D_MODEL // X_HEADS

N_EXPERTS = 16
N_GROUPS = 4
EPG = N_EXPERTS // N_GROUPS
TOP_K = 2
D_EXPERT = 384

N_EVEN = (DEPTH + 1) // 2
N_ODD = DEPTH // 2

NSA_QW = NSA_HEADS * HEAD_DIM
NSA_KVW = NSA_KV * HEAD_DIM
GLA_QKW = GLA_HEADS * GLA_DK
GLA_VW = GLA_HEADS * GLA_DV
HYB_SIZES = (NSA_QW, NSA_KVW, NSA_KVW, NSA_KVW, NSA_KVW, NSA_KVW, NSA_KVW, 3 * NSA_HEADS,
             GLA_QKW, GLA_QKW, GLA_VW, GLA_RANK, GLA_VW)
HYB_IN = sum(HYB_SIZES)
HYB_SPLITS = tuple(int(s) for s in np.cumsum(HYB_SIZES)[:-1])
HYB_OUT = NSA_QW + GLA_VW

kernel_name = 'hybrid_nsa_gla_sgu_xmem_moe'

def rmsnorm(x, g):
    xf = x.astype(jnp.float32)
    y = xf * lax.rsqrt(jnp.mean(xf * xf, axis=-1, keepdims=True) + EPS)
    return (y * g.astype(jnp.float32)).astype(x.dtype)

def layernorm(x, g, b):
    xf = x.astype(jnp.float32)
    xc = xf - jnp.mean(xf, axis=-1, keepdims=True)
    y = xc * lax.rsqrt(jnp.mean(xc * xc, axis=-1, keepdims=True) + EPS)
    return (y * g.astype(jnp.float32) + b.astype(jnp.float32)).astype(x.dtype)

def rope(x, pos):
    half = x.shape[-1] // 2
    freq = ROPE_THETA ** (-jnp.arange(half, dtype=jnp.float32) / half)
    ang = pos.astype(jnp.float32)[..., None] * freq
    cos = jnp.cos(ang)[:, :, None, :]
    sin = jnp.sin(ang)[:, :, None, :]
    xf = x.astype(jnp.float32)
    x1, x2 = xf[..., :half], xf[..., half:]
    return jnp.concatenate([x1 * cos - x2 * sin, x2 * cos + x1 * sin], axis=-1).astype(x.dtype)

def masked_softmax(s, mask):
    s = jnp.where(mask, s.astype(jnp.float32), -jnp.inf)
    m = jnp.max(s, axis=-1, keepdims=True)
    m = jnp.where(jnp.isfinite(m), m, 0.0)
    p = jnp.exp(s - m)
    return p / jnp.maximum(jnp.sum(p, axis=-1, keepdims=True), 1e-30)

def nsa_mixer(q, k_cmp, v_cmp, k_slc, v_slc, k_win, v_win, gate_logit, positions,
              q_g, k_g, cmp_pe, cmp_w1, cmp_w2, gate_b):
    B, S = q.shape[:2]
    scale = HEAD_DIM ** -0.5
    q = rope(rmsnorm(q.reshape(B, S, NSA_HEADS, HEAD_DIM), q_g), positions)
    q = q.reshape(B, S, NSA_KV, NSA_HPG, HEAD_DIM)
    kvr = lambda t: t.reshape(B, S, NSA_KV, HEAD_DIM)
    t_idx = np.arange(S)
    nqb = S // QB

    n_cmp = (S - CMP_LEN) // CMP_STRIDE + 1
    blk_idx = np.arange(n_cmp)[:, None] * CMP_STRIDE + np.arange(CMP_LEN)[None, :]
    blk_end = blk_idx[:, -1]

    def compress(t, pe, w1, w2):
        blk = kvr(t)[:, blk_idx] + pe[:, None, :]
        blk = blk.transpose(0, 1, 3, 2, 4).reshape(B, n_cmp, NSA_KV, CMP_LEN * HEAD_DIM)
        return jax.nn.gelu(blk @ w1) @ w2

    kc = compress(k_cmp, cmp_pe[0], cmp_w1[0], cmp_w2[0])
    vc = compress(v_cmp, cmp_pe[1], cmp_w1[1], cmp_w2[1])
    kc = rope(rmsnorm(kc, k_g[0]), positions[:, blk_end])
    mask_c = jnp.asarray(blk_end[None, :] <= t_idx[:, None])
    p_c = masked_softmax(jnp.einsum('bsghd,bcgd->bghsc', q, kc) * scale, mask_c)
    o_c = jnp.einsum('bghsc,bcgd->bsghd', p_c.astype(vc.dtype), vc)

    n_slc = S // SLC_LEN
    top_n = min(SLC_TOPN, n_slc)
    cs = np.arange(n_cmp) * CMP_STRIDE
    ss = np.arange(n_slc) * SLC_LEN
    overlap = np.clip(np.minimum(cs[:, None] + CMP_LEN, ss[None, :] + SLC_LEN)
                      - np.maximum(cs[:, None], ss[None, :]), 0, None).astype(np.float32) / CMP_LEN
    imp = jnp.einsum('bghsc,cj->bgsj', p_c, jnp.asarray(overlap))
    cur = (t_idx // SLC_LEN)[:, None]
    jb = np.arange(n_slc)[None, :]
    valid = jnp.asarray(jb <= cur)
    forced = jnp.asarray((jb == 0) | (jb == cur) | (jb == cur - 1))
    score = jnp.where(valid, imp + jnp.where(forced, FORCE_BONUS, 0.0), -jnp.inf)
    top_val, top_idx = lax.top_k(score, top_n)
    top_ok = jnp.isfinite(top_val)
    ks = rope(rmsnorm(kvr(k_slc), k_g[1]), positions)
    kb = ks.reshape(B, n_slc, SLC_LEN, NSA_KV, HEAD_DIM).transpose(0, 3, 1, 2, 4)
    vb = kvr(v_slc).reshape(B, n_slc, SLC_LEN, NSA_KV, HEAD_DIM).transpose(0, 3, 1, 2, 4)
    bi = jnp.arange(B)[:, None, None, None]
    gi = jnp.arange(NSA_KV)[None, :, None, None]

    def slc_block(args):
        qb, ib, okb, tb = args
        kg = kb[bi, gi, ib].reshape(B, NSA_KV, QB, top_n * SLC_LEN, HEAD_DIM)
        vg = vb[bi, gi, ib].reshape(B, NSA_KV, QB, top_n * SLC_LEN, HEAD_DIM)
        kpos = ib[..., None] * SLC_LEN + jnp.arange(SLC_LEN)
        m = (okb[..., None] & (kpos <= tb[None, None, :, None, None])).reshape(B, NSA_KV, QB, top_n * SLC_LEN)
        p = masked_softmax(jnp.einsum('bqghd,bgqkd->bgqhk', qb, kg) * scale, m[:, :, :, None, :])
        return jnp.einsum('bgqhk,bgqkd->bqghd', p.astype(vg.dtype), vg)

    q_blk = q.reshape(B, nqb, QB, NSA_KV, NSA_HPG, HEAD_DIM).transpose(1, 0, 2, 3, 4, 5)
    i_blk = top_idx.reshape(B, NSA_KV, nqb, QB, top_n).transpose(2, 0, 1, 3, 4)
    ok_blk = top_ok.reshape(B, NSA_KV, nqb, QB, top_n).transpose(2, 0, 1, 3, 4)
    t_blk = jnp.arange(S, dtype=jnp.int32).reshape(nqb, QB)
    o_s = lax.map(slc_block, (q_blk, i_blk, ok_blk, t_blk))
    o_s = o_s.transpose(1, 0, 2, 3, 4, 5).reshape(B, S, NSA_KV, NSA_HPG, HEAD_DIM)

    nwb = WINDOW // QB
    kwin = (nwb + 1) * QB

    def band(t):
        tp = jnp.pad(t, ((0, 0), (WINDOW, 0), (0, 0), (0, 0))).reshape(B, nqb + nwb, QB, NSA_KV, HEAD_DIM)
        return jnp.concatenate([tp[:, j:j + nqb] for j in range(nwb + 1)], axis=2)

    kw = band(rope(rmsnorm(kvr(k_win), k_g[2]), positions))
    vw = band(kvr(v_win))
    kpos = np.arange(nqb)[:, None, None] * QB - WINDOW + np.arange(kwin)[None, None, :]
    tq = t_idx.reshape(nqb, QB)[:, :, None]
    mask_w = jnp.asarray((kpos >= 0) & (kpos <= tq) & (kpos > tq - WINDOW))
    qw = q.reshape(B, nqb, QB, NSA_KV, NSA_HPG, HEAD_DIM)
    p_w = masked_softmax(jnp.einsum('bnqghd,bnkgd->bnghqk', qw, kw) * scale, mask_w[None, :, None, None])
    o_w = jnp.einsum('bnghqk,bnkgd->bnqghd', p_w.astype(vw.dtype), vw).reshape(B, S, NSA_KV, NSA_HPG, HEAD_DIM)

    g = jax.nn.sigmoid(gate_logit + gate_b).reshape(B, S, NSA_KV, NSA_HPG, 3)
    o = g[..., 0:1] * o_c + g[..., 1:2] * o_s + g[..., 2:3] * o_w
    return o.reshape(B, S, NSA_QW)

def gla_mixer(q, k, v, a_low, r, wa2, ba, o_g):
    B, S = q.shape[:2]
    f32 = jnp.float32
    q = q.reshape(B, S, GLA_HEADS, GLA_DK).astype(f32) * (GLA_DK ** -0.5)
    k = k.reshape(B, S, GLA_HEADS, GLA_DK).astype(f32)
    v = v.reshape(B, S, GLA_HEADS, GLA_DV).astype(f32)
    log_a = (jax.nn.log_sigmoid((a_low @ wa2 + ba).astype(f32)) / GLA_TAU).reshape(B, S, GLA_HEADS, GLA_DK)
    n_ch = S // GLA_CHUNK

    def chunks(t):
        return t.reshape(B, n_ch, GLA_CHUNK, *t.shape[2:]).swapaxes(0, 1)

    tri = jnp.tril(jnp.ones((GLA_CHUNK, GLA_CHUNK), dtype=bool))[None, :, :, None, None]

    def step(state, xs):
        qc, kc, vc, gc = xs
        b = jnp.cumsum(gc, axis=1)
        o_inter = jnp.einsum('bchk,bhkv->bchv', qc * jnp.exp(b), state)
        diff = b[:, :, None] - b[:, None, :]
        decay = jnp.where(tri, jnp.exp(jnp.where(tri, diff, 0.0)), 0.0)
        att = jnp.einsum('bihd,bjhd,bijhd->bhij', qc, kc, decay)
        o_intra = jnp.einsum('bhij,bjhv->bihv', att, vc)
        b_last = b[:, -1]
        state = jnp.exp(b_last)[..., None] * state + jnp.einsum(
            'bjhk,bjhv->bhkv', kc * jnp.exp(b_last[:, None] - b), vc)
        return state, o_inter + o_intra

    state0 = jnp.zeros((B, GLA_HEADS, GLA_DK, GLA_DV), f32)
    _, o = lax.scan(step, state0, (chunks(q), chunks(k), chunks(v), chunks(log_a)))
    o = o.swapaxes(0, 1).reshape(B, S, GLA_HEADS, GLA_DV)
    o = rmsnorm(o, o_g).reshape(B, S, GLA_VW)
    return (o * jax.nn.silu(r.astype(f32))).astype(r.dtype)

def sgu_mixer(h, w_in, ln_g, ln_b, ws, bs, w_out):
    B, S = h.shape[:2]
    z = jax.nn.gelu(h @ w_in)
    u, v = z[..., :SG_WIDTH], z[..., SG_WIDTH:]
    v = layernorm(v, ln_g, ln_b).reshape(B, S // SG_CHUNK, SG_CHUNK, SG_GROUPS, SG_GW)
    w_causal = ws * jnp.tril(jnp.ones((SG_CHUNK, SG_CHUNK), ws.dtype))
    mixed = jnp.einsum('gts,bnsgc->bntgc', w_causal, v) + bs.T[None, None, :, :, None]
    return (u * mixed.reshape(B, S, SG_WIDTH)) @ w_out

def memory_xattn(h, mem, mem_g, wq, wkv, wo, q_g, k_g):
    B, S = h.shape[:2]
    m = rmsnorm(mem, mem_g)
    q = rmsnorm((h @ wq).reshape(B, S, X_HEADS, X_HD), q_g)
    kv = (m @ wkv).reshape(B, m.shape[1], 2, X_HEADS, X_HD)
    k = rmsnorm(kv[:, :, 0], k_g)
    v = kv[:, :, 1]
    s = jnp.einsum('bshd,bmhd->bhsm', q, k).astype(jnp.float32) * (X_HD ** -0.5)
    p = jax.nn.softmax(s, axis=-1).astype(v.dtype)
    o = jnp.einsum('bhsm,bmhd->bshd', p, v).reshape(B, S, X_HEADS * X_HD)
    return o @ wo

def moe_ffn(h, router_w, router_b, w_in, w_out):
    B, S, D = h.shape
    t = h.reshape(B * S, D)
    logits = (t @ router_w).astype(jnp.float32) + router_b.astype(jnp.float32)
    probs = jax.nn.softmax(logits, axis=-1).reshape(B * S, N_GROUPS, EPG)
    g_idx = jnp.argmax(jnp.max(probs, axis=-1), axis=-1)
    g_sel = jax.nn.one_hot(g_idx, N_GROUPS, dtype=jnp.float32)
    in_group = jnp.einsum('tge,tg->te', probs, g_sel)
    top_p, top_e = lax.top_k(in_group, TOP_K)
    top_w = top_p / jnp.sum(top_p, axis=-1, keepdims=True)
    expert = g_idx[:, None] * EPG + top_e
    gates = jnp.sum(jax.nn.one_hot(expert, N_EXPERTS, dtype=jnp.float32) * top_w[..., None], axis=1).astype(t.dtype)
    y = jnp.zeros_like(t)
    for e in range(N_EXPERTS):
        gu = t @ w_in[e]
        act = jax.nn.silu(gu[:, :D_EXPERT]) * gu[:, D_EXPERT:]
        y = y + gates[:, e:e + 1] * (act @ w_out[e])
    return y.reshape(B, S, D)

def setup_inputs(seed: int = 0) -> dict:
    key = jax.random.key(seed)
    keys = iter(jax.random.split(key, 40))

    def nrm(shape, scale):
        return jax.random.normal(next(keys), shape, jnp.float32) * scale

    def gain(shape):
        return 1.0 + 0.02 * jax.random.normal(next(keys), shape, jnp.float32)

    D = D_MODEL
    out_s = (3 * DEPTH) ** -0.5
    x = nrm((BATCH, SEQ, D), 1.0)
    mem = nrm((BATCH, N_MEM, D), 1.0)
    positions = (jax.random.randint(next(keys), (BATCH, 1), 0, 1024, dtype=jnp.int32)
                 + jnp.arange(SEQ, dtype=jnp.int32)[None, :])
    return {
        'x': x,
        'mem': mem,
        'positions': positions,
        'norm_mix': gain((DEPTH, D)),
        'norm_xattn': gain((DEPTH, D)),
        'norm_mem': gain((DEPTH, D)),
        'norm_ffn': gain((DEPTH, D)),
        'hyb_w_in': nrm((N_EVEN, D, HYB_IN), D ** -0.5),
        'hyb_w_out': nrm((N_EVEN, HYB_OUT, D), HYB_OUT ** -0.5 * out_s),
        'nsa_qnorm': gain((N_EVEN, HEAD_DIM)),
        'nsa_knorm': gain((N_EVEN, 3, HEAD_DIM)),
        'nsa_cmp_pe': nrm((N_EVEN, 2, CMP_LEN, HEAD_DIM), 0.2),
        'nsa_cmp_w1': nrm((N_EVEN, 2, CMP_LEN * HEAD_DIM, HEAD_DIM), (CMP_LEN * HEAD_DIM) ** -0.5),
        'nsa_cmp_w2': nrm((N_EVEN, 2, HEAD_DIM, HEAD_DIM), HEAD_DIM ** -0.5),
        'nsa_gate_b': nrm((N_EVEN, 3 * NSA_HEADS), 0.1),
        'gla_wa2': nrm((N_EVEN, GLA_RANK, GLA_QKW), GLA_RANK ** -0.5),
        'gla_ba': nrm((N_EVEN, GLA_QKW), 0.1),
        'gla_onorm': gain((N_EVEN, GLA_DV)),
        'sg_w_in': nrm((N_ODD, D, 2 * SG_WIDTH), D ** -0.5),
        'sg_ln_g': gain((N_ODD, SG_WIDTH)),
        'sg_ln_b': nrm((N_ODD, SG_WIDTH), 0.02),
        'sg_ws': nrm((N_ODD, SG_GROUPS, SG_CHUNK, SG_CHUNK), SG_CHUNK ** -0.5),
        'sg_bs': gain((N_ODD, SG_GROUPS, SG_CHUNK)),
        'sg_w_out': nrm((N_ODD, SG_WIDTH, D), SG_WIDTH ** -0.5 * out_s),
        'x_wq': nrm((DEPTH, D, X_HEADS * X_HD), D ** -0.5),
        'x_wkv': nrm((DEPTH, D, 2 * X_HEADS * X_HD), D ** -0.5),
        'x_wo': nrm((DEPTH, X_HEADS * X_HD, D), (X_HEADS * X_HD) ** -0.5 * out_s),
        'x_qnorm': gain((DEPTH, X_HD)),
        'x_knorm': gain((DEPTH, X_HD)),
        'router_w': nrm((D, N_EXPERTS), D ** -0.5),
        'router_b': nrm((N_EXPERTS,), 0.01),
        'moe_w_in': nrm((DEPTH, N_EXPERTS, D, 2 * D_EXPERT), D ** -0.5),
        'moe_w_out': nrm((DEPTH, N_EXPERTS, D_EXPERT, D), D_EXPERT ** -0.5 * out_s),
    }

def reference(x, mem, positions, norm_mix, norm_xattn, norm_mem, norm_ffn,
              hyb_w_in, hyb_w_out, nsa_qnorm, nsa_knorm, nsa_cmp_pe, nsa_cmp_w1, nsa_cmp_w2,
              nsa_gate_b, gla_wa2, gla_ba, gla_onorm,
              sg_w_in, sg_ln_g, sg_ln_b, sg_ws, sg_bs, sg_w_out,
              x_wq, x_wkv, x_wo, x_qnorm, x_knorm,
              router_w, router_b, moe_w_in, moe_w_out):
    for layer in range(DEPTH):
        i = layer // 2
        h = rmsnorm(x, norm_mix[layer])
        if layer % 2 == 0:
            (q_a, kc, vc, ks, vs, kw, vw, ga,
             q_b, k_b, v_b, a_low, r_b) = jnp.split(h @ hyb_w_in[i], HYB_SPLITS, axis=-1)
            o_a = nsa_mixer(q_a, kc, vc, ks, vs, kw, vw, ga, positions,
                            nsa_qnorm[i], nsa_knorm[i], nsa_cmp_pe[i], nsa_cmp_w1[i], nsa_cmp_w2[i],
                            nsa_gate_b[i])
            o_b = gla_mixer(q_b, k_b, v_b, a_low, r_b, gla_wa2[i], gla_ba[i], gla_onorm[i])
            mix = jnp.concatenate([o_a, o_b], axis=-1) @ hyb_w_out[i]
        else:
            mix = sgu_mixer(h, sg_w_in[i], sg_ln_g[i], sg_ln_b[i], sg_ws[i], sg_bs[i], sg_w_out[i])
        x = x + mix
        x = x + memory_xattn(rmsnorm(x, norm_xattn[layer]), mem, norm_mem[layer],
                             x_wq[layer], x_wkv[layer], x_wo[layer], x_qnorm[layer], x_knorm[layer])
        x = x + moe_ffn(rmsnorm(x, norm_ffn[layer]), router_w, router_b, moe_w_in[layer], moe_w_out[layer])
    return x


_drawn_inputs = setup_inputs


def setup_inputs(seed=0):
    import zlib

    import numpy as np

    out = dict(_drawn_inputs(seed))
    spreads = {}
    factors = {'norm_xattn': 8.0,
     'norm_mem': 6.385,
     'nsa_qnorm': 8.0,
     'nsa_knorm': 3.61,
     'nsa_gate_b': 6.326,
     'gla_onorm': 5.727,
     'sg_ln_g': 6.3,
     'sg_ln_b': 8.0,
     'sg_bs': 8.0,
     'x_qnorm': 6.64,
     'x_knorm': 8.0,
     'router_b': 2.693}
    for name, (base, spread) in spreads.items():
        noise = np.random.default_rng([zlib.crc32(name.encode()), seed]).standard_normal(out[name].shape)
        drawn = base * np.exp(spread * noise) if base else spread * noise
        out[name] = jnp.asarray(drawn.astype(out[name].dtype))
    for name, factor in factors.items():
        out[name] = (out[name] * factor).astype(out[name].dtype)
    return out
```

```python
from contextlib import ExitStack

import numpy as np
import concourse.bass as bass
from concourse import mybir

F32 = mybir.dt.float32
F32R = mybir.dt.float32r
I32 = mybir.dt.int32
ACT = mybir.ActivationFunctionType
ALU = mybir.AluOpType
AX = mybir.AxisListType

P = 128
D = 1024
S = 512
T = S // P
KD = D // P
DEPTH = 2
N_MEM = 256
MT = N_MEM // P
EPS = 1e-6
NEG = -1e30
GC = 512
KH = 4

HEADS, KVH, HD = 8, 2, 64
HPG = HEADS // KVH
CMP_LEN, CMP_STRIDE = 32, 16
N_CMP = (S - CMP_LEN) // CMP_STRIDE + 1
CP = 32
WINDOW = 256
WT = WINDOW // P

GH, GDK, GDV, GRANK, GTAU, GCH = 4, 64, 128, 16, 16.0, 64
SUB = 16
NSUB = GCH // SUB
NCH = S // GCH

SGW = 2 * D
SGG = 8
XH, XHD = 4, 256
NE, NG, EPG, DE = 16, 4, 4, 384
MAXB = (2 * S) // P + NE - 1
SLOTS = (MAXB + 1) * P

SIZES = (512, 128, 128, 128, 128, 128, 128, 24, 256, 256, 512, 16, 512)
OFF = [0]
for _s in SIZES:
    OFF.append(OFF[-1] + _s)
(O_QA, O_KC, O_VC, O_KS, O_VS, O_KW, O_VW, O_GA, O_QB, O_KB, O_VB, O_AL, O_R, O_END) = OFF


PHASE_SEMS = 48

class Chain:

    def __init__(self, engine, sem):
        self.engine, self.sem, self.n = engine, sem, 0

    def link(self, ins):
        self.n += 1
        ins.then_inc(self.sem, 1)
        self.engine.wait_ge(self.sem, self.n)


class Core:

    def __init__(self, nc, ctx, a):
        self.nc, self.ctx, self.a = nc, ctx, a
        self.turn, self.taken = 0, 0
        self.banks = [[self.sem(f"phase{b}_{i}") for i in range(PHASE_SEMS)] for b in range(2)]
        sb, sem = self.sb, self.sem
        self.x = sb(ctx, "x_res", [P, T, D])
        self.ident = sb(ctx, "ident", [P, P])
        self.stage = [sb(ctx, f"w_stage{h}", [P, KH, GC]) for h in range(2)]
        self.w_hi = [sb(ctx, f"w_hi{h}", [P, KH, GC], F32R) for h in range(2)]
        self.w_lo = [sb(ctx, f"w_lo{h}", [P, KH, GC], F32R) for h in range(2)]
        self.psum = [ctx.enter_context(nc.psum_tensor(f"bank{b}", [P, GC], F32)) for b in range(8)]
        self.landed = [sem(f"w_landed{h}") for h in range(2)]
        self.hi_done = [sem(f"w_hi_done{h}") for h in range(2)]
        self.lo_done = [sem(f"w_lo_done{h}") for h in range(2)]
        self.used = [sem(f"w_used{h}") for h in range(2)]
        self.y_dram = nc.dram_tensor("moe_y", [SLOTS, D], F32).ap()
        self.cleared = sem("y_cleared")
        self.groups = []
        self.asked = 0

    def sb(self, ctx, name, shape, dt=F32):
        return ctx.enter_context(self.nc.sbuf_tensor(name, shape, dt))

    def split_pair(self, ctx, name, k=KD, n=S):
        return (self.sb(ctx, f"{name}_hi", [P, k, n], F32R), self.sb(ctx, f"{name}_lo", [P, k, n], F32R))

    def clear_outputs(self, sp, zeros):
        for b in range(2 * S // P, SLOTS // P):
            sp.dma_start(self.y_dram[b * P:(b + 1) * P, :], zeros).then_inc(self.cleared, 16)
        sp.wait_ge(self.cleared, 16 * (SLOTS // P - 2 * S // P))

    def sem(self, name):
        return self.ctx.enter_context(self.nc.semaphore(name))

    def phase(self):
        self.turn += 1
        self.taken = 0
        if self.turn > 1:
            last = self.banks[self.turn % 2]
            self.nc.gpsimd.sem_clear(range(last[0].num, last[-1].num + 1))

    def psem(self, name):
        s = self.banks[(self.turn + 1) % 2][self.taken]
        self.taken += 1
        return s

    def add_linear(self, w, cols):
        for c0, c1 in cols:
            for k0 in range(0, w.shape[0], 2 * KH * P):
                self.groups.append(([w[k0 + h * KH * P:k0 + (h + 1) * KH * P, c0:c1]
                                     .rearrange("(k p) n -> p k n", p=P) for h in range(2)], c1 - c0))

    def load(self, sp, upto):
        while self.asked < min(upto, len(self.groups)):
            n = self.asked
            srcs, cols = self.groups[n]
            for h in range(2):
                if n:
                    sp.wait_ge(self.lo_done[h], n)
                sp.dma_start(self.stage[h][:, :, :cols], srcs[h]).then_inc(self.landed[h], 16)
            self.asked += 1

    def split_hi(self, act, n):
        cols = self.groups[n][1]
        for h in range(2):
            act.wait_ge(self.landed[h], 16 * (n + 1))
            if n:
                act.wait_ge(self.used[h], n)
            act.activation(self.w_hi[h][:, :, :cols], self.stage[h][:, :, :cols], ACT.Copy)\
               .then_inc(self.hi_done[h], 1)

    def split_lo(self, dve, n):
        cols = self.groups[n][1]
        for h in range(2):
            dve.wait_ge(self.hi_done[h], n + 1)
            dve.tensor_tensor(self.w_lo[h][:, :, :cols], self.stage[h][:, :, :cols],
                              self.w_hi[h][:, :, :cols], ALU.subtract).then_inc(self.lo_done[h], 1)

    def product(self, pe, n, feature_major, banks, hi, lo, tiles=T, first=True, last=True, k0=0):
        cols = self.groups[n][1]
        for h in range(2):
            pe.wait_ge(self.lo_done[h], n + 1)
            for b in range(cols // P if feature_major else tiles):
                for kk in range(KH):
                    k = k0 + KH * h + kk
                    for term, (x_part, w_part) in enumerate(((hi, self.w_hi[h]), (hi, self.w_lo[h]), (lo, self.w_hi[h]))):
                        start = first and h == 0 and kk == 0 and term == 0
                        stop = last and h == 1 and kk == KH - 1 and term == 2
                        if feature_major:
                            ins = pe.matmul(banks[b][:, :tiles * P], w_part[:, kk, b * P:(b + 1) * P],
                                            x_part[:, k, :tiles * P], start=start, stop=stop)
                        else:
                            ins = pe.matmul(banks[b][:, :cols], x_part[:, k, b * P:(b + 1) * P],
                                            w_part[:, kk, :cols], start=start, stop=stop)
            ins.then_inc(self.used[h], 1)

    def done(self, engine, n):
        engine.wait_ge(self.used[1], n + 1)


def setup(m):
    m.phase()
    nc, ctx = m.nc, m.ctx
    loaded = m.x_loaded = m.psem("x_loaded")
    made = m.psem("consts_made")
    m.causal = m.sb(ctx, "causal_neg", [P, P])
    m.beyond = m.sb(ctx, "beyond_neg", [P, P])
    with nc.Block() as block:
        @block.sync
        def _(sp):
            for t in range(T):
                sp.dma_start(m.x[:, t, :], m.a["x"][0, t * P:(t + 1) * P, :]).then_inc(loaded, 16)
            m.load(sp, 1)
            sp.wait_ge(loaded, 16 * T)

        @block.gpsimd
        def _(pool):
            pool.memset(m.ident[:, :], 0.0).then_inc(made, 1)
            pool.memset(m.causal[:, :], 0.0).then_inc(made, 1)
            pool.memset(m.beyond[:, :], 0.0).then_inc(made, 1)
            pool.wait_ge(made, 3)
            pool.affine_select(out=m.ident[:, :], in_=m.ident[:, :], compare_op=ALU.not_equal, fill=1.0,
                               base=0, pattern=[[-1, P]], channel_multiplier=1).then_inc(made, 1)
            pool.affine_select(out=m.causal[:, :], in_=m.causal[:, :], compare_op=ALU.is_ge, fill=NEG,
                               base=0, pattern=[[-1, P]], channel_multiplier=1).then_inc(made, 1)
            pool.affine_select(out=m.beyond[:, :], in_=m.beyond[:, :], compare_op=ALU.is_gt, fill=NEG,
                               base=0, pattern=[[1, P]], channel_multiplier=-1).then_inc(made, 1)
            pool.wait_ge(made, 6)


def norm_transpose(m, name, src, gain, tiles, hi, lo, plain=None, h_dram=None):
    m.phase()
    nc = m.nc
    with ExitStack() as c:
        xn = m.sb(c, f"{name}_xn", [P, tiles, D])
        g = m.sb(c, f"{name}_gain", [P, KD])
        junk = m.sb(c, f"{name}_sq", [P, D])
        ms = m.sb(c, f"{name}_ms", [P, tiles])
        root = m.sb(c, f"{name}_root", [P, tiles])
        rstd = m.sb(c, f"{name}_rstd", [P, tiles])
        gain_in, squared, mean, rooted, normed, turned, hi_out, lo_out, dve_c, act_c, stored = (
            m.psem(f"{name}_{s}") for s in ("gain_in", "squared", "mean", "rooted", "normed", "turned",
                                           "hi_out", "lo_out", "dve", "act", "stored"))
        gb = m.sb(c, f"{name}_gain_row", [P, D]) if plain is not None else None
        with nc.Block() as block:
            @block.sync
            def _(sp):
                if plain is None:
                    with nc.allow_non_contiguous_dma(reason="one gain per partition"):
                        sp.dma_start(g[:, :], gain.rearrange("(k p) -> p k", p=P)).then_inc(gain_in, 16)
                else:
                    sp.dma_start(gb[:, :], gain.partition_broadcast(P)).then_inc(gain_in, 16)
                    for t in range(tiles):
                        sp.wait_ge(normed, t + 1)
                        sp.dma_start(h_dram[t * P:(t + 1) * P, :], xn[:, t, :]).then_inc(stored, 16)
                    sp.wait_ge(stored, 16 * tiles)

            @block.scalar
            def _(act):
                link = Chain(act, act_c).link
                for t in range(tiles):
                    if t:
                        act.wait_ge(squared, t)
                    act.activation(junk[:, :], src[:, t, :], ACT.Square, accum_out=ms[:, t:t + 1])\
                       .then_inc(squared, 1)
                act.wait_ge(mean, 1)
                act.activation(root[:, :], ms[:, :], ACT.Sqrt).then_inc(rooted, 1)
                if plain is None:
                    act.wait_ge(gain_in, 16)
                for k in range(KD):
                    act.wait_ge(turned, k + 1)
                    if plain is None:
                        act.activation(hi[:, k, :tiles * P], m.psum[k][:, :tiles * P], ACT.Copy,
                                       scale=g[:, k:k + 1]).then_inc(hi_out, 1)
                    elif k % 2 == 0:
                        act.activation(plain[:, k, :tiles * P], m.psum[k][:, :tiles * P], ACT.Copy).then_inc(hi_out, 1)

            @block.vector
            def _(dve):
                link = Chain(dve, dve_c).link
                dve.wait_ge(squared, tiles)
                dve.tensor_scalar(ms[:, :], ms[:, :], 1.0 / D, EPS, ALU.mult, ALU.add).then_inc(mean, 1)
                dve.wait_ge(rooted, 1)
                link(dve.reciprocal(rstd[:, :], root[:, :]))
                if plain is not None:
                    dve.wait_ge(gain_in, 16)
                for t in range(tiles):
                    if plain is None:
                        dve.tensor_scalar(xn[:, t, :], src[:, t, :], rstd[:, t:t + 1], None, ALU.mult).then_inc(normed, 1)
                    else:
                        dve.scalar_tensor_tensor(out=xn[:, t, :], in0=src[:, t, :], scalar=rstd[:, t:t + 1],
                                                 in1=gb[:, :], op0=ALU.mult, op1=ALU.mult).then_inc(normed, 1)
                if plain is None:
                    for k in range(KD):
                        dve.wait_ge(hi_out, k + 1)
                        dve.scalar_tensor_tensor(out=lo[:, k, :tiles * P], in0=m.psum[k][:, :tiles * P],
                                                 scalar=g[:, k:k + 1], in1=hi[:, k, :tiles * P],
                                                 op0=ALU.mult, op1=ALU.subtract).then_inc(lo_out, 1)
                else:
                    for k in range(1, KD, 2):
                        dve.wait_ge(turned, k + 1)
                        dve.tensor_copy(plain[:, k, :tiles * P], m.psum[k][:, :tiles * P]).then_inc(lo_out, 1)

            @block.tensor
            def _(pe):
                pe.wait_ge(normed, tiles)
                for k in range(KD):
                    for t in range(tiles):
                        ins = pe.transpose(m.psum[k][:, t * P:(t + 1) * P], xn[:, t, k * P:(k + 1) * P], m.ident[:, :])
                    ins.then_inc(turned, 1)


def store_x(m, out):
    m.phase()
    stored = m.psem("x_stored")
    with m.nc.Block() as block:
        @block.sync
        def _(sp):
            for t in range(T):
                sp.dma_start(out[0, t * P:(t + 1) * P, :], m.x[:, t, :]).then_inc(stored, 16)
            sp.wait_ge(stored, 16 * T)


def projection_outputs(m, c):
    qk = m.sb(c, "qk", [P, T, HEADS + 2 * KVH, HD])
    v_sw = m.sb(c, "v_sw", [P, T, 2, KVH * HD])
    kvc = m.sb(c, "kvc", [P, 2, S])
    gqk = m.sb(c, "gla_qk", [P, 4, S])
    gv = m.sb(c, "gla_v", [P, T, GH * GDV])
    gr = m.sb(c, "gla_r", [P, T, GH * GDV])
    ga = m.sb(c, "gates", [P, T, 3 * HEADS])
    al = m.sb(c, "a_low", [P, T, GRANK])
    return qk, v_sw, kvc, gqk, gv, gr, ga, al


def hybrid_projection(m, outputs, first, hi, lo):
    m.phase()
    nc = m.nc
    qk, v_sw, kvc, gqk, gv, gr, ga, al = outputs
    out_act, out_dve = m.psem("proj_out_act"), m.psem("proj_out_dve")
    kinds = [(False, 4), (False, 4), (True, 2), (True, 4), (False, 4), (False, 4), (False, 4), (False, 4)]

    def bank(j, b):
        return m.psum[4 * (j % 2) + b]

    with nc.Block() as block:
        @block.sync
        def _(sp):
            m.load(sp, first + len(kinds) + 1)

        @block.tensor
        def _(pe):
            for j, (fm, _) in enumerate(kinds):
                if j >= 2:
                    pe.wait_ge(out_act, sum(k[1] // 2 for k in kinds[:j - 1]))
                    pe.wait_ge(out_dve, sum(k[1] // 2 for k in kinds[:j - 1]))
                m.product(pe, first + j, fm, [bank(j, b) for b in range(4)], hi, lo)

        def read_out(engine, copy, j, b):
            ps = bank(j, b)
            if j == 0:
                copy(qk[:, b, 0:HEADS, :].rearrange("p (i g) d -> p g i d", g=KVH),
                     ps[:, :].rearrange("p (g i d) -> p g i d", g=KVH, d=HD)).then_inc(engine, 1)
            elif j == 1:
                parts = ps[:, :].rearrange("p (w kv c) -> p w kv c", w=2, kv=2)
                copy(qk[:, b, HEADS:, :].rearrange("p (w g) d -> p w (g d)", w=2), parts[:, :, 0, :])
                copy(v_sw[:, b, :, :], parts[:, :, 1, :]).then_inc(engine, 1)
            elif j == 2:
                copy(kvc[:, b, :], ps[:, :]).then_inc(engine, 1)
            elif j == 3:
                copy(gqk[:, b, :], ps[:, :], GDK ** -0.5 if b < 2 else 1.0).then_inc(engine, 1)
            elif j == 4:
                copy(gv[:, b, :], ps[:, :]).then_inc(engine, 1)
            elif j == 5:
                copy(gr[:, b, :], ps[:, :]).then_inc(engine, 1)
            elif j == 6:
                copy(ga[:, b, :], ps[:, 0:3 * HEADS]).then_inc(engine, 1)
            else:
                copy(al[:, b, :], ps[:, 0:GRANK]).then_inc(engine, 1)

        @block.scalar
        def _(act):
            def copy(out, ps, scale=1.0):
                return act.activation(out, ps, ACT.Copy, scale=scale)
            m.split_hi(act, first)
            for j, (_, n_banks) in enumerate(kinds):
                if j + 1 < len(kinds):
                    m.split_hi(act, first + j + 1)
                m.done(act, first + j)
                for b in range(0, n_banks, 2):
                    read_out(out_act, copy, j, b)

        @block.vector
        def _(dve):
            def copy(out, ps, scale=1.0):
                return dve.tensor_scalar(out, ps, scale, None, ALU.mult)
            m.split_lo(dve, first)
            for j, (_, n_banks) in enumerate(kinds):
                if j + 1 < len(kinds):
                    m.split_lo(dve, first + j + 1)
                m.done(dve, first + j)
                for b in range(1, n_banks, 2):
                    read_out(out_dve, copy, j, b)


def nsa_prepare(m, c, qk, kvc):
    m.phase()
    nc, a = m.nc, m.a
    NP6 = (HEADS + 2 * KVH) // 2
    QH = HEADS + 2 * KVH
    HF = HD // 2
    MAGIC = 1.5 * 2 ** 23
    TWO_PI = 2 * np.pi
    C1 = 6.28125
    C2 = float(np.float32(np.round((TWO_PI - C1) * 2 ** 22) / 2 ** 22))
    C3 = float(TWO_PI - C1 - C2)

    qkT = m.sb(c, "qkT", [P, NP6, S])
    kcT = m.sb(c, "kcT", [P, CP])
    vbd = m.sb(c, "vc_diag", [P, KVH, HPG, HD])
    with ExitStack() as t:
        pos_i = m.sb(t, "pos_i", [P, T + 1], I32)
        pos = m.sb(t, "pos", [P, T + 1])
        freq = m.sb(t, "freq", [P, HF])
        ang = m.sb(t, "ang", [P, T + 1, HF])
        turns = m.sb(t, "turns", [P, T + 1, HF])
        sin = m.sb(t, "sin", [P, T + 1, HF])
        cos = m.sb(t, "cos", [P, T + 1, HF])
        gains = m.sb(t, "head_gains", [P, QH, HD])
        kc_gain = m.sb(t, "kc_gain", [P, HD])
        sq = m.sb(t, "head_sq", [P, QH * HD])
        rot = m.sb(t, "head_rot", [P, QH, HD])
        tmp = m.sb(t, "head_tmp", [P, 2, QH, HF])
        ss = m.sb(t, "head_ss", [P, T * QH])
        root = m.sb(t, "head_root", [P, T * QH])
        w1 = m.sb(t, "cmp_w1", [P, 2, CMP_LEN, P])
        w2 = m.sb(t, "cmp_w2", [P, 2, P])
        pe_t = m.sb(t, "cmp_pe", [P, 2, CMP_LEN])
        blk = m.sb(t, "cmp_blocks", [P, CMP_LEN, CP])
        act1 = m.sb(t, "cmp_act", [P, 2, CP])
        kc = m.sb(t, "kc", [CP, KVH, HD])
        kc_sq = m.sb(t, "kc_sq", [CP, KVH, HD])
        kc_n = m.sb(t, "kc_n", [CP, KVH, HD])
        kc_r = m.sb(t, "kc_r", [CP, KVH, HD])
        kc_ss = m.sb(t, "kc_ss", [CP, KVH])
        kc_tmp = m.sb(t, "kc_tmp", [CP, 2, KVH, HF])
        vc = m.sb(t, "vc", [CP, KVH * HD])
        (small_in, w_in, zeroed, dve_c, act_c, angles, sines, sqr, means, roots, heads_done, turned, kept,
         blocks, hidden, gelued, out2, kc_mean, kc_root, kc_done, kc_turned, v_here, v_spread) = (
            m.psem(f"prep_{s}") for s in (
                "small_in", "w_in", "zeroed", "dve", "act", "angles", "sines", "sqr", "means", "roots",
                "heads_done", "turned", "kept", "blocks", "hidden", "gelued", "out2", "kc_mean",
                "kc_root", "kc_done", "kc_turned", "v_here", "v_spread"))

        def rotate(dve, link, out, xin, cs, sn, tmp2, n):
            x1, x2 = xin[:, :, 0:HF], xin[:, :, HF:HD]
            p = xin.shape[0]
            cb = cs.unsqueeze(1).to_broadcast([p, n, HF])
            sb = sn.unsqueeze(1).to_broadcast([p, n, HF])
            dve.tensor_tensor(tmp2[:, 0], x2, sb, ALU.mult)
            dve.tensor_tensor(tmp2[:, 1], x1, sb, ALU.mult)
            dve.tensor_tensor(out[:, :, 0:HF], x1, cb, ALU.mult)
            link(dve.tensor_tensor(out[:, :, HF:HD], x2, cb, ALU.mult))
            dve.tensor_tensor(out[:, :, 0:HF], out[:, :, 0:HF], tmp2[:, 0], ALU.subtract)
            return dve.tensor_tensor(out[:, :, HF:HD], out[:, :, HF:HD], tmp2[:, 1], ALU.add)

        with nc.Block() as block:
            @block.sync
            def _(sp):
                with nc.allow_non_contiguous_dma(reason="small tables, one element per partition"):
                    sp.dma_start(pos_i[:, 0:T], a["positions"][0].rearrange("(t p) -> p t", p=P)).then_inc(small_in, 16)
                    sp.wait_ge(angles, 1)
                    sp.dma_start(pos_i[0:N_CMP, T:T + 1],
                                 a["positions"][0:1, CMP_LEN - 1:CMP_LEN - 1 + CMP_STRIDE * (N_CMP - 1) + 1:CMP_STRIDE]
                                 .rearrange("a c -> c a")).then_inc(small_in, 16)
                    sp.dma_start(freq[:, :], a["rope_freq"].partition_broadcast(P)).then_inc(small_in, 16)
                    for g0, n, src in ((0, HEADS, a["nsa_qnorm"][0]), (HEADS, KVH, a["nsa_knorm"][0, 1]),
                                       (HEADS + KVH, KVH, a["nsa_knorm"][0, 2])):
                        for i in range(n):
                            sp.dma_start(gains[:, g0 + i, :], src.partition_broadcast(P)).then_inc(small_in, 16)
                    sp.dma_start(kc_gain[:, :], a["nsa_knorm"][0, 0].partition_broadcast(P)).then_inc(small_in, 16)
                    sp.wait_ge(zeroed, 4)
                    for kv in range(2):
                        for g in range(KVH):
                            half = slice(g * HD, (g + 1) * HD)
                            sp.dma_start(w1[half, kv, :, half], a["nsa_cmp_w1"][0, kv].rearrange("(l d) e -> d l e", d=HD)).then_inc(w_in, 16)
                            sp.dma_start(w2[half, kv, half], a["nsa_cmp_w2"][0, kv]).then_inc(w_in, 16)
                            sp.dma_start(pe_t[half, kv, :], a["nsa_cmp_pe"][0, kv].rearrange("l d -> d l")).then_inc(w_in, 16)
                    sp.wait_ge(v_here, 1)
                    for g in range(KVH):
                        for i in range(HPG):
                            sp.dma_start(vbd[i * CP:i * CP + N_CMP, g, i, :], vc[0:N_CMP, g * HD:(g + 1) * HD]).then_inc(v_spread, 16)
                    sp.wait_ge(v_spread, 16 * KVH * HPG)

            @block.gpsimd
            def _(pool):
                pool.memset(w1[:, :, :, :], 0.0).then_inc(zeroed, 1)
                pool.memset(w2[:, :, :], 0.0).then_inc(zeroed, 1)
                pool.memset(vbd[:, :, :, :], 0.0).then_inc(zeroed, 1)
                pool.memset(kcT[:, :], 0.0).then_inc(zeroed, 1)

            @block.vector
            def _(dve):
                link = Chain(dve, dve_c).link
                dve.memset(pos_i[:, T:T + 1], 0).then_inc(angles, 1)
                dve.wait_ge(small_in, 16 * (3 + QH + 1))
                link(dve.tensor_copy(pos[:, :], pos_i[:, :]))
                for i in range(T + 1):
                    ins = dve.tensor_scalar(ang[:, i, :], freq[:, :], pos[:, i:i + 1], None, ALU.mult)
                link(ins)
                link(dve.tensor_scalar(turns[:, :, :], ang[:, :, :], 1 / TWO_PI, MAGIC, ALU.mult, ALU.add))
                link(dve.tensor_scalar(turns[:, :, :], turns[:, :, :], MAGIC, None, ALU.subtract))
                for part in (C1, C2, C3):
                    link(dve.scalar_tensor_tensor(out=ang[:, :, :], in0=turns[:, :, :], scalar=-part,
                                                  in1=ang[:, :, :], op0=ALU.mult, op1=ALU.add))
                dve.tensor_scalar(ang[:, :, :], ang[:, :, :], 3.1415925, -3.1415925, ALU.min, ALU.max).then_inc(angles, 1)
                for i in range(T):
                    link(dve.tensor_tensor(sq[:, :], qk[:, i].rearrange("p h d -> p (h d)"),
                                           qk[:, i].rearrange("p h d -> p (h d)"), ALU.mult))
                    link(dve.tensor_reduce(ss[:, i * QH:(i + 1) * QH], sq[:, :].rearrange("p (h d) -> p h d", d=HD), AX.X, ALU.add))
                dve.tensor_scalar(ss[:, :], ss[:, :], 1.0 / HD, EPS, ALU.mult, ALU.add).then_inc(means, 1)
                dve.wait_ge(w_in, 16 * 12)
                for kv in range(2):
                    if kv:
                        dve.wait_ge(hidden, 1)
                    for lh in range(2):
                        src = kvc[:, kv, lh * 16:lh * 16 + 16 * N_CMP].rearrange("p (c l) -> p l c", l=16)
                        dve.tensor_tensor(blk[:, lh * 16:lh * 16 + 16, 0:N_CMP], src,
                                          pe_t[:, kv, lh * 16:lh * 16 + 16].unsqueeze(2).to_broadcast([P, 16, N_CMP]),
                                          ALU.add).then_inc(blocks, 1)
                dve.wait_ge(sines, 2)
                link(dve.tensor_tensor(cos[:, :, :], cos[:, :, :], cos[:, :, :], ALU.mult))
                link(dve.tensor_scalar(cos[:, :, :], cos[:, :, :], -2.0, 1.0, ALU.mult, ALU.add))
                dve.wait_ge(roots, 1)
                link(dve.reciprocal(ss[:, :], root[:, :]))
                link(dve.tensor_scalar(gains[:, 0:HEADS, :], gains[:, 0:HEADS, :], HD ** -0.5, None, ALU.mult))
                for i in range(T):
                    r = ss[:, i * QH:(i + 1) * QH].unsqueeze(2).to_broadcast([P, QH, HD])
                    link(dve.tensor_tensor(rot[:, :, :], qk[:, i], r, ALU.mult))
                    link(dve.tensor_tensor(rot[:, :, :], rot[:, :, :], gains[:, :, :], ALU.mult))
                    rotate(dve, link, qk[:, i], rot[:, :, :], cos[:, i], sin[:, i], tmp, QH).then_inc(heads_done, 1)
                    dve.wait_ge(heads_done, i + 1)
                dve.wait_ge(out2, 1)
                link(dve.tensor_copy(kc[0:N_CMP], m.psum[6][0:N_CMP, 0:P].rearrange("p (g d) -> p g d", g=KVH)))
                link(dve.tensor_tensor(kc_sq[0:N_CMP], kc[0:N_CMP], kc[0:N_CMP], ALU.mult))
                link(dve.tensor_reduce(kc_ss[0:N_CMP], kc_sq[0:N_CMP], AX.X, ALU.add))
                dve.tensor_scalar(kc_ss[0:N_CMP], kc_ss[0:N_CMP], 1.0 / HD, EPS, ALU.mult, ALU.add).then_inc(kc_mean, 1)
                dve.wait_ge(kc_root, 1)
                link(dve.reciprocal(kc_ss[0:N_CMP], kc_sq[0:N_CMP, 0, 0:KVH]))
                link(dve.tensor_tensor(kc_n[0:N_CMP], kc[0:N_CMP], kc_ss[0:N_CMP].unsqueeze(2).to_broadcast([N_CMP, KVH, HD]), ALU.mult))
                link(dve.tensor_tensor(kc_n[0:N_CMP], kc_n[0:N_CMP], kc_gain[0:N_CMP].unsqueeze(1).to_broadcast([N_CMP, KVH, HD]), ALU.mult))
                rotate(dve, link, kc_r[0:N_CMP], kc_n[0:N_CMP], cos[0:N_CMP, T], sin[0:N_CMP, T], kc_tmp[0:N_CMP], KVH).then_inc(kc_done, 1)
                dve.wait_ge(zeroed, 4)
                dve.wait_ge(kc_turned, 1)
                dve.tensor_copy(kcT[:, 0:N_CMP], m.psum[7][:, 0:N_CMP])

            @block.scalar
            def _(act):
                act.wait_ge(angles, 2)
                act.activation(sin[:, :, :], ang[:, :, :], ACT.Sin).then_inc(sines, 1)
                act.activation(cos[:, :, :], ang[:, :, :], ACT.Sin, scale=0.5).then_inc(sines, 1)
                act.wait_ge(means, 1)
                act.activation(root[:, :], ss[:, :], ACT.Sqrt).then_inc(roots, 1)
                for kv in range(2):
                    act.wait_ge(hidden, kv + 1)
                    act.activation(act1[:, kv, 0:N_CMP], m.psum[kv][:, 0:N_CMP], ACT.Gelu_apprx_tanh).then_inc(gelued, 1)
                act.wait_ge(out2, 2)
                act.activation(vc[0:N_CMP], m.psum[7][0:N_CMP, 0:P], ACT.Copy).then_inc(v_here, 1)
                act.wait_ge(kc_mean, 1)
                act.activation(kc_sq[0:N_CMP, 0, 0:KVH], kc_ss[0:N_CMP], ACT.Sqrt).then_inc(kc_root, 1)
                for i in range(T):
                    act.wait_ge(turned, i + 1)
                    act.activation(qkT[:, 0:4, i * P:(i + 1) * P],
                                   m.psum[2 + 2 * (i % 2)][:, :].rearrange("p (k t) -> p k t", k=4), ACT.Copy)
                    act.activation(qkT[:, 4:6, i * P:(i + 1) * P],
                                   m.psum[3 + 2 * (i % 2)][:, 0:2 * P].rearrange("p (k t) -> p k t", k=2), ACT.Copy).then_inc(kept, 1)

            @block.tensor
            def _(pe):
                for kv in range(2):
                    pe.wait_ge(blocks, 2 * kv + 2)
                    for l in range(CMP_LEN):
                        ins = pe.matmul(m.psum[kv][:, 0:N_CMP], w1[:, kv, l, :], blk[:, l, 0:N_CMP],
                                        start=l == 0, stop=l == CMP_LEN - 1)
                    ins.then_inc(hidden, 1)
                for kv in range(2):
                    pe.wait_ge(gelued, kv + 1)
                    pe.matmul(m.psum[6 + kv][0:N_CMP, 0:P], act1[:, kv, 0:N_CMP], w2[:, kv, :],
                              start=True, stop=True).then_inc(out2, 1)
                for i in range(T):
                    pe.wait_ge(heads_done, i + 1)
                    if i >= 2:
                        pe.wait_ge(kept, i - 1)
                    for pair in range(NP6):
                        ins = pe.transpose(m.psum[2 + 2 * (i % 2) + pair // 4][:, (pair % 4) * P:(pair % 4 + 1) * P],
                                           qk[:, i, 2 * pair:2 * pair + 2, :].rearrange("p h d -> p (h d)"), m.ident[:, :])
                    ins.then_inc(turned, 1)
                pe.wait_ge(kc_done, 1)
                pe.wait_ge(v_here, 1)
                pe.transpose(m.psum[7][:, 0:N_CMP], kc_r[0:N_CMP].rearrange("p g d -> p (g d)"),
                             m.ident[0:N_CMP, 0:N_CMP]).then_inc(kc_turned, 1)
    return qkT, kcT, vbd


def nsa_attention(m, qkT, kcT, vbd, v_sw, ga, mix):
    m.phase()
    nc, a = m.nc, m.a
    with ExitStack() as t:
        cmask = m.sb(t, "cmp_neg", [P, T, CP])
        cone = m.sb(t, "cmp_one", [P, T, CP])
        gate_b = m.sb(t, "gate_b", [P, 3 * HEADS])
        gate = m.sb(t, "gate", [P, T, HEADS, 3])
        prob = m.sb(t, "prob", [P, HPG, S])
        probT = m.sb(t, "probT", [P, 2, S])
        nmax = m.sb(t, "nmax", [P, HPG])
        sums = m.sb(t, "sums", [P, 3, HPG])
        coef = m.sb(t, "coef", [P, 3, HPG])
        cs = m.sb(t, "cmp_s", [P, HPG, CP])
        cp = m.sb(t, "cmp_p", [P, HPG, CP])
        cpT = m.sb(t, "cmp_pT", [P, P])
        part = m.sb(t, "part", [P, 3, HPG, HD])
        zeros = m.sb(t, "zeros", [P, D])
        zeroed = m.psem("attn_zeroed")
        (gb_in, masks, gated, g_lin, dve_c, cmp_s, cmp_sub, cmp_e, cmp_p, cmp_t, cmp_k, scored, maxed, exped,
         turned, kept, summed, combined) = (m.psem(f"attn_{s}") for s in (
            "gb_in", "masks", "gated", "g_lin", "dve", "cmp_s", "cmp_sub", "cmp_e", "cmp_p", "cmp_t", "cmp_k",
            "scored", "maxed", "exped", "turned", "kept", "summed", "combined"))
        steps = [(i, g) for i in range(T) for g in range(KVH)]

        def keys(i, br):
            return list(range(0 if br == 0 else max(0, i - WT), i + 1))

        with nc.Block() as block:
            @block.sync
            def _(sp):
                sp.dma_start(gate_b[:, :], a["nsa_gate_b"][0].partition_broadcast(P)).then_inc(gb_in, 16)
                sp.wait_ge(zeroed, 1)
                m.clear_outputs(sp, zeros[:, :])

            @block.gpsimd
            def _(pool):
                pool.memset(zeros[:, :], 0.0).then_inc(zeroed, 1)
                pool.memset(cmask[:, :, :], 0.0).then_inc(masks, 1)
                pool.memset(cone[:, :, :], 1.0).then_inc(masks, 1)
                pool.wait_ge(masks, 2)
                for tile_, fill in ((cmask, NEG), (cone, 0.0)):
                    pool.affine_select(out=tile_[:, :, :], in_=tile_[:, :, :], compare_op=ALU.is_ge, fill=fill,
                                       base=-(CMP_LEN - 1), pattern=[[P, T], [-CMP_STRIDE, CP]],
                                       channel_multiplier=1).then_inc(masks, 1)

            @block.tensor
            def _(pe):
                for n, (i, g) in enumerate(steps):
                    half = slice(g * HD, (g + 1) * HD)
                    tok = slice(i * P, (i + 1) * P)
                    if n:
                        pe.wait_ge(combined, n)
                    for h in range(HPG):
                        ins = pe.matmul(m.psum[7][:, h * CP:(h + 1) * CP], qkT[half, h, tok], kcT[half, :],
                                        start=True, stop=True)
                    ins.then_inc(cmp_s, 1)
                    for br in range(2):
                        kt = keys(i, br)
                        w = len(kt) * P
                        u = 2 * n + br
                        if u:
                            pe.wait_ge(exped, HPG * u)
                        for h in range(HPG):
                            ins = pe.matmul(m.psum[h][:, 0:w], qkT[half, h, tok],
                                            qkT[half, 4 + br, kt[0] * P:(kt[-1] + 1) * P], start=True, stop=True)
                        ins.then_inc(scored, 1)
                        if br == 0:
                            pe.wait_ge(cmp_p, n + 1)
                            pe.transpose(m.psum[7][:, P:2 * P], cp[:, :, :].rearrange("p h c -> p (h c)"),
                                         m.ident[:, :]).then_inc(cmp_t, 1)
                            pe.wait_ge(cmp_k, n + 1)
                            pe.matmul(m.psum[7][:, 2 * P:4 * P], cpT[:, :], vbd[:, g].rearrange("p h d -> p (h d)"),
                                      start=True, stop=True)
                        for h in range(HPG):
                            pe.wait_ge(exped, HPG * u + h + 1)
                            v = HPG * u + h
                            if v >= 2:
                                pe.wait_ge(kept, v - 1)
                            for j in range(len(kt)):
                                ins = pe.transpose(m.psum[4 + v % 2][:, j * P:(j + 1) * P],
                                                   prob[:, h, j * P:(j + 1) * P], m.ident[:, :])
                            ins.then_inc(turned, 1)
                            pe.wait_ge(kept, v + 1)
                            for j, k in enumerate(kt):
                                ins = pe.matmul(m.psum[6][:, br * 256 + h * HD:br * 256 + (h + 1) * HD],
                                                probT[:, v % 2, j * P:(j + 1) * P], v_sw[:, k, br, half],
                                                start=j == 0, stop=j == len(kt) - 1)
                    ins.then_inc(summed, 1)

            @block.scalar
            def _(act):
                act.wait_ge(g_lin, 1)
                act.activation(gate[:, :, :, :].rearrange("p t h b -> p (t h b)"),
                               ga[:, :, :].rearrange("p t c -> p (t c)"), ACT.Sigmoid).then_inc(gated, 1)
                for n, (i, g) in enumerate(steps):
                    act.wait_ge(cmp_sub, n + 1)
                    act.activation(cp[:, :, :], cs[:, :, :], ACT.Exp).then_inc(cmp_e, 1)
                    for br in range(2):
                        u = 2 * n + br
                        w = len(keys(i, br)) * P
                        act.wait_ge(maxed, u + 1)
                        for h in range(HPG):
                            if u:
                                act.wait_ge(turned, HPG * (u - 1) + h + 1)
                            act.activation(prob[:, h, 0:w], m.psum[h][:, 0:w], ACT.Exp, bias=nmax[:, h:h + 1],
                                           accum_out=sums[:, 1 + br, h:h + 1]).then_inc(exped, 1)
                        if br == 0:
                            act.wait_ge(cmp_t, n + 1)
                            act.activation(cpT[:, :], m.psum[7][:, P:2 * P], ACT.Copy).then_inc(cmp_k, 1)
                        for h in range(HPG):
                            v = HPG * u + h
                            act.wait_ge(turned, v + 1)
                            act.activation(probT[:, v % 2, 0:w], m.psum[4 + v % 2][:, 0:w], ACT.Copy).then_inc(kept, 1)

            @block.vector
            def _(dve):
                link = Chain(dve, dve_c).link
                dve.wait_ge(gb_in, 16)
                dve.tensor_tensor(ga[:, :, :], ga[:, :, :], gate_b[:, :].unsqueeze(1).to_broadcast([P, T, 3 * HEADS]),
                                  ALU.add).then_inc(g_lin, 1)
                dve.wait_ge(masks, 4)
                dve.wait_ge(gated, 1)
                for n, (i, g) in enumerate(steps):
                    dve.wait_ge(cmp_s, n + 1)
                    if n:
                        dve.wait_ge(cmp_t, n)
                    link(dve.tensor_tensor(cs[:, :, :], m.psum[7][:, 0:P].rearrange("p (h c) -> p h c", h=HPG),
                                           cmask[:, i].unsqueeze(1).to_broadcast([P, HPG, CP]), ALU.add))
                    link(dve.tensor_reduce(nmax[:, :], cs[:, :, :], AX.X, ALU.max))
                    dve.tensor_tensor(cs[:, :, :], cs[:, :, :], nmax[:, :].unsqueeze(2).to_broadcast([P, HPG, CP]),
                                      ALU.subtract).then_inc(cmp_sub, 1)
                    for br in range(2):
                        kt = keys(i, br)
                        u = 2 * n + br
                        dve.wait_ge(scored, u + 1)
                        for h in range(HPG):
                            diag = m.psum[h][:, (len(kt) - 1) * P:len(kt) * P]
                            ins = dve.tensor_tensor(diag, diag, m.causal[:, :], ALU.add)
                            if br and i >= WT:
                                far = m.psum[h][:, 0:P]
                                ins = dve.tensor_tensor(far, far, m.beyond[:, :], ALU.add)
                        link(ins)
                        if u:
                            dve.wait_ge(exped, HPG * u)
                        for h in range(HPG):
                            ins = dve.tensor_reduce(nmax[:, h:h + 1], m.psum[h][:, 0:len(kt) * P], AX.X, ALU.max, negate=True)
                        ins.then_inc(maxed, 1)
                        if br == 0:
                            dve.wait_ge(cmp_e, n + 1)
                            link(dve.tensor_tensor(cp[:, :, :], cp[:, :, :], cone[:, i].unsqueeze(1).to_broadcast([P, HPG, CP]), ALU.mult))
                            dve.tensor_reduce(sums[:, 0, :], cp[:, :, :], AX.X, ALU.add).then_inc(cmp_p, 1)
                    dve.wait_ge(summed, n + 1)
                    dve.wait_ge(exped, HPG * (2 * n + 2))
                    link(dve.tensor_scalar(coef[:, :, :], sums[:, :, :], 1e-30, None, ALU.max))
                    link(dve.reciprocal(coef[:, :, :], coef[:, :, :]))
                    link(dve.tensor_tensor(coef[:, :, :], coef[:, :, :],
                                           gate[:, i, g * HPG:(g + 1) * HPG, :].rearrange("p h b -> p b h"), ALU.mult))
                    outs = (m.psum[7][:, 2 * P:4 * P], m.psum[6][:, 0:256], m.psum[6][:, 256:512])
                    for b in range(3):
                        ins = dve.tensor_tensor(part[:, b], outs[b].rearrange("p (h d) -> p h d", h=HPG),
                                                coef[:, b].unsqueeze(2).to_broadcast([P, HPG, HD]), ALU.mult)
                    ins.then_inc(combined, 1)
                    dve.wait_ge(combined, n + 1)
                    link(dve.tensor_tensor(part[:, 0], part[:, 0], part[:, 1], ALU.add))
                    link(dve.tensor_tensor(mix[:, i, g * HPG * HD:(g + 1) * HPG * HD].rearrange("p (h d) -> p h d", h=HPG),
                                           part[:, 0], part[:, 2], ALU.add))


def gla(m, gqk, gv, gr, al, mix):
    m.phase()
    nc, a = m.nc, m.a
    NF = GH * GDK // P
    CAP = 80.0
    with ExitStack() as t:
        alT = m.sb(t, "alT", [GRANK + 1, S])
        wa = m.sb(t, "wa2", [GRANK + 1, GH * GDK])
        tri = m.sb(t, "tri16", [P, P])
        keep = m.sb(t, "keep", [P, GCH])
        la = m.sb(t, "log_a", [P, T, GH * GDK])
        ex = m.sb(t, "ex", [P, T, GH * GDK])
        b = m.sb(t, "b", [P, NF, S])
        qb = m.sb(t, "q_decayed", [P, NF, S])
        qe = m.sb(t, "q_ref", [P, NF, S])
        kl = m.sb(t, "k_last", [P, NF, S])
        ks = m.sb(t, "k_ref", [P, NSUB, S])
        klt = m.sb(t, "k_last_tok", [P, T, NF * P])
        att = m.sb(t, "att", [P, GH, T, P])
        state = m.sb(t, "state", [P, NF, NCH, 2 * GDV])
        dec = m.sb(t, "dec", [P, NF, NCH])
        o = m.sb(t, "gla_o", [P, T, GH * GDV])
        sq = m.sb(t, "gla_sq", [P, T, GH * GDV])
        ms = m.sb(t, "gla_ms", [P, T * GH])
        root = m.sb(t, "gla_root", [P, T * GH])
        og = m.sb(t, "gla_onorm_row", [P, GDV])
        (small_in, made, dve_c, act_c, al_t, al_k, lin, lin_v, absd, exped, plus1, logged, la_done, cum, cum_k,
         d_qb, e_qb, d_qe, e_qe, d_kl, e_kl, d_ks, e_ks, ks_done, q_done, kl_done, kl_t, kl_k, atted, att_k,
         kv_done, kv_k, states, o_done, o_k, silu, mean, rooted) = (m.psem(f"gla_{s}") for s in (
            "small_in", "made", "dve", "act", "al_t", "al_k", "lin", "lin_v", "absd", "exped", "plus1", "logged",
            "la_done", "cum", "cum_k", "d_qb", "e_qb", "d_qe", "e_qe", "d_kl", "e_kl", "d_ks", "e_ks", "ks_done",
            "q_done", "kl_done", "kl_t", "kl_k", "atted", "att_k", "kv_done", "kv_k", "states", "o_done", "o_k",
            "silu", "mean", "rooted"))

        def read_scores(dve, f):
            for h in (2 * f, 2 * f + 1):
                for p in range(2):
                    half = slice(p * GCH, (p + 1) * GCH)
                    src = m.psum[h % 2][half, :].rearrange("p (i c) -> p i c", i=T)[:, :, p * GCH:(p + 1) * GCH]
                    ins = dve.tensor_tensor(att[half, h, :, p * GCH:(p + 1) * GCH], src,
                                            keep[half, :].unsqueeze(1).to_broadcast([GCH, T, GCH]), ALU.mult)
            ins.then_inc(att_k, 1)

        def sub_ref(f):
            return b[:, f, :].rearrange("p (r j) -> p r j", j=SUB)[:, :, SUB // 2:SUB // 2 + 1]

        with nc.Block() as block:
            @block.sync
            def _(sp):
                sp.dma_start(wa[0:GRANK, :], a["gla_wa2"][0]).then_inc(small_in, 16)
                sp.dma_start(wa[GRANK:GRANK + 1, :], a["gla_ba"]).then_inc(small_in, 16)
                sp.dma_start(og[:, :], a["gla_onorm"][0].partition_broadcast(P)).then_inc(small_in, 16)

            @block.gpsimd
            def _(pool):
                pool.memset(alT[:, :], 1.0).then_inc(made, 1)
                pool.memset(tri[:, :], 1.0 / GTAU).then_inc(made, 1)
                pool.memset(keep[:, :], 1.0).then_inc(made, 1)
                pool.memset(att[:, :, :, :], 0.0).then_inc(made, 1)
                pool.memset(state[:, :, :, :], 0.0).then_inc(made, 1)
                pool.wait_ge(made, 5)
                pool.affine_select(out=tri[:, :], in_=tri[:, :], compare_op=ALU.is_ge, fill=0.0, base=0,
                                   pattern=[[1, P]], channel_multiplier=-1).then_inc(made, 1)
                for p in range(2):
                    pool.wait_ge(made, 6 + p)
                    pool.affine_select(out=keep[p * GCH:(p + 1) * GCH, :], in_=keep[p * GCH:(p + 1) * GCH, :],
                                       compare_op=ALU.is_ge, fill=0.0, base=0, pattern=[[1, GCH]],
                                       channel_multiplier=-1).then_inc(made, 1)
                pool.wait_ge(made, 8)
                pool.memset(tri[0:GCH, GCH:P], 0.0).then_inc(made, 1)

            @block.tensor
            def _(pe):
                for i in range(T):
                    ins = pe.transpose(m.psum[0][0:GRANK, i * P:(i + 1) * P], al[:, i, :], m.ident[:, :])
                ins.then_inc(al_t, 1)
                pe.wait_ge(small_in, 48)
                pe.wait_ge(al_k, 1)
                for i in range(T):
                    ins = pe.matmul(m.psum[1 + i // 2][:, (i % 2) * 256:(i % 2 + 1) * 256],
                                    alT[:, i * P:(i + 1) * P], wa[:, :], start=True, stop=True)
                ins.then_inc(lin, 1)
                pe.wait_ge(made, 9)
                pe.wait_ge(la_done, 1)
                for f in range(NF):
                    for i in range(T):
                        ins = pe.matmul(m.psum[3 + f][:, i * P:(i + 1) * P], la[:, i, f * P:(f + 1) * P], tri[:, :],
                                        start=True, stop=True)
                ins.then_inc(cum, 1)
                pe.wait_ge(q_done, 2 * NF)
                for f in range(NF):
                    pe.wait_ge(ks_done, f + 1)
                    for h in (2 * f, 2 * f + 1):
                        half = slice((h % 2) * GDK, (h % 2 + 1) * GDK)
                        for c in range(NCH):
                            for s in range(NSUB):
                                q0 = c * GCH + s * SUB
                                col = (c // 2) * P + (c % 2) * GCH + s * SUB
                                ins = pe.matmul(m.psum[h % 2][(c % 2) * GCH:(c % 2 + 1) * GCH, col:col + SUB],
                                                ks[half, s, c * GCH:(c + 1) * GCH], qe[half, f, q0:q0 + SUB],
                                                start=True, stop=True)
                    ins.then_inc(atted, 1)
                    if f == 0:
                        pe.wait_ge(kl_done, NF)
                        for i in range(T):
                            for f2 in range(NF):
                                ins = pe.transpose(m.psum[2 + i // 2][:, (i % 2) * 256 + f2 * P:(i % 2) * 256 + (f2 + 1) * P],
                                                   kl[:, f2, i * P:(i + 1) * P], m.ident[:, :])
                        ins.then_inc(kl_t, 1)
                        pe.wait_ge(att_k, 1)
                pe.wait_ge(kl_k, 1)
                for c in range(NCH - 1):
                    i, half = c // 2, slice((c % 2) * GCH, (c % 2 + 1) * GCH)
                    for f in range(NF):
                        if c >= 2:
                            pe.wait_ge(states, NF * (c - 1))
                        ins = pe.matmul(m.psum[2 + c % 2][:, f * 256:(f + 1) * 256], klt[half, i, f * P:(f + 1) * P],
                                        gv[half, i, f * 2 * GDV:(f + 1) * 2 * GDV], start=True, stop=True)
                    ins.then_inc(kv_done, 1)
                pe.wait_ge(att_k, NF)
                pe.wait_ge(states, NF * (NCH - 1))
                for i in range(T):
                    out = m.psum[4 + i]
                    for h in range(GH):
                        pe.matmul(out[:, h * GDV:(h + 1) * GDV], att[:, h, i, :], gv[:, i, h * GDV:(h + 1) * GDV],
                                  start=h == 0, stop=False, skip_group_check=True)
                    for c in (2 * i, 2 * i + 1):
                        if c:
                            for f in range(NF):
                                half = slice((c % 2) * GCH, (c % 2 + 1) * GCH)
                                ins = pe.matmul(out[half, f * 256:(f + 1) * 256], qb[:, f, c * GCH:(c + 1) * GCH],
                                                state[:, f, c, :], start=False, stop=True, skip_group_check=True)
                    ins.then_inc(o_done, 1)

            @block.scalar
            def _(act):
                act.wait_ge(absd, 1)
                act.activation(ex[:, :, :], ex[:, :, :], ACT.Exp).then_inc(exped, 1)
                act.wait_ge(plus1, 1)
                act.activation(ex[:, :, :], ex[:, :, :], ACT.Ln).then_inc(logged, 1)
                for f in range(NF):
                    act.wait_ge(cum_k, f + 1)
                    act.activation(qb[:, f, :], b[:, f, :], ACT.Exp).then_inc(e_qb, 1)
                    act.activation(dec[:, f, :], b[:, f, :].rearrange("p (c j) -> p c j", j=GCH)[:, :, GCH - 1], ACT.Exp)
                    act.wait_ge(d_qe, f + 1)
                    act.activation(qe[:, f, :], qe[:, f, :], ACT.Exp).then_inc(e_qe, 1)
                    act.wait_ge(d_kl, f + 1)
                    act.activation(kl[:, f, :], kl[:, f, :], ACT.Exp).then_inc(e_kl, 1)
                for f in range(NF):
                    act.wait_ge(d_ks, f + 1)
                    act.activation(ks[:, :, :], ks[:, :, :], ACT.Exp).then_inc(e_ks, 1)
                    if f == 0:
                        act.wait_ge(kl_t, 1)
                        for i2 in range(2):
                            ins = act.activation(klt[:, 2 * i2:2 * i2 + 2, :], m.psum[2 + i2][:, :].rearrange("p (i f) -> p i f", i=2), ACT.Copy)
                        ins.then_inc(kl_k, 1)
                act.activation(gr[:, :, :], gr[:, :, :], ACT.Silu).then_inc(silu, 1)
                for i in range(T):
                    act.wait_ge(o_done, i + 1)
                    act.activation(o[:, i, :], m.psum[4 + i][:, :], ACT.Copy).then_inc(o_k, 1)
                act.wait_ge(mean, 1)
                act.activation(root[:, :], ms[:, :], ACT.Sqrt).then_inc(rooted, 1)

            @block.vector
            def _(dve):
                link = Chain(dve, dve_c).link
                dve.wait_ge(made, 5)
                dve.wait_ge(al_t, 1)
                dve.tensor_copy(alT[0:GRANK, :], m.psum[0][0:GRANK, :]).then_inc(al_k, 1)
                dve.wait_ge(lin, 1)
                for i2 in range(2):
                    ins = dve.tensor_copy(la[:, 2 * i2:2 * i2 + 2, :], m.psum[1 + i2][:, :].rearrange("p (i f) -> p i f", i=2))
                link(ins)
                dve.scalar_tensor_tensor(out=ex[:, :, :], in0=la[:, :, :], scalar=-1.0, in1=la[:, :, :],
                                         op0=ALU.mult, op1=ALU.min).then_inc(absd, 1)
                dve.wait_ge(exped, 1)
                dve.tensor_scalar(ex[:, :, :], ex[:, :, :], 1.0, None, ALU.add).then_inc(plus1, 1)
                dve.wait_ge(logged, 1)
                dve.scalar_tensor_tensor(out=la[:, :, :], in0=la[:, :, :], scalar=0.0, in1=ex[:, :, :],
                                         op0=ALU.min, op1=ALU.subtract).then_inc(la_done, 1)
                dve.wait_ge(cum, 1)
                for f in range(NF):
                    dve.tensor_copy(b[:, f, :], m.psum[3 + f][:, :]).then_inc(cum_k, 1)
                    dve.wait_ge(cum_k, f + 1)
                    link(dve.tensor_tensor(qe[:, f, :].rearrange("p (r j) -> p r j", j=SUB),
                                           b[:, f, :].rearrange("p (r j) -> p r j", j=SUB),
                                           sub_ref(f).to_broadcast([P, S // SUB, SUB]), ALU.subtract))
                    dve.tensor_scalar(qe[:, f, :], qe[:, f, :], CAP, None, ALU.min).then_inc(d_qe, 1)
                    bc = b[:, f, :].rearrange("p (c j) -> p c j", j=GCH)
                    dve.tensor_tensor(kl[:, f, :].rearrange("p (c j) -> p c j", j=GCH),
                                      bc[:, :, GCH - 1:GCH].to_broadcast([P, NCH, GCH]), bc, ALU.subtract).then_inc(d_kl, 1)
                for f in range(NF):
                    dve.wait_ge(e_qb, f + 1)
                    dve.tensor_tensor(qb[:, f, :], qb[:, f, :], gqk[:, f, :], ALU.mult).then_inc(q_done, 1)
                    dve.wait_ge(e_qe, f + 1)
                    dve.tensor_tensor(qe[:, f, :], qe[:, f, :], gqk[:, f, :], ALU.mult).then_inc(q_done, 1)
                    dve.wait_ge(e_kl, f + 1)
                    dve.tensor_tensor(kl[:, f, :], kl[:, f, :], gqk[:, NF + f, :], ALU.mult).then_inc(kl_done, 1)
                for f in range(NF):
                    if f:
                        dve.wait_ge(atted, f)
                    bc = b[:, f, :].rearrange("p (c j) -> p c j", j=GCH)
                    for s in range(NSUB):
                        at = s * SUB + SUB // 2
                        ins = dve.tensor_tensor(ks[:, s, :].rearrange("p (c j) -> p c j", j=GCH),
                                                bc[:, :, at:at + 1].to_broadcast([P, NCH, GCH]), bc, ALU.subtract)
                    link(ins)
                    dve.tensor_scalar(ks[:, :, :], ks[:, :, :], CAP, None, ALU.min).then_inc(d_ks, 1)
                    if f:
                        dve.wait_ge(made, 8)
                        read_scores(dve, f - 1)
                    dve.wait_ge(e_ks, f + 1)
                    dve.tensor_tensor(ks[:, :, :], ks[:, :, :], gqk[:, NF + f, :].unsqueeze(1).to_broadcast([P, NSUB, S]),
                                      ALU.mult).then_inc(ks_done, 1)
                dve.wait_ge(atted, NF)
                read_scores(dve, NF - 1)
                for c in range(NCH - 1):
                    dve.wait_ge(kv_done, c + 1)
                    for f in range(NF):
                        for h in range(2):
                            half, cols = slice(h * GDK, (h + 1) * GDK), slice(h * GDV, (h + 1) * GDV)
                            ins = dve.scalar_tensor_tensor(
                                out=state[half, f, c + 1, cols], in0=state[half, f, c, cols], scalar=dec[half, f, c:c + 1],
                                in1=m.psum[2 + c % 2][half, f * 256 + h * GDV:f * 256 + (h + 1) * GDV],
                                op0=ALU.mult, op1=ALU.add)
                        ins.then_inc(states, 1)
                    dve.wait_ge(states, NF * (c + 1))
                dve.wait_ge(o_k, T)
                link(dve.tensor_tensor(sq[:, :, :], o[:, :, :], o[:, :, :], ALU.mult))
                link(dve.tensor_reduce(ms[:, :], sq[:, :, :].rearrange("p t (h d) -> p (t h) d", d=GDV), AX.X, ALU.add))
                dve.tensor_scalar(ms[:, :], ms[:, :], 1.0 / GDV, EPS, ALU.mult, ALU.add).then_inc(mean, 1)
                dve.wait_ge(silu, 1)
                link(dve.tensor_tensor(gr[:, :, :], gr[:, :, :], o[:, :, :], ALU.mult))
                link(dve.tensor_tensor(gr[:, :, :].rearrange("p t (h d) -> p (t h) d", d=GDV),
                                       gr[:, :, :].rearrange("p t (h d) -> p (t h) d", d=GDV),
                                       og[:, :].unsqueeze(1).to_broadcast([P, T * GH, GDV]), ALU.mult))
                dve.wait_ge(rooted, 1)
                link(dve.reciprocal(ms[:, :], root[:, :]))
                for i in range(T):
                    ins = dve.tensor_tensor(mix[:, i, HEADS * HD:].rearrange("p (h d) -> p h d", d=GDV),
                                            gr[:, i, :].rearrange("p (h d) -> p h d", d=GDV),
                                            ms[:, i * GH:(i + 1) * GH].unsqueeze(2).to_broadcast([P, GH, GDV]), ALU.mult)
                link(ins)



def split_transpose(m, name, src, hi, lo):
    m.phase()
    turned, hi_out, lo_out = (m.psem(f"{name}_{s}") for s in ("turned", "hi_out", "lo_out"))
    with m.nc.Block() as block:
        @block.tensor
        def _(pe):
            for k in range(KD):
                for t in range(T):
                    ins = pe.transpose(m.psum[k][:, t * P:(t + 1) * P], src[:, t, k * P:(k + 1) * P], m.ident[:, :])
                ins.then_inc(turned, 1)

        @block.scalar
        def _(act):
            for k in range(KD):
                act.wait_ge(turned, k + 1)
                act.activation(hi[:, k, :], m.psum[k][:, :], ACT.Copy).then_inc(hi_out, 1)

        @block.vector
        def _(dve):
            for k in range(KD):
                dve.wait_ge(hi_out, k + 1)
                dve.tensor_tensor(lo[:, k, :], m.psum[k][:, :], hi[:, k, :], ALU.subtract).then_inc(lo_out, 1)


def linear_residual(m, name, first, n_cols, parts):
    m.phase()
    added = m.psem(f"{name}_added")
    total = n_cols * len(parts)

    def add(dve, j):
        n = j // len(parts)
        m.done(dve, first + j)
        for t in range(T):
            cols = slice(n * GC, (n + 1) * GC)
            dve.tensor_tensor(m.x[:, t, cols], m.x[:, t, cols], m.psum[4 * (n % 2) + t][:, :], ALU.add).then_inc(added, 1)

    with m.nc.Block() as block:
        @block.sync
        def _(sp):
            m.load(sp, first + total + 1)

        @block.scalar
        def _(act):
            for j in range(total):
                m.split_hi(act, first + j)

        @block.tensor
        def _(pe):
            for n in range(n_cols):
                if n >= 2:
                    pe.wait_ge(added, T * (n - 1))
                for q, (hi, lo) in enumerate(parts):
                    m.product(pe, first + n * len(parts) + q, False, m.psum[4 * (n % 2):4 * (n % 2) + 4], hi, lo,
                              first=q == 0, last=q == len(parts) - 1)

        @block.vector
        def _(dve):
            for j in range(total):
                m.split_lo(dve, first + j)
                done = j - 1
                if done >= 0 and done % len(parts) == len(parts) - 1:
                    add(dve, done)
            add(dve, total - 1)


def hybrid_layer(m, first, mix_out=None):
    a = m.a
    with ExitStack() as c:
        mix = m.sb(c, "mix", [P, T, D])
        with ExitStack() as c2:
            outputs = qk, v_sw, kvc, gqk, gv, gr, ga, al = projection_outputs(m, c2)
            with ExitStack() as c3:
                hi, lo = m.split_pair(c3, "h_mix0")
                norm_transpose(m, "mix0", m.x, a["norm_mix"][0], T, hi, lo)
                hybrid_projection(m, outputs, first, hi, lo)
            with ExitStack() as c3:
                qkT, kcT, vbd = nsa_prepare(m, c3, qk, kvc)
                nsa_attention(m, qkT, kcT, vbd, v_sw, ga, mix)
            gla(m, gqk, gv, gr, al, mix)
        if mix_out is not None:
            m.phase(); s = m.psem("mixdbg")
            with m.nc.Block() as block:
                @block.sync
                def _(sp):
                    for t in range(T):
                        sp.dma_start(mix_out[t * P:(t + 1) * P, :], mix[:, t, :]).then_inc(s, 16)
                    sp.wait_ge(s, 64)
        hi, lo = m.split_pair(c, "mixT")
        split_transpose(m, "mix0o", mix, hi, lo)
        linear_residual(m, "hyb_out", first + 8, 2, [(hi, lo)])


def project_heads(m, name, first, n_groups, normed, tiles, hi, lo, out, ms):
    m.phase()
    nc = m.nc
    out_act, out_dve = m.psem(f"{name}_out_act"), m.psem(f"{name}_out_dve")
    hpg = GC // XHD
    n_normed = normed // GC
    with ExitStack() as t:
        junk = m.sb(t, f"{name}_junk", [P, GC])
        with nc.Block() as block:
            @block.sync
            def _(sp):
                m.load(sp, first + n_groups + 1)

            @block.tensor
            def _(pe):
                for n in range(n_groups):
                    if n >= 2:
                        pe.wait_ge(out_act, tiles * min(n - 1, n_normed))
                        if n - 1 > n_normed:
                            pe.wait_ge(out_dve, tiles * (n - 1))
                        else:
                            pe.wait_ge(out_dve, tiles * (n - 1))
                    m.product(pe, first + n, False, m.psum[4 * (n % 2):4 * (n % 2) + 4], hi, lo, tiles=tiles)

            @block.scalar
            def _(act):
                m.split_hi(act, first)
                for n in range(n_groups):
                    if n + 1 < n_groups:
                        m.split_hi(act, first + n + 1)
                    if n >= n_normed:
                        continue
                    m.done(act, first + n)
                    for i in range(tiles):
                        for h in range(hpg):
                            ins = act.activation(junk[:, h * XHD:(h + 1) * XHD],
                                                 m.psum[4 * (n % 2) + i][:, h * XHD:(h + 1) * XHD], ACT.Square,
                                                 accum_out=ms[:, i, n * hpg + h:n * hpg + h + 1])
                        ins.then_inc(out_act, 1)
                        act.wait_ge(out_act, n * tiles + i + 1)

            @block.vector
            def _(dve):
                m.split_lo(dve, first)
                for n in range(n_groups):
                    if n + 1 < n_groups:
                        m.split_lo(dve, first + n + 1)
                    m.done(dve, first + n)
                    for i in range(tiles):
                        if n < n_normed:
                            dve.wait_ge(out_act, n * tiles + i + 1)
                        dve.tensor_copy(out[:, i, n * GC:(n + 1) * GC], m.psum[4 * (n % 2) + i][:, :]).then_inc(out_dve, 1)


def norm_heads(m, name, src, tiles, gain, scale, ms, dst):
    m.phase()
    nc = m.nc
    g_in, mean, rooted, normed, turned, out_act, out_dve, dve_c = (
        m.psem(f"{name}_{s}") for s in ("g_in", "mean", "rooted", "normed", "turned", "out_act", "out_dve", "dve"))
    with ExitStack() as t:
        g = m.sb(t, f"{name}_g", [P, XHD])
        root = m.sb(t, f"{name}_root", [P, tiles * XH])
        with nc.Block() as block:
            @block.sync
            def _(sp):
                sp.dma_start(g[:, :], gain.partition_broadcast(P)).then_inc(g_in, 16)

            @block.scalar
            def _(act):
                act.wait_ge(mean, 1)
                act.activation(root[:, :], ms[:, :, :].rearrange("p t h -> p (t h)"), ACT.Sqrt).then_inc(rooted, 1)
                for k in range(0, KD, 2):
                    act.wait_ge(turned, k + 1)
                    act.activation(dst[:, k, :], m.psum[k][:, 0:tiles * P], ACT.Copy).then_inc(out_act, 1)

            @block.vector
            def _(dve):
                link = Chain(dve, dve_c).link
                dve.tensor_scalar(ms[:, :, :], ms[:, :, :], 1.0 / XHD, EPS, ALU.mult, ALU.add).then_inc(mean, 1)
                dve.wait_ge(g_in, 16)
                link(dve.tensor_scalar(g[:, :], g[:, :], scale, None, ALU.mult))
                dve.wait_ge(rooted, 1)
                link(dve.reciprocal(ms[:, :, :].rearrange("p t h -> p (t h)"), root[:, :]))
                for i in range(tiles):
                    for h in range(XH):
                        cols = slice(h * XHD, (h + 1) * XHD)
                        ins = dve.scalar_tensor_tensor(out=src[:, i, cols], in0=src[:, i, cols], scalar=ms[:, i, h:h + 1],
                                                       in1=g[:, :], op0=ALU.mult, op1=ALU.mult)
                    ins.then_inc(normed, 1)
                for k in range(1, KD, 2):
                    dve.wait_ge(turned, k + 1)
                    dve.tensor_copy(dst[:, k, :], m.psum[k][:, 0:tiles * P]).then_inc(out_dve, 1)

            @block.tensor
            def _(pe):
                pe.wait_ge(normed, tiles)
                for k in range(KD):
                    for i in range(tiles):
                        ins = pe.transpose(m.psum[k][:, i * P:(i + 1) * P], src[:, i, k * P:(k + 1) * P], m.ident[:, :])
                    ins.then_inc(turned, 1)


def cross_attend(m, name, qT, kT, v, o_hi, o_lo):
    m.phase()
    nc = m.nc
    HH = XHD // P
    units = [(h, i) for h in range(XH) for i in range(T)]
    (scored, maxed, exped, normed, turned, kept, summed, o_hi_out, o_lo_out, dve_c) = (m.psem(f"{name}_{s}") for s in (
        "scored", "maxed", "exped", "normed", "turned", "kept", "summed", "o_hi_out", "o_lo_out", "dve"))
    with ExitStack() as t:
        prob = m.sb(t, f"{name}_prob", [P, 2, N_MEM])
        pT = m.sb(t, f"{name}_pT", [P, 2, MT, S])
        nmax = m.sb(t, f"{name}_nmax", [P, len(units)])
        sums = m.sb(t, f"{name}_sums", [P, len(units)])
        with nc.Block() as block:
            @block.tensor
            def _(pe):
                def score(u):
                    h, i = units[u]
                    if u >= 2:
                        pe.wait_ge(exped, u - 1)
                    for d in range(HH):
                        ins = pe.matmul(m.psum[u % 2][:, 0:N_MEM], qT[:, HH * h + d, i * P:(i + 1) * P], kT[:, HH * h + d, :],
                                        start=d == 0, stop=d == HH - 1)
                    ins.then_inc(scored, 1)

                score(0)
                for u, (h, i) in enumerate(units):
                    if u + 1 < len(units):
                        score(u + 1)
                    pe.wait_ge(normed, u + 1)
                    if u >= 2:
                        pe.wait_ge(kept, u - 1)
                    for j in range(MT):
                        ins = pe.transpose(m.psum[2 + u % 2][:, j * P:(j + 1) * P], prob[:, u % 2, j * P:(j + 1) * P], m.ident[:, :])
                    ins.then_inc(turned, 1)
                    if i == T - 1:
                        pe.wait_ge(kept, u + 1)
                        if h >= 2:
                            pe.wait_ge(o_lo_out, HH * (h - 1))
                        for d in range(HH):
                            for j in range(MT):
                                ins = pe.matmul(m.psum[4 + 2 * (h % 2) + d][:, :], v[:, j, h * XHD + d * P:h * XHD + (d + 1) * P],
                                                pT[:, h % 2, j, :], start=j == 0, stop=j == MT - 1)
                            ins.then_inc(summed, 1)

            @block.scalar
            def _(act):
                def keep(u):
                    h, i = units[u]
                    act.wait_ge(turned, u + 1)
                    if h >= 2 and i == 0:
                        act.wait_ge(summed, HH * (h - 1))
                    act.activation(pT[:, h % 2, :, i * P:(i + 1) * P],
                                   m.psum[2 + u % 2][:, 0:MT * P].rearrange("p (j t) -> p j t", j=MT), ACT.Copy).then_inc(kept, 1)

                def output(h):
                    for d in range(HH):
                        act.wait_ge(summed, HH * h + d + 1)
                        act.activation(o_hi[:, HH * h + d, :], m.psum[4 + 2 * (h % 2) + d][:, :], ACT.Copy).then_inc(o_hi_out, 1)

                for u, (h, i) in enumerate(units):
                    act.wait_ge(maxed, u + 1)
                    if u >= 2:
                        act.wait_ge(turned, u - 1)
                    act.activation(prob[:, u % 2, :], m.psum[u % 2][:, 0:N_MEM], ACT.Exp, bias=nmax[:, u:u + 1],
                                   accum_out=sums[:, u:u + 1]).then_inc(exped, 1)
                    if u:
                        keep(u - 1)
                    if h and i == 1:
                        output(h - 1)
                keep(len(units) - 1)
                output(XH - 1)

            @block.vector
            def _(dve):
                link = Chain(dve, dve_c).link

                def maximum(u):
                    dve.wait_ge(scored, u + 1)
                    dve.tensor_reduce(nmax[:, u:u + 1], m.psum[u % 2][:, 0:N_MEM], AX.X, ALU.max, negate=True).then_inc(maxed, 1)

                def rest(h):
                    for d in range(HH):
                        dve.wait_ge(o_hi_out, HH * h + d + 1)
                        dve.tensor_tensor(o_lo[:, HH * h + d, :], m.psum[4 + 2 * (h % 2) + d][:, :], o_hi[:, HH * h + d, :],
                                          ALU.subtract).then_inc(o_lo_out, 1)

                maximum(0)
                for u, (h, i) in enumerate(units):
                    if u + 1 < len(units):
                        maximum(u + 1)
                    dve.wait_ge(exped, u + 1)
                    link(dve.reciprocal(sums[:, u:u + 1], sums[:, u:u + 1]))
                    dve.tensor_scalar(prob[:, u % 2, :], prob[:, u % 2, :], sums[:, u:u + 1], None, ALU.mult).then_inc(normed, 1)
                    if h and i == 2:
                        rest(h - 1)
                rest(XH - 1)


def cross_attention(m, layer, first):
    a, nm = m.a, f"x{layer}"
    with ExitStack() as c:
        kT = m.sb(c, f"{nm}_kT", [P, KD, N_MEM])
        v = m.sb(c, f"{nm}_kv", [P, MT, 2 * D])
        with ExitStack() as c2:
            mem = m.sb(c2, f"{nm}_mem", [P, MT, D])
            ms = m.sb(c2, f"{nm}_kms", [P, MT, XH])
            m.phase()
            loaded = m.psem(f"{nm}_mem_in")
            with m.nc.Block() as block:
                @block.sync
                def _(sp):
                    for i in range(MT):
                        sp.dma_start(mem[:, i, :], a["mem"][0, i * P:(i + 1) * P, :]).then_inc(loaded, 16)
                    sp.wait_ge(loaded, 16 * MT)
            hi, lo = m.split_pair(c2, f"{nm}_mem", n=N_MEM)
            norm_transpose(m, f"{nm}_nm", mem, a["norm_mem"][layer], MT, hi, lo)
            project_heads(m, f"{nm}_kv", first, 4, D, MT, hi, lo, v, ms)
            norm_heads(m, f"{nm}_kn", v, MT, a["x_knorm"][layer], 1.0, ms, kT)
        qT = m.sb(c, f"{nm}_qT", [P, KD, S])
        with ExitStack() as c2:
            q = m.sb(c2, f"{nm}_q", [P, T, D])
            ms = m.sb(c2, f"{nm}_qms", [P, T, XH])
            hi, lo = m.split_pair(c2, f"{nm}_h")
            norm_transpose(m, f"{nm}_nx", m.x, a["norm_xattn"][layer], T, hi, lo)
            project_heads(m, f"{nm}_q", first + 4, 2, D, T, hi, lo, q, ms)
            norm_heads(m, f"{nm}_qn", q, T, a["x_qnorm"][layer], XHD ** -0.5, ms, qT)
        o_hi, o_lo = m.split_pair(c, f"{nm}_o")
        cross_attend(m, f"{nm}_at", qT, kT, v[:, :, D:2 * D], o_hi, o_lo)
        linear_residual(m, f"{nm}_wo", first + 6, 2, [(o_hi, o_lo)])


def sgu_layer(m, layer, first):
    nc, a = m.nc, m.a
    NGR = SGW // GC
    KU = SGW // P
    with ExitStack() as c:
        uT = m.sb(c, "uT", [P, KU, S])
        v = m.sb(c, "sg_v", [P, T, SGW])
        wsT = m.sb(c, "sg_wsT", [P, SGG, P])
        bsr = m.sb(c, "sg_bs_row", [P, SGG, P])
        vsum = m.sb(c, "sg_vsum", [P, T, NGR])
        with ExitStack() as c2:
            hi, lo = m.split_pair(c2, "h_sg")
            norm_transpose(m, "mix1", m.x, a["norm_mix"][layer], T, hi, lo)
            m.phase()
            read = m.psem("sg_read")
            with nc.Block() as block:
                @block.sync
                def _(sp):
                    m.load(sp, first + 2 * NGR + 1)

                @block.tensor
                def _(pe):
                    for n in range(2 * NGR):
                        if n >= 2:
                            pe.wait_ge(read, 4 * (n - 1))
                        m.product(pe, first + n, n < NGR, m.psum[4 * (n % 2):4 * (n % 2) + 4], hi, lo)

                @block.scalar
                def _(act):
                    m.split_hi(act, first)
                    for n in range(2 * NGR):
                        if n + 1 < 2 * NGR:
                            m.split_hi(act, first + n + 1)
                        m.done(act, first + n)
                        for b in range(4):
                            ps = m.psum[4 * (n % 2) + b][:, :]
                            if n < NGR:
                                act.activation(uT[:, 4 * n + b, :], ps, ACT.Gelu_apprx_tanh).then_inc(read, 1)
                            else:
                                j = n - NGR
                                act.activation(v[:, b, j * GC:(j + 1) * GC], ps, ACT.Gelu_apprx_tanh,
                                               accum_out=vsum[:, b, j:j + 1]).then_inc(read, 1)

                @block.vector
                def _(dve):
                    for n in range(2 * NGR):
                        m.split_lo(dve, first + n)
        with ExitStack() as c2:
            ws = m.sb(c2, "sgu_ws", [P, SGG, P])
            g = m.sb(c2, "sgu_g", [P, SGW])
            b = m.sb(c2, "sgu_b", [P, SGW])
            nmean = m.sb(c2, "sg_nmean", [P, T])
            m.phase()
            var = m.sb(c2, "sg_var", [P, T])
            root = m.sb(c2, "sg_root", [P, T])
            (small_in, ws_in, ws_masked, mean, squared, varied, rooted, dve_c, centred, gained, turned, ws_out) = (
                m.psem(f"sg_{s}") for s in ("small_in", "ws_in", "ws_masked", "mean", "squared", "varied", "rooted", "dve",
                                           "centred", "gained", "turned", "ws_out"))
            junk = m.sb(c2, "sg_junk", [P, SGW])
            with nc.Block() as block:
                @block.sync
                def _(sp):
                    sp.dma_start(ws[:, :, :], a["sg_ws"][0].rearrange("g t s -> t g s")).then_inc(ws_in, 16)
                    sp.dma_start(g[:, :], a["sg_ln_g"][0].partition_broadcast(P)).then_inc(small_in, 16)
                    sp.dma_start(b[:, :], a["sg_ln_b"][0].partition_broadcast(P)).then_inc(small_in, 16)
                    sp.dma_start(bsr[:, :, :], a["sg_bs"][0].partition_broadcast(P)).then_inc(small_in, 16)

                @block.gpsimd
                def _(pool):
                    pool.wait_ge(ws_in, 16)
                    pool.affine_select(out=ws[:, :, :], in_=ws[:, :, :], compare_op=ALU.is_ge, fill=0.0, base=0,
                                       pattern=[[0, SGG], [-1, P]], channel_multiplier=1).then_inc(ws_masked, 1)
                    pool.wait_ge(small_in, 48)
                    for i in range(T):
                        pool.wait_ge(centred, i + 1)
                        pool.tensor_tensor(v[:, i, :], v[:, i, :], g[:, :], ALU.mult).then_inc(gained, 1)

                @block.scalar
                def _(act):
                    act.wait_ge(mean, 1)
                    for i in range(T):
                        if i:
                            act.wait_ge(squared, i)
                        act.activation(junk[:, :], v[:, i, :], ACT.Square, bias=nmean[:, i:i + 1],
                                       accum_out=var[:, i:i + 1]).then_inc(squared, 1)
                    act.wait_ge(varied, 1)
                    act.activation(root[:, :], var[:, :], ACT.Sqrt).then_inc(rooted, 1)
                    for q in range(2):
                        act.wait_ge(turned, q + 1)
                        act.activation(wsT[:, 4 * q:4 * q + 4, :], m.psum[q][:, :].rearrange("p (g t) -> p g t", g=4), ACT.Copy)

                @block.vector
                def _(dve):
                    link = Chain(dve, dve_c).link
                    link(dve.tensor_reduce(nmean[:, :], vsum[:, :, :], AX.X, ALU.add))
                    dve.tensor_scalar(nmean[:, :], nmean[:, :], -1.0 / SGW, None, ALU.mult).then_inc(mean, 1)
                    dve.wait_ge(squared, T)
                    dve.tensor_scalar(var[:, :], var[:, :], 1.0 / SGW, EPS, ALU.mult, ALU.add).then_inc(varied, 1)
                    dve.wait_ge(rooted, 1)
                    link(dve.reciprocal(var[:, :], root[:, :]))
                    for i in range(T):
                        dve.tensor_scalar(v[:, i, :], v[:, i, :], nmean[:, i:i + 1], var[:, i:i + 1], ALU.add, ALU.mult)\
                           .then_inc(centred, 1)
                    for i in range(T):
                        dve.wait_ge(gained, i + 1)
                        ins = dve.tensor_tensor(v[:, i, :], v[:, i, :], b[:, :], ALU.add)
                    link(ins)

                @block.tensor
                def _(pe):
                    pe.wait_ge(ws_masked, 1)
                    for q in range(2):
                        for j in range(4):
                            ins = pe.transpose(m.psum[q][:, j * P:(j + 1) * P], ws[:, 4 * q + j, :], m.ident[:, :])
                        ins.then_inc(turned, 1)
        um_hi, um_lo = m.split_pair(c, "um", k=KU)
        m.phase()
        mixed, biased, gated, split, lo_out = (m.psem(f"sg_{s}") for s in ("mixed", "biased", "gated", "split", "lo_out"))
        with nc.Block() as block:
            @block.tensor
            def _(pe):
                for k in range(KU):
                    if k >= 8:
                        pe.wait_ge(biased, k - 7)
                    for i in range(T):
                        ins = pe.matmul(m.psum[k % 8][:, i * P:(i + 1) * P], v[:, i, k * P:(k + 1) * P],
                                        wsT[:, k * SGG // KU, :], start=True, stop=True)
                    ins.then_inc(mixed, 1)

            @block.vector
            def _(dve):
                for k in range(KU):
                    dve.wait_ge(mixed, k + 1)
                    dve.tensor_tensor(m.psum[k % 8][:, :].rearrange("p (i t) -> p i t", i=T),
                                      m.psum[k % 8][:, :].rearrange("p (i t) -> p i t", i=T),
                                      bsr[:, k * SGG // KU, :].unsqueeze(1).to_broadcast([P, T, P]), ALU.add).then_inc(split, 1)
                    dve.wait_ge(split, k + 1)
                    dve.tensor_tensor(uT[:, k, :], uT[:, k, :], m.psum[k % 8][:, :], ALU.mult).then_inc(biased, 1)

            @block.scalar
            def _(act):
                for k in range(KU):
                    act.wait_ge(biased, k + 1)
                    act.activation(um_hi[:, k, :], uT[:, k, :], ACT.Copy).then_inc(gated, 1)

            @block.gpsimd
            def _(pool):
                for k in range(KU):
                    pool.wait_ge(gated, k + 1)
                    pool.tensor_tensor(um_lo[:, k, :], uT[:, k, :], um_hi[:, k, :], ALU.subtract).then_inc(lo_out, 1)
                pool.wait_ge(lo_out, KU)
        linear_residual(m, "sg_out", first + 2 * NGR, 2, [(um_hi[:, 0:KD], um_lo[:, 0:KD]), (um_hi[:, KD:KU], um_lo[:, KD:KU])])


def moe_route(m, layer, hT, slot_i, wgt, meta, idx_dram):
    m.phase()
    nc, a, nm = m.nc, m.a, f"r{layer}"
    NB = MAXB + 1
    with ExitStack() as t:
        def tile(name, shape, dt=F32):
            return m.sb(t, f"{nm}_{name}", shape, dt)
        rw = tile("rw", [P, KD, NE])
        rb = tile("rb", [P, NE])
        ones, before = tile("ones", [P, P]), tile("before", [P, P])
        e_row, g_row, b_row, thr = tile("e_row", [P, NE]), tile("g_row", [P, NG]), tile("b_row", [P, NB]), tile("thr", [P, T])
        lower = tile("lower", [P, NE, NE])
        zeros_i = tile("zeros_i", [P, SLOTS // P], I32)
        tok_i = tile("tok_i", [P, T], I32)
        lg, pr = tile("lg", [P, T, NE]), tile("pr", [P, T, NE])
        mx, sm = tile("mx", [P, T]), tile("sm", [P, T])
        gm, ge = tile("gm", [P, T, NG]), tile("ge", [P, T, NG])
        gb, gi = tile("gb", [P, T]), tile("gi", [P, T])
        pm, cand = tile("pm", [P, T, NE]), tile("cand", [P, T, NE])
        top, ti = tile("top", [P, 2, T]), tile("ti", [P, 2, T])
        oh = tile("oh", [P, 2, T, NE])
        both = tile("both", [P, T, NE])
        cnt, nb, nbx = tile("cnt", [P, NE]), tile("nb", [P, NE]), tile("nbx", [P, NE, T])
        low, cum, off = tile("low", [P, NE, NE]), tile("cum", [P, NE]), tile("off", [P, NE])
        rank = tile("rank", [P, T, NE])
        sl, slot_f = tile("sl", [P, 2, T, NE]), tile("slot_f", [P, 2, T])
        be, ebf = tile("be", [P, NB, NE]), tile("ebf", [P, NB + 1])
        (ins_in, made, dve_c, logits, maxed, exped, counted, counts, zeroed, slots_at) = (m.psem(f"{nm}_{s}") for s in (
            "ins_in", "made", "dve", "logits", "maxed", "exped", "counted", "counts", "zeroed", "slots_at"))
        scattered = m.sem(f"{nm}_scattered")
        with nc.Block() as block:
            @block.sync
            def _(sp):
                sp.dma_start(rw[:, :, :], a["router_w"].rearrange("(k p) e -> p k e", p=P)).then_inc(ins_in, 16)
                sp.dma_start(rb[:, :], a["router_b"].partition_broadcast(P)).then_inc(ins_in, 16)
                sp.wait_ge(made, 1)
                with nc.allow_non_contiguous_dma(reason="a small table of slots"):
                    sp.dma_start(idx_dram.rearrange("(b p) o -> p (b o)", p=P), zeros_i[:, :]).then_inc(zeroed, 16)
                sp.wait_ge(zeroed, 16)

            @block.gpsimd
            def _(pool):
                pool.memset(zeros_i[:, :], 0).then_inc(made, 1)
                pool.memset(ones[:, :], 1.0).then_inc(made, 1)
                pool.memset(before[:, :], 1.0).then_inc(made, 1)
                pool.memset(lower[:, :, :], 1.0).then_inc(made, 1)
                for row, n, base, step in ((e_row, NE, -NE, 1), (g_row, NG, -NG, 1), (b_row, NB, 0, 1), (thr, T, 0, P)):
                    pool.iota(row[:, :], pattern=[[step, n]], base=base, channel_multiplier=0,
                              allow_small_or_imprecise_dtypes=True).then_inc(made, 1)
                pool.iota(tok_i[:, :], pattern=[[P, T]], base=0, channel_multiplier=1).then_inc(made, 1)
                pool.wait_ge(made, 9)
                pool.affine_select(out=before[:, :], in_=before[:, :], compare_op=ALU.is_gt, fill=0.0, base=0,
                                   pattern=[[1, P]], channel_multiplier=-1).then_inc(made, 1)
                pool.affine_select(out=lower[:, :, :], in_=lower[:, :, :], compare_op=ALU.is_ge, fill=0.0, base=0,
                                   pattern=[[1, NE], [-1, NE]], channel_multiplier=0).then_inc(made, 1)
                pool.wait_ge(made, 11)
                pool.wait_ge(zeroed, 16)
                pool.wait_ge(slots_at, 1)
                for c in range(2):
                    for i in range(T):
                        pool.indirect_dma_start(out=idx_dram, out_offset=bass.IndirectOffsetOnAxis(ap=slot_i[:, c * T + i:c * T + i + 1], axis=0),
                                                in_=tok_i[:, i:i + 1], in_offset=None).then_inc(scattered, 16)
                pool.wait_ge(scattered, 16 * 2 * T)

            @block.tensor
            def _(pe):
                pe.wait_ge(ins_in, 32)
                for i in range(T):
                    for k in range(KD):
                        ins = pe.matmul(m.psum[0][:, i * NE:(i + 1) * NE], hT[:, k, i * P:(i + 1) * P], rw[:, k, :],
                                        start=k == 0, stop=k == KD - 1)
                ins.then_inc(logits, 1)
                pe.wait_ge(made, 11)
                pe.wait_ge(counted, 1)
                for i in range(T):
                    for j in range(i + 1):
                        pe.matmul(m.psum[1][:, i * NE:(i + 1) * NE], before[:, :] if j == i else ones[:, :], both[:, j, :],
                                  start=j == 0, stop=j == i)
                for j in range(T):
                    ins = pe.matmul(m.psum[1][:, T * NE:(T + 1) * NE], ones[:, :], both[:, j, :], start=j == 0, stop=j == T - 1)
                ins.then_inc(counts, 1)

            @block.scalar
            def _(act):
                act.wait_ge(maxed, 1)
                act.activation(pr[:, :, :], lg[:, :, :], ACT.Exp).then_inc(exped, 1)

            @block.vector
            def _(dve):
                link = Chain(dve, dve_c).link

                def wide(x, n):
                    return x.unsqueeze(2).to_broadcast([P, T, n])

                def row(x, n):
                    return x[:, :].unsqueeze(1).to_broadcast([P, T, n])

                dve.wait_ge(ins_in, 32)
                dve.wait_ge(made, 11)
                dve.wait_ge(logits, 1)
                link(dve.tensor_tensor(lg[:, :, :], m.psum[0][:, 0:T * NE].rearrange("p (t e) -> p t e", e=NE), row(rb, NE), ALU.add))
                link(dve.tensor_reduce(mx[:, :], lg[:, :, :], AX.X, ALU.max))
                dve.tensor_tensor(lg[:, :, :], lg[:, :, :], wide(mx[:, :], NE), ALU.subtract).then_inc(maxed, 1)
                dve.wait_ge(exped, 1)
                link(dve.tensor_reduce(sm[:, :], pr[:, :, :], AX.X, ALU.add))
                link(dve.reciprocal(sm[:, :], sm[:, :]))
                link(dve.tensor_tensor(pr[:, :, :], pr[:, :, :], wide(sm[:, :], NE), ALU.mult))
                link(dve.tensor_reduce(gm[:, :, :], pr[:, :, :].rearrange("p t (g e) -> p t g e", e=EPG), AX.X, ALU.max))
                link(dve.tensor_reduce(gb[:, :], gm[:, :, :], AX.X, ALU.max))
                link(dve.tensor_tensor(ge[:, :, :], gm[:, :, :], wide(gb[:, :], NG), ALU.is_equal))
                link(dve.tensor_tensor(ge[:, :, :], ge[:, :, :], row(g_row, NG), ALU.mult))
                link(dve.tensor_reduce(gi[:, :], ge[:, :, :], AX.X, ALU.min))
                link(dve.tensor_tensor(ge[:, :, :], row(g_row, NG), wide(gi[:, :], NG), ALU.is_equal))
                for e in range(EPG):
                    ins = dve.tensor_scalar(cand[:, :, e::EPG], ge[:, :, :], 2.0, -2.0, ALU.mult, ALU.add)
                link(ins)
                link(dve.tensor_tensor(pm[:, :, :], pr[:, :, :], cand[:, :, :], ALU.add))
                for c in range(2):
                    link(dve.tensor_reduce(top[:, c, :], pm[:, :, :], AX.X, ALU.max))
                    link(dve.tensor_tensor(cand[:, :, :], pm[:, :, :], wide(top[:, c, :], NE), ALU.is_equal))
                    link(dve.tensor_tensor(cand[:, :, :], cand[:, :, :], row(e_row, NE), ALU.mult))
                    link(dve.tensor_reduce(ti[:, c, :], cand[:, :, :], AX.X, ALU.min))
                    link(dve.tensor_tensor(oh[:, c], row(e_row, NE), wide(ti[:, c, :], NE), ALU.is_equal))
                    if c == 0:
                        link(dve.scalar_tensor_tensor(out=pm[:, :, :], in0=oh[:, 0], scalar=-4.0, in1=pm[:, :, :],
                                                      op0=ALU.mult, op1=ALU.add))
                link(dve.tensor_tensor(sm[:, :], top[:, 0, :], top[:, 1, :], ALU.add))
                link(dve.reciprocal(sm[:, :], sm[:, :]))
                for c in range(2):
                    dve.tensor_tensor(wgt[:, c * T:(c + 1) * T], top[:, c, :], sm[:, :], ALU.mult)
                dve.tensor_tensor(both[:, :, :], oh[:, 0], oh[:, 1], ALU.add).then_inc(counted, 1)
                dve.wait_ge(counts, 1)
                link(dve.tensor_copy(cnt[:, :], m.psum[1][:, T * NE:(T + 1) * NE]))
                link(dve.tensor_tensor(nbx[:, :, :], cnt[:, :].unsqueeze(2).to_broadcast([P, NE, T]),
                                       thr[:, :].unsqueeze(1).to_broadcast([P, NE, T]), ALU.is_gt))
                link(dve.tensor_reduce(nb[:, :], nbx[:, :, :], AX.X, ALU.add))
                link(dve.tensor_tensor(low[:, :, :], lower[:, :, :], nb[:, :].unsqueeze(1).to_broadcast([P, NE, NE]), ALU.mult))
                link(dve.tensor_reduce(cum[:, :], low[:, :, :], AX.X, ALU.add))
                link(dve.tensor_tensor(off[:, :], cum[:, :], nb[:, :], ALU.subtract))
                link(dve.scalar_tensor_tensor(out=rank[:, :, :], in0=off[:, :].unsqueeze(1).to_broadcast([P, T, NE]), scalar=float(P),
                                              in1=m.psum[1][:, 0:T * NE].rearrange("p (t e) -> p t e", e=NE),
                                              op0=ALU.mult, op1=ALU.add))
                for c in range(2):
                    ins = dve.tensor_tensor(sl[:, c], oh[:, c], rank[:, :, :], ALU.mult)
                link(ins)
                for c in range(2):
                    ins = dve.tensor_reduce(slot_f[:, c, :], sl[:, c], AX.X, ALU.add)
                link(ins)
                dve.tensor_copy(slot_i[:, :], slot_f[:, :, :].rearrange("p c t -> p (c t)")).then_inc(slots_at, 1)
                link(dve.tensor_tensor(be[:, :, :], b_row[:, :].unsqueeze(2).to_broadcast([P, NB, NE]),
                                       cum[:, :].unsqueeze(1).to_broadcast([P, NB, NE]), ALU.is_ge))
                link(dve.tensor_reduce(ebf[:, 0:NB], be[:, :, :], AX.X, ALU.add))
                dve.tensor_scalar(ebf[:, 0:NB], ebf[:, 0:NB], float(NE - 1), None, ALU.min)
                link(dve.tensor_copy(ebf[:, NB:NB + 1], cum[:, NE - 1:NE]))
                link(dve.tensor_copy(meta[:, :], ebf[0:1, :]))


def moe_experts(m, layer, meta, h_dram, idx_dram, y_dram):
    m.phase()
    nc, a, nm = m.nc, m.a, f"e{layer}"
    NB = MAXB + 1
    CI, CO = 4, DE // P
    KC = KD // CI
    w_in = a["moe_w_in"][layer].rearrange("e d n -> (e d) n")
    w_out = a["moe_w_out"][layer].rearrange("e f n -> (e f) n")
    gate_ps, up_ps, turn_ps, act_ps, y_ps = m.psum[0], m.psum[1], m.psum[2:4], m.psum[4], m.psum[5:7]
    with ExitStack() as t:
        wi = [m.sb(t, f"{nm}_wi{q}", [P, KC, 2 * DE]) for q in range(CI)]
        wo = [m.sb(t, f"{nm}_wo{q}", [P, D]) for q in range(CO)]
        ix = m.sb(t, f"{nm}_ix", [P, 1], I32)
        hx = m.sb(t, f"{nm}_hx", [P, D])
        hxT = m.sb(t, f"{nm}_hxT", [P, KD, P])
        sg = m.sb(t, f"{nm}_silu", [P, DE])
        au = m.sb(t, f"{nm}_act", [P, DE])
        auT = m.sb(t, f"{nm}_actT", [P, CO, P])
        y = m.sb(t, f"{nm}_y", [P, D])
        wi_in = [m.psem(f"{nm}_wi_in{q}") for q in range(CI)]
        wo_in = [m.psem(f"{nm}_wo_in{q}") for q in range(CO)]
        wi_used = [m.psem(f"{nm}_wi_used{q}") for q in range(CI)]
        wo_used = [m.psem(f"{nm}_wo_used{q}") for q in range(CO)]
        passed = m.psem(f"{nm}_passed")
        ix_in, hx_in = m.sem(f"{nm}_ix_in"), m.sem(f"{nm}_hx_in")
        (h_turned, hT_act, hT_dve, silued, multiplied, a_turned, aT_out, y_act, y_dve, stored) = (
            m.psem(f"{nm}_{s}") for s in ("h_turned", "hT_act", "hT_dve", "silued", "multiplied",
                                         "a_turned", "aT_out", "y_act", "y_dve", "stored"))

        def blocks(engine):
            return engine.value_load(meta[0:1, NB:NB + 1], min_val=1, max_val=MAXB)

        with nc.Block() as block:
            @block.sync
            def _(sp):
                with sp.Fori(0, blocks(sp)) as b:
                    e = sp.value_load(meta[0:1, bass.ds(b, 1)], min_val=0, max_val=NE - 1)
                    for q in range(CI):
                        sp.wait_ge(wi_used[q], b + 1)
                        sp.dma_start(wi[q][:, :, :], w_in[bass.ds(e * D + q * KC * P, KC * P), :]
                                     .rearrange("(k p) n -> p k n", p=P)).then_inc(wi_in[q], 16)
                    for q in range(CO):
                        sp.wait_ge(wo_used[q], b + 1)
                        sp.dma_start(wo[q][:, :], w_out[bass.ds(e * DE + q * P, P), :]).then_inc(wo_in[q], 16)

            @block.gpsimd
            def _(pool):
                with pool.Fori(0, blocks(pool) + 1) as b:
                    pool.wait_ge(h_turned, b + 1)
                    pool.dma_start(ix[:, :], idx_dram[bass.ds(b * P, P), :]).then_inc(ix_in, 16)
                    pool.wait_ge(ix_in, b * 16 + 16)
                    pool.sem_inc(passed, 1)
                    pool.indirect_dma_start(out=hx[:, :], out_offset=None, in_=h_dram,
                                            in_offset=bass.IndirectOffsetOnAxis(ap=ix[:, 0:1], axis=0)).then_inc(hx_in, 16)
                pool.wait_ge(h_turned, blocks(pool) + 2)

            @block.tensor
            def _(pe):
                def turn_tokens(b):
                    pe.wait_ge(hx_in, b * 16 + 16)
                    for k in range(KD):
                        ins = pe.transpose(turn_ps[k // 4][:, (k % 4) * P:(k % 4 + 1) * P], hx[:, k * P:(k + 1) * P], m.ident[:, :])
                    ins.then_inc(h_turned, 1)

                for free in wi_used + wo_used + [h_turned]:
                    pe.sem_inc(free, 1)
                turn_tokens(0)
                with pe.Fori(0, blocks(pe)) as b:
                    pe.wait_ge(hT_act, b + 1)
                    pe.wait_ge(hT_dve, b + 1)
                    for q in range(CI):
                        pe.wait_ge(wi_in[q], b * 16 + 16)
                        for kk in range(KC):
                            k = q * KC + kk
                            pe.matmul(gate_ps[:, 0:DE], hxT[:, k, :], wi[q][:, kk, 0:DE], start=k == 0, stop=k == KD - 1)
                            ins = pe.matmul(up_ps[:, 0:DE], hxT[:, k, :], wi[q][:, kk, DE:2 * DE], start=k == 0, stop=k == KD - 1)
                        ins.then_inc(wi_used[q], 1)
                    turn_tokens(b + 1)
                    pe.wait_ge(multiplied, b + 1)
                    for f in range(CO):
                        ins = pe.transpose(act_ps[:, f * P:(f + 1) * P], au[:, f * P:(f + 1) * P], m.ident[:, :])
                    ins.then_inc(a_turned, 1)
                    pe.wait_ge(aT_out, b + 1)
                    pe.wait_ge(y_act, b + 1)
                    pe.wait_ge(y_dve, b + 1)
                    for f in range(CO):
                        pe.wait_ge(wo_in[f], b * 16 + 16)
                        for n in range(2):
                            ins = pe.matmul(y_ps[n][:, :], auT[:, f, :], wo[f][:, n * GC:(n + 1) * GC], start=f == 0, stop=f == CO - 1)
                        ins.then_inc(wo_used[f], 1)

            @block.scalar
            def _(act):
                act.sem_inc(y_act, 1)
                act.sem_inc(stored, 16)
                act.wait_ge(h_turned, 2)
                act.activation(hxT[:, 0:4, :], turn_ps[0][:, :].rearrange("p (k t) -> p k t", k=4), ACT.Copy).then_inc(hT_act, 1)
                nb = blocks(act)
                with act.Fori(0, nb) as b:
                    act.wait_ge(wi_used[CI - 1], b + 2)
                    act.activation(sg[:, :], gate_ps[:, 0:DE], ACT.Silu).then_inc(silued, 1)
                    act.wait_ge(h_turned, b + 3)
                    act.activation(hxT[:, 0:4, :], turn_ps[0][:, :].rearrange("p (k t) -> p k t", k=4), ACT.Copy).then_inc(hT_act, 1)
                    act.wait_ge(a_turned, b + 1)
                    act.activation(auT[:, :, :], act_ps[:, 0:DE].rearrange("p (f t) -> p f t", f=CO), ACT.Copy).then_inc(aT_out, 1)
                    act.wait_ge(wo_used[CO - 1], b + 2)
                    act.wait_ge(stored, b * 16 + 16)
                    act.activation(y[:, 0:GC], y_ps[0][:, :], ACT.Copy).then_inc(y_act, 1)
                    act.wait_ge(y_act, b + 2)
                    act.wait_ge(y_dve, b + 2)
                    act.dma_start(y_dram[bass.ds(b * P, P), :], y[:, :]).then_inc(stored, 16)
                act.wait_ge(stored, nb * 16 + 16)
                act.sem_inc(passed, 1)

            @block.vector
            def _(dve):
                dve.sem_inc(y_dve, 1)
                dve.wait_ge(h_turned, 2)
                dve.tensor_copy(hxT[:, 4:8, :], turn_ps[1][:, :].rearrange("p (k t) -> p k t", k=4)).then_inc(hT_dve, 1)
                with dve.Fori(0, blocks(dve)) as b:
                    dve.wait_ge(silued, b + 1)
                    dve.tensor_tensor(au[:, :], up_ps[:, 0:DE], sg[:, :], ALU.mult).then_inc(multiplied, 1)
                    dve.wait_ge(h_turned, b + 3)
                    dve.tensor_copy(hxT[:, 4:8, :], turn_ps[1][:, :].rearrange("p (k t) -> p k t", k=4)).then_inc(hT_dve, 1)
                    dve.wait_ge(wo_used[CO - 1], b + 2)
                    dve.wait_ge(stored, b * 16 + 16)
                    dve.tensor_copy(y[:, GC:D], y_ps[1][:, :]).then_inc(y_dve, 1)


def moe_combine(m, layer, slot_i, wgt, y_dram):
    m.phase()
    nc = m.nc
    with ExitStack() as t:
        yg = m.sb(t, f"c{layer}_y", [P, 2 * T, D])
        got = [m.sem(f"c{layer}_got{j}") for j in range(2 * T)]
        added = m.psem(f"c{layer}_added")
        order = [c * T + i for i in range(T) for c in range(2)]
        with nc.Block() as block:
            @block.gpsimd
            def _(pool):
                for j in order:
                    pool.indirect_dma_start(out=yg[:, j, :], out_offset=None, in_=y_dram,
                                            in_offset=bass.IndirectOffsetOnAxis(ap=slot_i[:, j:j + 1], axis=0)).then_inc(got[j], 16)

            @block.vector
            def _(dve):
                for n, j in enumerate(order):
                    dve.wait_ge(got[j], 16)
                    if n:
                        dve.wait_ge(added, n)
                    dve.scalar_tensor_tensor(out=m.x[:, j % T, :], in0=yg[:, j, :], scalar=wgt[:, j:j + 1],
                                             in1=m.x[:, j % T, :], op0=ALU.mult, op1=ALU.add).then_inc(added, 1)


def moe(m, layer):
    nm = f"moe{layer}"
    h_dram = m.nc.dram_tensor(f"{nm}_h", [S, D], F32).ap()
    idx_dram = m.nc.dram_tensor(f"{nm}_idx", [SLOTS, 1], I32).ap()
    y_dram = m.y_dram
    with ExitStack() as c:
        slot_i = m.sb(c, f"{nm}_slot", [P, 2 * T], I32)
        wgt = m.sb(c, f"{nm}_wgt", [P, 2 * T])
        meta = m.sb(c, f"{nm}_meta", [1, MAXB + 2], I32)
        with ExitStack() as c2:
            hT = m.sb(c2, f"{nm}_hT", [P, KD, S])
            norm_transpose(m, nm, m.x, m.a["norm_ffn"][layer], T, None, None, plain=hT, h_dram=h_dram)
            moe_route(m, layer, hT, slot_i, wgt, meta, idx_dram)
        moe_experts(m, layer, meta, h_dram, idx_dram, y_dram)
        moe_combine(m, layer, slot_i, wgt, y_dram)


def build_trunk(nc, a, out, parts="all"):
    with ExitStack() as ctx:
        m = Core(nc, ctx, a)
        two = [(0, GC), (GC, 2 * GC)]
        four = [(n * GC, (n + 1) * GC) for n in range(4)]
        eight = [(n * GC, (n + 1) * GC) for n in range(8)]
        at = {}

        def add(name, w, cols):
            at[name] = len(m.groups)
            m.add_linear(w, cols)

        if parts in ("all", "hyb"):
            add("hyb", a["hyb_w_in"][0], [(O_QA, O_KC), (O_KS, O_GA), (O_KC, O_KS), (O_QB, O_VB), (O_VB, O_AL),
                                          (O_R, O_END), (O_GA, O_QB), (O_AL, O_R)])
            add("hyb_out", a["hyb_w_out"][0], two)
        for layer in range(DEPTH):
            if layer == 1 and parts in ("all", "sgu"):
                add("sgu", a["sg_w_in"][0], eight)
                add("sgu_out", a["sg_w_out"][0], two)
            if parts == "all" or parts == f"x{layer}":
                add(f"x{layer}", a["x_wkv"][layer], four)
                add(f"xq{layer}", a["x_wq"][layer], two)
                add(f"xo{layer}", a["x_wo"][layer], two)
        setup(m)
        if parts != "all":
            m.phase()
            z = m.sb(ctx, "ztest", [P, D]); zs = m.psem("ztest")
            with nc.Block() as block:
                @block.gpsimd
                def _(pool):
                    pool.memset(z[:, :], 0.0).then_inc(zs, 1)
                @block.sync
                def _(sp):
                    sp.wait_ge(zs, 1)
                    m.clear_outputs(sp, z[:, :])
        for layer in range(DEPTH):
            if layer == 0 and "hyb" in at:
                hybrid_layer(m, at["hyb"])
            elif layer == 1 and "sgu" in at:
                sgu_layer(m, layer, at["sgu"])
            if f"x{layer}" in at:
                cross_attention(m, layer, at[f"x{layer}"])
            if parts == "all" or parts == f"moe{layer}":
                moe(m, layer)
        store_x(m, out)


_INS = ["x", "mem", "positions", "norm_mix", "norm_xattn", "norm_mem", "norm_ffn", "hyb_w_in", "hyb_w_out",
        "nsa_qnorm", "nsa_knorm", "nsa_cmp_pe", "nsa_cmp_w1", "nsa_cmp_w2", "nsa_gate_b", "gla_wa2", "gla_ba",
        "gla_onorm", "sg_w_in", "sg_ln_g", "sg_ln_b", "sg_ws", "sg_bs", "sg_w_out", "x_wq", "x_wkv", "x_wo",
        "x_qnorm", "x_knorm", "router_w", "router_b", "moe_w_in", "moe_w_out"]


def kernel(**inputs):
    import concourse.bacc as _bacc
    from concourse.bass_utils import run_bass_kernel_spmd as _run

    nc = _bacc.Bacc("TRN2", target_bir_lowering=False, num_devices=1)
    arrays, args = {}, {}
    for name in _INS:
        arrays[f"in_{name}"] = np.ascontiguousarray(inputs[name])
        args[name] = nc.dram_tensor(f"in_{name}", arrays[f"in_{name}"].shape,
                                    mybir.dt.from_np(arrays[f"in_{name}"].dtype), kind="ExternalInput").ap()
    half = HD // 2
    arrays["rope_freq"] = (np.float32(10000.0) ** (-np.arange(half, dtype=np.float32) / half)).astype(np.float32)
    args["rope_freq"] = nc.dram_tensor("rope_freq", (half,), F32, kind="ExternalInput").ap()
    out = nc.dram_tensor("out_x", (1, S, D), F32, kind="ExternalOutput").ap()
    build_trunk(nc, args, out)
    r = _run(nc, [arrays], core_ids=[0])
    return r.results[0]["out_x"]
```

```python
from contextlib import ExitStack

import numpy as np
import concourse.bass as bass
from concourse import mybir

F32 = mybir.dt.float32
F32R = mybir.dt.float32r
I32 = mybir.dt.int32
ACT = mybir.ActivationFunctionType
ALU = mybir.AluOpType
AX = mybir.AxisListType

P = 128
D = 1024
S = 512
T = S // P
KD = D // P
DEPTH = 2
N_MEM = 256
MT = N_MEM // P
EPS = 1e-6
NEG = -1e30
GC = 512
KH = 4

HEADS, KVH, HD = 8, 2, 64
HPG = HEADS // KVH
CMP_LEN, CMP_STRIDE = 32, 16
N_CMP = (S - CMP_LEN) // CMP_STRIDE + 1
CP = 32
WINDOW = 256
WT = WINDOW // P

GH, GDK, GDV, GRANK, GTAU, GCH = 4, 64, 128, 16, 16.0, 64
SUB = 16
NSUB = GCH // SUB
NCH = S // GCH

SGW = 2 * D
SGG = 8
XH, XHD = 4, 256
NE, NG, EPG, DE = 16, 4, 4, 384
MAXB = (2 * S) // P + NE - 1
SLOTS = (MAXB + 1) * P

SIZES = (512, 128, 128, 128, 128, 128, 128, 24, 256, 256, 512, 16, 512)
OFF = [0]
for _s in SIZES:
    OFF.append(OFF[-1] + _s)
(O_QA, O_KC, O_VC, O_KS, O_VS, O_KW, O_VW, O_GA, O_QB, O_KB, O_VB, O_AL, O_R, O_END) = OFF


PHASE_SEMS = 48

class Chain:

    def __init__(self, engine, sem):
        self.engine, self.sem, self.n = engine, sem, 0

    def link(self, ins):
        self.n += 1
        ins.then_inc(self.sem, 1)
        self.engine.wait_ge(self.sem, self.n)


class Core:

    def __init__(self, nc, ctx, a):
        self.nc, self.ctx, self.a = nc, ctx, a
        self.turn, self.taken = 0, 0
        self.banks = [[self.sem(f"phase{b}_{i}") for i in range(PHASE_SEMS)] for b in range(2)]
        sb, sem = self.sb, self.sem
        self.x = sb(ctx, "x_res", [P, T, D])
        self.ident = sb(ctx, "ident", [P, P])
        self.stage = [sb(ctx, f"w_stage{h}", [P, KH, GC]) for h in range(2)]
        self.w_hi = [sb(ctx, f"w_hi{h}", [P, KH, GC], F32R) for h in range(2)]
        self.w_lo = [sb(ctx, f"w_lo{h}", [P, KH, GC], F32R) for h in range(2)]
        self.psum = [ctx.enter_context(nc.psum_tensor(f"bank{b}", [P, GC], F32)) for b in range(8)]
        self.landed = [sem(f"w_landed{h}") for h in range(2)]
        self.hi_done = [sem(f"w_hi_done{h}") for h in range(2)]
        self.lo_done = [sem(f"w_lo_done{h}") for h in range(2)]
        self.used = [sem(f"w_used{h}") for h in range(2)]
        self.y_dram = nc.dram_tensor("moe_y", [SLOTS, D], F32).ap()
        self.cleared = sem("y_cleared")
        self.groups = []
        self.asked = 0

    def sb(self, ctx, name, shape, dt=F32):
        return ctx.enter_context(self.nc.sbuf_tensor(name, shape, dt))

    def split_pair(self, ctx, name, k=KD, n=S):
        return (self.sb(ctx, f"{name}_hi", [P, k, n], F32R), self.sb(ctx, f"{name}_lo", [P, k, n], F32R))

    def clear_outputs(self, sp, zeros):
        for b in range(2 * S // P, SLOTS // P):
            sp.dma_start(self.y_dram[b * P:(b + 1) * P, :], zeros).then_inc(self.cleared, 16)
        sp.wait_ge(self.cleared, 16 * (SLOTS // P - 2 * S // P))

    def sem(self, name):
        return self.ctx.enter_context(self.nc.semaphore(name))

    def phase(self):
        self.turn += 1
        self.taken = 0
        if self.turn > 1:
            last = self.banks[self.turn % 2]
            self.nc.gpsimd.sem_clear(range(last[0].num, last[-1].num + 1))

    def psem(self, name):
        s = self.banks[(self.turn + 1) % 2][self.taken]
        self.taken += 1
        return s

    def add_linear(self, w, cols):
        for c0, c1 in cols:
            for k0 in range(0, w.shape[0], 2 * KH * P):
                self.groups.append(([w[k0 + h * KH * P:k0 + (h + 1) * KH * P, c0:c1]
                                     .rearrange("(k p) n -> p k n", p=P) for h in range(2)], c1 - c0))

    def load(self, sp, upto):
        while self.asked < min(upto, len(self.groups)):
            n = self.asked
            srcs, cols = self.groups[n]
            for h in range(2):
                if n:
                    sp.wait_ge(self.lo_done[h], n)
                sp.dma_start(self.stage[h][:, :, :cols], srcs[h]).then_inc(self.landed[h], 16)
            self.asked += 1

    def split_hi(self, act, n):
        cols = self.groups[n][1]
        for h in range(2):
            act.wait_ge(self.landed[h], 16 * (n + 1))
            if n:
                act.wait_ge(self.used[h], n)
            act.activation(self.w_hi[h][:, :, :cols], self.stage[h][:, :, :cols], ACT.Copy)\
               .then_inc(self.hi_done[h], 1)

    def split_lo(self, dve, n):
        cols = self.groups[n][1]
        for h in range(2):
            dve.wait_ge(self.hi_done[h], n + 1)
            dve.tensor_tensor(self.w_lo[h][:, :, :cols], self.stage[h][:, :, :cols],
                              self.w_hi[h][:, :, :cols], ALU.subtract).then_inc(self.lo_done[h], 1)

    def product(self, pe, n, feature_major, banks, hi, lo, tiles=T, first=True, last=True, k0=0):
        cols = self.groups[n][1]
        for h in range(2):
            pe.wait_ge(self.lo_done[h], n + 1)
            for b in range(cols // P if feature_major else tiles):
                for kk in range(KH):
                    k = k0 + KH * h + kk
                    for term, (x_part, w_part) in enumerate(((hi, self.w_hi[h]), (hi, self.w_lo[h]), (lo, self.w_hi[h]))):
                        start = first and h == 0 and kk == 0 and term == 0
                        stop = last and h == 1 and kk == KH - 1 and term == 2
                        if feature_major:
                            ins = pe.matmul(banks[b][:, :tiles * P], w_part[:, kk, b * P:(b + 1) * P],
                                            x_part[:, k, :tiles * P], start=start, stop=stop)
                        else:
                            ins = pe.matmul(banks[b][:, :cols], x_part[:, k, b * P:(b + 1) * P],
                                            w_part[:, kk, :cols], start=start, stop=stop)
            ins.then_inc(self.used[h], 1)

    def done(self, engine, n):
        engine.wait_ge(self.used[1], n + 1)


def setup(m):
    m.phase()
    nc, ctx = m.nc, m.ctx
    loaded = m.x_loaded = m.psem("x_loaded")
    made = m.psem("consts_made")
    m.causal = m.sb(ctx, "causal_neg", [P, P])
    m.beyond = m.sb(ctx, "beyond_neg", [P, P])
    with nc.Block() as block:
        @block.sync
        def _(sp):
            for t in range(T):
                sp.dma_start(m.x[:, t, :], m.a["x"][0, t * P:(t + 1) * P, :]).then_inc(loaded, 16)
            m.load(sp, 1)
            sp.wait_ge(loaded, 16 * T)

        @block.gpsimd
        def _(pool):
            pool.memset(m.ident[:, :], 0.0).then_inc(made, 1)
            pool.memset(m.causal[:, :], 0.0).then_inc(made, 1)
            pool.memset(m.beyond[:, :], 0.0).then_inc(made, 1)
            pool.wait_ge(made, 3)
            pool.affine_select(out=m.ident[:, :], in_=m.ident[:, :], compare_op=ALU.not_equal, fill=1.0,
                               base=0, pattern=[[-1, P]], channel_multiplier=1).then_inc(made, 1)
            pool.affine_select(out=m.causal[:, :], in_=m.causal[:, :], compare_op=ALU.is_ge, fill=NEG,
                               base=0, pattern=[[-1, P]], channel_multiplier=1).then_inc(made, 1)
            pool.affine_select(out=m.beyond[:, :], in_=m.beyond[:, :], compare_op=ALU.is_gt, fill=NEG,
                               base=0, pattern=[[1, P]], channel_multiplier=-1).then_inc(made, 1)
            pool.wait_ge(made, 6)


def norm_transpose(m, name, src, gain, tiles, hi, lo, plain=None, h_dram=None):
    m.phase()
    nc = m.nc
    with ExitStack() as c:
        xn = m.sb(c, f"{name}_xn", [P, tiles, D])
        g = m.sb(c, f"{name}_gain", [P, KD])
        junk = m.sb(c, f"{name}_sq", [P, D])
        ms = m.sb(c, f"{name}_ms", [P, tiles])
        root = m.sb(c, f"{name}_root", [P, tiles])
        rstd = m.sb(c, f"{name}_rstd", [P, tiles])
        gain_in, squared, mean, rooted, normed, turned, hi_out, lo_out, dve_c, act_c, stored = (
            m.psem(f"{name}_{s}") for s in ("gain_in", "squared", "mean", "rooted", "normed", "turned",
                                           "hi_out", "lo_out", "dve", "act", "stored"))
        gb = m.sb(c, f"{name}_gain_row", [P, D]) if plain is not None else None
        with nc.Block() as block:
            @block.sync
            def _(sp):
                if plain is None:
                    with nc.allow_non_contiguous_dma(reason="one gain per partition"):
                        sp.dma_start(g[:, :], gain.rearrange("(k p) -> p k", p=P)).then_inc(gain_in, 16)
                else:
                    sp.dma_start(gb[:, :], gain.partition_broadcast(P)).then_inc(gain_in, 16)
                    for t in range(tiles):
                        sp.wait_ge(normed, t + 1)
                        sp.dma_start(h_dram[t * P:(t + 1) * P, :], xn[:, t, :]).then_inc(stored, 16)
                    sp.wait_ge(stored, 16 * tiles)

            @block.scalar
            def _(act):
                link = Chain(act, act_c).link
                for t in range(tiles):
                    if t:
                        act.wait_ge(squared, t)
                    act.activation(junk[:, :], src[:, t, :], ACT.Square, accum_out=ms[:, t:t + 1])\
                       .then_inc(squared, 1)
                act.wait_ge(mean, 1)
                act.activation(root[:, :], ms[:, :], ACT.Sqrt).then_inc(rooted, 1)
                if plain is None:
                    act.wait_ge(gain_in, 16)
                for k in range(KD):
                    act.wait_ge(turned, k + 1)
                    if plain is None:
                        act.activation(hi[:, k, :tiles * P], m.psum[k][:, :tiles * P], ACT.Copy,
                                       scale=g[:, k:k + 1]).then_inc(hi_out, 1)
                    elif k % 2 == 0:
                        act.activation(plain[:, k, :tiles * P], m.psum[k][:, :tiles * P], ACT.Copy).then_inc(hi_out, 1)

            @block.vector
            def _(dve):
                link = Chain(dve, dve_c).link
                dve.wait_ge(squared, tiles)
                dve.tensor_scalar(ms[:, :], ms[:, :], 1.0 / D, EPS, ALU.mult, ALU.add).then_inc(mean, 1)
                dve.wait_ge(rooted, 1)
                link(dve.reciprocal(rstd[:, :], root[:, :]))
                if plain is not None:
                    dve.wait_ge(gain_in, 16)
                for t in range(tiles):
                    if plain is None:
                        dve.tensor_scalar(xn[:, t, :], src[:, t, :], rstd[:, t:t + 1], None, ALU.mult).then_inc(normed, 1)
                    else:
                        dve.scalar_tensor_tensor(out=xn[:, t, :], in0=src[:, t, :], scalar=rstd[:, t:t + 1],
                                                 in1=gb[:, :], op0=ALU.mult, op1=ALU.mult).then_inc(normed, 1)
                if plain is None:
                    for k in range(KD):
                        dve.wait_ge(hi_out, k + 1)
                        dve.scalar_tensor_tensor(out=lo[:, k, :tiles * P], in0=m.psum[k][:, :tiles * P],
                                                 scalar=g[:, k:k + 1], in1=hi[:, k, :tiles * P],
                                                 op0=ALU.mult, op1=ALU.subtract).then_inc(lo_out, 1)
                else:
                    for k in range(1, KD, 2):
                        dve.wait_ge(turned, k + 1)
                        dve.tensor_copy(plain[:, k, :tiles * P], m.psum[k][:, :tiles * P]).then_inc(lo_out, 1)

            @block.tensor
            def _(pe):
                pe.wait_ge(normed, tiles)
                for k in range(KD):
                    for t in range(tiles):
                        ins = pe.transpose(m.psum[k][:, t * P:(t + 1) * P], xn[:, t, k * P:(k + 1) * P], m.ident[:, :])
                    ins.then_inc(turned, 1)


def store_x(m, out):
    m.phase()
    stored = m.psem("x_stored")
    with m.nc.Block() as block:
        @block.sync
        def _(sp):
            for t in range(T):
                sp.dma_start(out[0, t * P:(t + 1) * P, :], m.x[:, t, :]).then_inc(stored, 16)
            sp.wait_ge(stored, 16 * T)


def projection_outputs(m, c):
    qk = m.sb(c, "qk", [P, T, HEADS + 2 * KVH, HD])
    v_sw = m.sb(c, "v_sw", [P, T, 2, KVH * HD])
    kvc = m.sb(c, "kvc", [P, 2, S])
    gqk = m.sb(c, "gla_qk", [P, 4, S])
    gv = m.sb(c, "gla_v", [P, T, GH * GDV])
    gr = m.sb(c, "gla_r", [P, T, GH * GDV])
    ga = m.sb(c, "gates", [P, T, 3 * HEADS])
    al = m.sb(c, "a_low", [P, T, GRANK])
    return qk, v_sw, kvc, gqk, gv, gr, ga, al


def hybrid_projection(m, outputs, first, hi, lo):
    m.phase()
    nc = m.nc
    qk, v_sw, kvc, gqk, gv, gr, ga, al = outputs
    out_act, out_dve = m.psem("proj_out_act"), m.psem("proj_out_dve")
    kinds = [(False, 4), (False, 4), (True, 2), (True, 4), (False, 4), (False, 4), (False, 4), (False, 4)]

    def bank(j, b):
        return m.psum[4 * (j % 2) + b]

    with nc.Block() as block:
        @block.sync
        def _(sp):
            m.load(sp, first + len(kinds) + 1)

        @block.tensor
        def _(pe):
            for j, (fm, _) in enumerate(kinds):
                if j >= 2:
                    pe.wait_ge(out_act, sum(k[1] // 2 for k in kinds[:j - 1]))
                    pe.wait_ge(out_dve, sum(k[1] // 2 for k in kinds[:j - 1]))
                m.product(pe, first + j, fm, [bank(j, b) for b in range(4)], hi, lo)

        def read_out(engine, copy, j, b):
            ps = bank(j, b)
            if j == 0:
                copy(qk[:, b, 0:HEADS, :].rearrange("p (i g) d -> p g i d", g=KVH),
                     ps[:, :].rearrange("p (g i d) -> p g i d", g=KVH, d=HD)).then_inc(engine, 1)
            elif j == 1:
                parts = ps[:, :].rearrange("p (w kv c) -> p w kv c", w=2, kv=2)
                copy(qk[:, b, HEADS:, :].rearrange("p (w g) d -> p w (g d)", w=2), parts[:, :, 0, :])
                copy(v_sw[:, b, :, :], parts[:, :, 1, :]).then_inc(engine, 1)
            elif j == 2:
                copy(kvc[:, b, :], ps[:, :]).then_inc(engine, 1)
            elif j == 3:
                copy(gqk[:, b, :], ps[:, :], GDK ** -0.5 if b < 2 else 1.0).then_inc(engine, 1)
            elif j == 4:
                copy(gv[:, b, :], ps[:, :]).then_inc(engine, 1)
            elif j == 5:
                copy(gr[:, b, :], ps[:, :]).then_inc(engine, 1)
            elif j == 6:
                copy(ga[:, b, :], ps[:, 0:3 * HEADS]).then_inc(engine, 1)
            else:
                copy(al[:, b, :], ps[:, 0:GRANK]).then_inc(engine, 1)

        @block.scalar
        def _(act):
            def copy(out, ps, scale=1.0):
                return act.activation(out, ps, ACT.Copy, scale=scale)
            m.split_hi(act, first)
            for j, (_, n_banks) in enumerate(kinds):
                if j + 1 < len(kinds):
                    m.split_hi(act, first + j + 1)
                m.done(act, first + j)
                for b in range(0, n_banks, 2):
                    read_out(out_act, copy, j, b)

        @block.vector
        def _(dve):
            def copy(out, ps, scale=1.0):
                return dve.tensor_scalar(out, ps, scale, None, ALU.mult)
            m.split_lo(dve, first)
            for j, (_, n_banks) in enumerate(kinds):
                if j + 1 < len(kinds):
                    m.split_lo(dve, first + j + 1)
                m.done(dve, first + j)
                for b in range(1, n_banks, 2):
                    read_out(out_dve, copy, j, b)


def nsa_prepare(m, c, qk, kvc):
    m.phase()
    nc, a = m.nc, m.a
    NP6 = (HEADS + 2 * KVH) // 2
    QH = HEADS + 2 * KVH
    HF = HD // 2
    MAGIC = 1.5 * 2 ** 23
    TWO_PI = 2 * np.pi
    C1 = 6.28125
    C2 = float(np.float32(np.round((TWO_PI - C1) * 2 ** 22) / 2 ** 22))
    C3 = float(TWO_PI - C1 - C2)

    qkT = m.sb(c, "qkT", [P, NP6, S])
    kcT = m.sb(c, "kcT", [P, CP])
    vbd = m.sb(c, "vc_diag", [P, KVH, HPG, HD])
    with ExitStack() as t:
        pos_i = m.sb(t, "pos_i", [P, T + 1], I32)
        pos = m.sb(t, "pos", [P, T + 1])
        freq = m.sb(t, "freq", [P, HF])
        ang = m.sb(t, "ang", [P, T + 1, HF])
        turns = m.sb(t, "turns", [P, T + 1, HF])
        sin = m.sb(t, "sin", [P, T + 1, HF])
        cos = m.sb(t, "cos", [P, T + 1, HF])
        gains = m.sb(t, "head_gains", [P, QH, HD])
        kc_gain = m.sb(t, "kc_gain", [P, HD])
        sq = m.sb(t, "head_sq", [P, QH * HD])
        rot = m.sb(t, "head_rot", [P, QH, HD])
        tmp = m.sb(t, "head_tmp", [P, 2, QH, HF])
        ss = m.sb(t, "head_ss", [P, T * QH])
        root = m.sb(t, "head_root", [P, T * QH])
        w1 = m.sb(t, "cmp_w1", [P, 2, CMP_LEN, P])
        w2 = m.sb(t, "cmp_w2", [P, 2, P])
        pe_t = m.sb(t, "cmp_pe", [P, 2, CMP_LEN])
        blk = m.sb(t, "cmp_blocks", [P, CMP_LEN, CP])
        act1 = m.sb(t, "cmp_act", [P, 2, CP])
        kc = m.sb(t, "kc", [CP, KVH, HD])
        kc_sq = m.sb(t, "kc_sq", [CP, KVH, HD])
        kc_n = m.sb(t, "kc_n", [CP, KVH, HD])
        kc_r = m.sb(t, "kc_r", [CP, KVH, HD])
        kc_ss = m.sb(t, "kc_ss", [CP, KVH])
        kc_tmp = m.sb(t, "kc_tmp", [CP, 2, KVH, HF])
        vc = m.sb(t, "vc", [CP, KVH * HD])
        (small_in, w_in, zeroed, dve_c, act_c, angles, sines, sqr, means, roots, heads_done, turned, kept,
         blocks, hidden, gelued, out2, kc_mean, kc_root, kc_done, kc_turned, v_here, v_spread) = (
            m.psem(f"prep_{s}") for s in (
                "small_in", "w_in", "zeroed", "dve", "act", "angles", "sines", "sqr", "means", "roots",
                "heads_done", "turned", "kept", "blocks", "hidden", "gelued", "out2", "kc_mean",
                "kc_root", "kc_done", "kc_turned", "v_here", "v_spread"))

        def rotate(dve, link, out, xin, cs, sn, tmp2, n):
            x1, x2 = xin[:, :, 0:HF], xin[:, :, HF:HD]
            p = xin.shape[0]
            cb = cs.unsqueeze(1).to_broadcast([p, n, HF])
            sb = sn.unsqueeze(1).to_broadcast([p, n, HF])
            dve.tensor_tensor(tmp2[:, 0], x2, sb, ALU.mult)
            dve.tensor_tensor(tmp2[:, 1], x1, sb, ALU.mult)
            dve.tensor_tensor(out[:, :, 0:HF], x1, cb, ALU.mult)
            link(dve.tensor_tensor(out[:, :, HF:HD], x2, cb, ALU.mult))
            dve.tensor_tensor(out[:, :, 0:HF], out[:, :, 0:HF], tmp2[:, 0], ALU.subtract)
            return dve.tensor_tensor(out[:, :, HF:HD], out[:, :, HF:HD], tmp2[:, 1], ALU.add)

        with nc.Block() as block:
            @block.sync
            def _(sp):
                with nc.allow_non_contiguous_dma(reason="small tables, one element per partition"):
                    sp.dma_start(pos_i[:, 0:T], a["positions"][0].rearrange("(t p) -> p t", p=P)).then_inc(small_in, 16)
                    sp.wait_ge(angles, 1)
                    sp.dma_start(pos_i[0:N_CMP, T:T + 1],
                                 a["positions"][0:1, CMP_LEN - 1:CMP_LEN - 1 + CMP_STRIDE * (N_CMP - 1) + 1:CMP_STRIDE]
                                 .rearrange("a c -> c a")).then_inc(small_in, 16)
                    sp.dma_start(freq[:, :], a["rope_freq"].partition_broadcast(P)).then_inc(small_in, 16)
                    for g0, n, src in ((0, HEADS, a["nsa_qnorm"][0]), (HEADS, KVH, a["nsa_knorm"][0, 1]),
                                       (HEADS + KVH, KVH, a["nsa_knorm"][0, 2])):
                        for i in range(n):
                            sp.dma_start(gains[:, g0 + i, :], src.partition_broadcast(P)).then_inc(small_in, 16)
                    sp.dma_start(kc_gain[:, :], a["nsa_knorm"][0, 0].partition_broadcast(P)).then_inc(small_in, 16)
                    sp.wait_ge(zeroed, 4)
                    for kv in range(2):
                        for g in range(KVH):
                            half = slice(g * HD, (g + 1) * HD)
                            sp.dma_start(w1[half, kv, :, half], a["nsa_cmp_w1"][0, kv].rearrange("(l d) e -> d l e", d=HD)).then_inc(w_in, 16)
                            sp.dma_start(w2[half, kv, half], a["nsa_cmp_w2"][0, kv]).then_inc(w_in, 16)
                            sp.dma_start(pe_t[half, kv, :], a["nsa_cmp_pe"][0, kv].rearrange("l d -> d l")).then_inc(w_in, 16)
                    sp.wait_ge(v_here, 1)
                    for g in range(KVH):
                        for i in range(HPG):
                            sp.dma_start(vbd[i * CP:i * CP + N_CMP, g, i, :], vc[0:N_CMP, g * HD:(g + 1) * HD]).then_inc(v_spread, 16)
                    sp.wait_ge(v_spread, 16 * KVH * HPG)

            @block.gpsimd
            def _(pool):
                pool.memset(w1[:, :, :, :], 0.0).then_inc(zeroed, 1)
                pool.memset(w2[:, :, :], 0.0).then_inc(zeroed, 1)
                pool.memset(vbd[:, :, :, :], 0.0).then_inc(zeroed, 1)
                pool.memset(kcT[:, :], 0.0).then_inc(zeroed, 1)

            @block.vector
            def _(dve):
                link = Chain(dve, dve_c).link
                dve.memset(pos_i[:, T:T + 1], 0).then_inc(angles, 1)
                dve.wait_ge(small_in, 16 * (3 + QH + 1))
                link(dve.tensor_copy(pos[:, :], pos_i[:, :]))
                for i in range(T + 1):
                    ins = dve.tensor_scalar(ang[:, i, :], freq[:, :], pos[:, i:i + 1], None, ALU.mult)
                link(ins)
                link(dve.tensor_scalar(turns[:, :, :], ang[:, :, :], 1 / TWO_PI, MAGIC, ALU.mult, ALU.add))
                link(dve.tensor_scalar(turns[:, :, :], turns[:, :, :], MAGIC, None, ALU.subtract))
                for part in (C1, C2, C3):
                    link(dve.scalar_tensor_tensor(out=ang[:, :, :], in0=turns[:, :, :], scalar=-part,
                                                  in1=ang[:, :, :], op0=ALU.mult, op1=ALU.add))
                dve.tensor_scalar(ang[:, :, :], ang[:, :, :], 3.1415925, -3.1415925, ALU.min, ALU.max).then_inc(angles, 1)
                for i in range(T):
                    link(dve.tensor_tensor(sq[:, :], qk[:, i].rearrange("p h d -> p (h d)"),
                                           qk[:, i].rearrange("p h d -> p (h d)"), ALU.mult))
                    link(dve.tensor_reduce(ss[:, i * QH:(i + 1) * QH], sq[:, :].rearrange("p (h d) -> p h d", d=HD), AX.X, ALU.add))
                dve.tensor_scalar(ss[:, :], ss[:, :], 1.0 / HD, EPS, ALU.mult, ALU.add).then_inc(means, 1)
                dve.wait_ge(w_in, 16 * 12)
                for kv in range(2):
                    if kv:
                        dve.wait_ge(hidden, 1)
                    for lh in range(2):
                        src = kvc[:, kv, lh * 16:lh * 16 + 16 * N_CMP].rearrange("p (c l) -> p l c", l=16)
                        dve.tensor_tensor(blk[:, lh * 16:lh * 16 + 16, 0:N_CMP], src,
                                          pe_t[:, kv, lh * 16:lh * 16 + 16].unsqueeze(2).to_broadcast([P, 16, N_CMP]),
                                          ALU.add).then_inc(blocks, 1)
                dve.wait_ge(sines, 2)
                link(dve.tensor_tensor(cos[:, :, :], cos[:, :, :], cos[:, :, :], ALU.mult))
                link(dve.tensor_scalar(cos[:, :, :], cos[:, :, :], -2.0, 1.0, ALU.mult, ALU.add))
                dve.wait_ge(roots, 1)
                link(dve.reciprocal(ss[:, :], root[:, :]))
                link(dve.tensor_scalar(gains[:, 0:HEADS, :], gains[:, 0:HEADS, :], HD ** -0.5, None, ALU.mult))
                for i in range(T):
                    r = ss[:, i * QH:(i + 1) * QH].unsqueeze(2).to_broadcast([P, QH, HD])
                    link(dve.tensor_tensor(rot[:, :, :], qk[:, i], r, ALU.mult))
                    link(dve.tensor_tensor(rot[:, :, :], rot[:, :, :], gains[:, :, :], ALU.mult))
                    rotate(dve, link, qk[:, i], rot[:, :, :], cos[:, i], sin[:, i], tmp, QH).then_inc(heads_done, 1)
                    dve.wait_ge(heads_done, i + 1)
                dve.wait_ge(out2, 1)
                link(dve.tensor_copy(kc[0:N_CMP], m.psum[6][0:N_CMP, 0:P].rearrange("p (g d) -> p g d", g=KVH)))
                link(dve.tensor_tensor(kc_sq[0:N_CMP], kc[0:N_CMP], kc[0:N_CMP], ALU.mult))
                link(dve.tensor_reduce(kc_ss[0:N_CMP], kc_sq[0:N_CMP], AX.X, ALU.add))
                dve.tensor_scalar(kc_ss[0:N_CMP], kc_ss[0:N_CMP], 1.0 / HD, EPS, ALU.mult, ALU.add).then_inc(kc_mean, 1)
                dve.wait_ge(kc_root, 1)
                link(dve.reciprocal(kc_ss[0:N_CMP], kc_sq[0:N_CMP, 0, 0:KVH]))
                link(dve.tensor_tensor(kc_n[0:N_CMP], kc[0:N_CMP], kc_ss[0:N_CMP].unsqueeze(2).to_broadcast([N_CMP, KVH, HD]), ALU.mult))
                link(dve.tensor_tensor(kc_n[0:N_CMP], kc_n[0:N_CMP], kc_gain[0:N_CMP].unsqueeze(1).to_broadcast([N_CMP, KVH, HD]), ALU.mult))
                rotate(dve, link, kc_r[0:N_CMP], kc_n[0:N_CMP], cos[0:N_CMP, T], sin[0:N_CMP, T], kc_tmp[0:N_CMP], KVH).then_inc(kc_done, 1)
                dve.wait_ge(zeroed, 4)
                dve.wait_ge(kc_turned, 1)
                dve.tensor_copy(kcT[:, 0:N_CMP], m.psum[7][:, 0:N_CMP])

            @block.scalar
            def _(act):
                act.wait_ge(angles, 2)
                act.activation(sin[:, :, :], ang[:, :, :], ACT.Sin).then_inc(sines, 1)
                act.activation(cos[:, :, :], ang[:, :, :], ACT.Sin, scale=0.5).then_inc(sines, 1)
                act.wait_ge(means, 1)
                act.activation(root[:, :], ss[:, :], ACT.Sqrt).then_inc(roots, 1)
                for kv in range(2):
                    act.wait_ge(hidden, kv + 1)
                    act.activation(act1[:, kv, 0:N_CMP], m.psum[kv][:, 0:N_CMP], ACT.Gelu_apprx_tanh).then_inc(gelued, 1)
                act.wait_ge(out2, 2)
                act.activation(vc[0:N_CMP], m.psum[7][0:N_CMP, 0:P], ACT.Copy).then_inc(v_here, 1)
                act.wait_ge(kc_mean, 1)
                act.activation(kc_sq[0:N_CMP, 0, 0:KVH], kc_ss[0:N_CMP], ACT.Sqrt).then_inc(kc_root, 1)
                for i in range(T):
                    act.wait_ge(turned, i + 1)
                    act.activation(qkT[:, 0:4, i * P:(i + 1) * P],
                                   m.psum[2 + 2 * (i % 2)][:, :].rearrange("p (k t) -> p k t", k=4), ACT.Copy)
                    act.activation(qkT[:, 4:6, i * P:(i + 1) * P],
                                   m.psum[3 + 2 * (i % 2)][:, 0:2 * P].rearrange("p (k t) -> p k t", k=2), ACT.Copy).then_inc(kept, 1)

            @block.tensor
            def _(pe):
                for kv in range(2):
                    pe.wait_ge(blocks, 2 * kv + 2)
                    for l in range(CMP_LEN):
                        ins = pe.matmul(m.psum[kv][:, 0:N_CMP], w1[:, kv, l, :], blk[:, l, 0:N_CMP],
                                        start=l == 0, stop=l == CMP_LEN - 1)
                    ins.then_inc(hidden, 1)
                for kv in range(2):
                    pe.wait_ge(gelued, kv + 1)
                    pe.matmul(m.psum[6 + kv][0:N_CMP, 0:P], act1[:, kv, 0:N_CMP], w2[:, kv, :],
                              start=True, stop=True).then_inc(out2, 1)
                for i in range(T):
                    pe.wait_ge(heads_done, i + 1)
                    if i >= 2:
                        pe.wait_ge(kept, i - 1)
                    for pair in range(NP6):
                        ins = pe.transpose(m.psum[2 + 2 * (i % 2) + pair // 4][:, (pair % 4) * P:(pair % 4 + 1) * P],
                                           qk[:, i, 2 * pair:2 * pair + 2, :].rearrange("p h d -> p (h d)"), m.ident[:, :])
                    ins.then_inc(turned, 1)
                pe.wait_ge(kc_done, 1)
                pe.wait_ge(v_here, 1)
                pe.transpose(m.psum[7][:, 0:N_CMP], kc_r[0:N_CMP].rearrange("p g d -> p (g d)"),
                             m.ident[0:N_CMP, 0:N_CMP]).then_inc(kc_turned, 1)
    return qkT, kcT, vbd


def compressed_branch(m, qkT, kcT, vbd, ga, mix, gate):
    m.phase()
    nc, a = m.nc, m.a
    with ExitStack() as t:
        cmask = m.sb(t, "cmp_neg", [P, T, CP])
        cone = m.sb(t, "cmp_one", [P, T, CP])
        gate_b = m.sb(t, "gate_b", [P, 3 * HEADS])
        cs = m.sb(t, "cmp_s", [P, KVH, T, HPG, CP])
        cp = m.sb(t, "cmp_p", [P, KVH, T, HPG, CP])
        cpT = m.sb(t, "cmp_pT", [P, KVH, T, P])
        cmax = m.sb(t, "cmp_max", [P, KVH, T, HPG])
        csum = m.sb(t, "cmp_sum", [P, KVH, T, HPG])
        (gb_in, masks, gated, g_lin, dve_c, subbed, exped, normed, turned, kept, out_ps) = (
            m.psem(f"cmp_{s}") for s in ("gb_in", "masks", "gated", "g_lin", "dve", "subbed",
                                         "exped", "normed", "turned", "kept", "out_ps"))
        scored = [m.psem(f"cmp_scored{g}") for g in range(KVH)]
        with nc.Block() as block:
            @block.sync
            def _(sp):
                sp.dma_start(gate_b[:, :], a["nsa_gate_b"][0].partition_broadcast(P)).then_inc(gb_in, 16)

            @block.gpsimd
            def _(pool):
                pool.memset(cmask[:, :, :], 0.0).then_inc(masks, 1)
                pool.memset(cone[:, :, :], 1.0).then_inc(masks, 1)
                pool.wait_ge(masks, 2)
                for tile_, fill in ((cmask, NEG), (cone, 0.0)):
                    pool.affine_select(out=tile_[:, :, :], in_=tile_[:, :, :], compare_op=ALU.is_ge, fill=fill,
                                       base=-(CMP_LEN - 1), pattern=[[P, T], [-CMP_STRIDE, CP]],
                                       channel_multiplier=1).then_inc(masks, 1)

            @block.tensor
            def _(pe):
                for i in range(T):
                    for h in range(HPG):
                        for g in range(KVH):
                            c0 = (i * HPG + h) * CP
                            ins = pe.matmul(m.psum[4 + g][:, c0:c0 + CP], qkT[g * HD:(g + 1) * HD, h, i * P:(i + 1) * P],
                                            kcT[g * HD:(g + 1) * HD, :], start=True, stop=True)
                            if i == T - 1 and h == HPG - 1:
                                ins.then_inc(scored[g], 1)
                pe.wait_ge(normed, 1)
                for g in range(KVH):
                    for i in range(T):
                        ins = pe.transpose(m.psum[6 + g][:, i * P:(i + 1) * P],
                                           cp[:, g, i].rearrange("p h c -> p (h c)"), m.ident[:, :])
                    ins.then_inc(turned, 1)
                pe.wait_ge(kept, KVH)
                for i in range(T):
                    for g in range(KVH):
                        ins = pe.matmul(m.psum[i][:, g * HPG * HD:(g + 1) * HPG * HD], cpT[:, g, i, :],
                                        vbd[:, g].rearrange("p h d -> p (h d)"), start=True, stop=True)
                    ins.then_inc(out_ps, 1)

            @block.scalar
            def _(act):
                act.wait_ge(subbed, 1)
                act.activation(cp[:, :, :, :, :], cs[:, :, :, :, :], ACT.Exp).then_inc(exped, 1)
                act.wait_ge(g_lin, 1)
                act.activation(gate[:, :, :, :].rearrange("p t h b -> p (t h b)"),
                               ga[:, :, :].rearrange("p t c -> p (t c)"), ACT.Sigmoid).then_inc(gated, 1)
                for g in range(KVH):
                    act.wait_ge(turned, g + 1)
                    act.activation(cpT[:, g], m.psum[6 + g][:, :].rearrange("p (i t) -> p i t", i=T), ACT.Copy).then_inc(kept, 1)

            @block.vector
            def _(dve):
                link = Chain(dve, dve_c).link
                dve.wait_ge(gb_in, 16)
                dve.tensor_tensor(ga[:, :, :], ga[:, :, :], gate_b[:, :].unsqueeze(1).to_broadcast([P, T, 3 * HEADS]),
                                  ALU.add).then_inc(g_lin, 1)
                dve.wait_ge(masks, 4)
                for g in range(KVH):
                    dve.wait_ge(scored[g], 1)
                    for i in range(T):
                        ins = dve.tensor_tensor(cs[:, g, i], m.psum[4 + g][:, i * P:(i + 1) * P].rearrange("p (h c) -> p h c", c=CP),
                                                cmask[:, i].unsqueeze(1).to_broadcast([P, HPG, CP]), ALU.add)
                link(ins)
                link(dve.tensor_reduce(cmax[:, :, :, :], cs[:, :, :, :, :], AX.X, ALU.max))
                for g in range(KVH):
                    ins = dve.tensor_tensor(cs[:, g], cs[:, g], cmax[:, g].unsqueeze(3).to_broadcast([P, T, HPG, CP]),
                                            ALU.subtract)
                ins.then_inc(subbed, 1)
                dve.wait_ge(exped, 1)
                for g in range(KVH):
                    for i in range(T):
                        ins = dve.tensor_tensor(cp[:, g, i], cp[:, g, i], cone[:, i].unsqueeze(1).to_broadcast([P, HPG, CP]), ALU.mult)
                ins.then_inc(normed, 1)
                dve.wait_ge(normed, 1)
                link(dve.tensor_reduce(csum[:, :, :, :], cp[:, :, :, :, :], AX.X, ALU.add))
                link(dve.tensor_scalar(csum[:, :, :, :], csum[:, :, :, :], 1e-30, None, ALU.max))
                link(dve.reciprocal(csum[:, :, :, :], csum[:, :, :, :]))
                dve.wait_ge(gated, 1)
                for g in range(KVH):
                    ins = dve.tensor_tensor(csum[:, g], csum[:, g], gate[:, :, g * HPG:(g + 1) * HPG, 0], ALU.mult)
                link(ins)
                for i in range(T):
                    dve.wait_ge(out_ps, i + 1)
                    for g in range(KVH):
                        cols = slice(g * HPG * HD, (g + 1) * HPG * HD)
                        dve.tensor_tensor(mix[:, i, cols].rearrange("p (h d) -> p h d", d=HD),
                                          m.psum[i][:, cols].rearrange("p (h d) -> p h d", d=HD),
                                          csum[:, g, i].unsqueeze(2).to_broadcast([P, HPG, HD]), ALU.mult)


def nsa_attention(m, qkT, kcT, vbd, v_sw, ga, mix):
    nc = m.nc
    units = [(i, br, h) for i in range(T) for br in range(2) for h in range(HPG)]
    NU = len(units)

    def keys(u):
        i, br, h = units[u]
        return list(range(0 if br == 0 else max(0, i - WT), i + 1))

    with ExitStack() as t:
        gate = m.sb(t, "gate", [P, T, HEADS, 3])
        compressed_branch(m, qkT, kcT, vbd, ga, mix, gate)
        m.phase()
        prob = m.sb(t, "prob", [P, 2, 2, S])
        probT = m.sb(t, "probT", [P, 2, S])
        nmax = m.sb(t, "nmax", [P, 2, 2])
        sums = m.sb(t, "sums", [P, 2, KVH, HPG])
        coef = m.sb(t, "coef", [P, HEADS])
        part = m.sb(t, "part", [P, 2, HEADS, HD])
        zeros = m.sb(t, "zeros", [P, D])
        (zeroed, dve_c, maxed, exped, turned, kept_act, kept_dve, summed, scaled, combined) = (
            m.psem(f"attn_{s}") for s in ("zeroed", "dve", "maxed", "exped", "turned", "kept_act",
                                          "kept_dve", "summed", "scaled", "combined"))
        scored = [m.psem(f"attn_scored{g}") for g in range(KVH)]
        with nc.Block() as block:
            @block.sync
            def _(sp):
                sp.wait_ge(zeroed, 1)
                m.clear_outputs(sp, zeros[:, :])

            @block.tensor
            def _(pe):
                def score(u):
                    i, br, h = units[u]
                    kt = keys(u)
                    for g in range(KVH):
                        half = slice(g * HD, (g + 1) * HD)
                        ins = pe.matmul(m.psum[2 * (u % 2) + g][:, 0:len(kt) * P], qkT[half, h, i * P:(i + 1) * P],
                                        qkT[half, 4 + br, kt[0] * P:(kt[-1] + 1) * P], start=True, stop=True)
                        ins.then_inc(scored[g], 1)

                score(0)
                score(1)
                for u, (i, br, h) in enumerate(units):
                    kt = keys(u)
                    for e in range(2):
                        pe.wait_ge(exped, 2 * u + e + 1)
                        for j in range(len(kt)):
                            ins = pe.transpose(m.psum[4 + e][:, j * P:(j + 1) * P],
                                               prob[:, u % 2, e, j * P:(j + 1) * P], m.ident[:, :])
                        ins.then_inc(turned, 1)
                    if u + 2 < NU:
                        score(u + 2)
                    n = u // HPG
                    if u % HPG == 0 and n >= 2:
                        pe.wait_ge(scaled, n - 1)
                    for e, kept in enumerate((kept_act, kept_dve)):
                        pe.wait_ge(kept, u + 1)
                        c0 = (e * HPG + h) * HD
                        for j, k in enumerate(kt):
                            ins = pe.matmul(m.psum[6 + n % 2][:, c0:c0 + HD], probT[:, e, j * P:(j + 1) * P],
                                            v_sw[:, k, br, e * HD:(e + 1) * HD], start=j == 0, stop=j == len(kt) - 1)
                    if u % HPG == HPG - 1:
                        ins.then_inc(summed, 1)

            @block.scalar
            def _(act):
                def exp(u):
                    i, br, h = units[u]
                    w = len(keys(u)) * P
                    act.wait_ge(maxed, u + 1)
                    if u >= 2:
                        act.wait_ge(turned, 2 * (u - 1))
                    if u % HPG == 0 and u >= 2 * HPG:
                        act.wait_ge(scaled, u // HPG - 1)
                    for e in range(2):
                        act.activation(prob[:, u % 2, e, 0:w], m.psum[2 * (u % 2) + e][:, 0:w], ACT.Exp,
                                       bias=nmax[:, u % 2, e:e + 1],
                                       accum_out=sums[:, br, e, h:h + 1]).then_inc(exped, 1)

                exp(0)
                for u in range(NU):
                    if u + 1 < NU:
                        exp(u + 1)
                    w = len(keys(u)) * P
                    act.wait_ge(turned, 2 * u + 1)
                    act.activation(probT[:, 0, 0:w], m.psum[4][:, 0:w], ACT.Copy).then_inc(kept_act, 1)

            @block.vector
            def _(dve):
                link = Chain(dve, dve_c).link

                def maximum(u):
                    i, br, h = units[u]
                    w = len(keys(u)) * P
                    for e in range(2):
                        dve.wait_ge(scored[e], u + 1)
                        s = m.psum[2 * (u % 2) + e]
                        ins = dve.tensor_tensor(s[:, w - P:w], s[:, w - P:w], m.causal[:, :], ALU.add)
                        if br and i >= WT:
                            ins = dve.tensor_tensor(s[:, 0:P], s[:, 0:P], m.beyond[:, :], ALU.add)
                    link(ins)
                    for e in range(2):
                        ins = dve.tensor_reduce(nmax[:, u % 2, e:e + 1], m.psum[2 * (u % 2) + e][:, 0:w], AX.X, ALU.max, negate=True)
                    ins.then_inc(maxed, 1)

                def scale(n):
                    i, br, h = units[n * HPG]
                    dve.wait_ge(exped, 2 * HPG * (n + 1))
                    link(dve.reciprocal(coef[:, :], sums[:, br].rearrange("p g h -> p (g h)")))
                    link(dve.tensor_tensor(coef[:, :], coef[:, :], gate[:, i, :, 1 + br], ALU.mult))
                    dve.wait_ge(summed, n + 1)
                    if n >= 2:
                        dve.wait_ge(combined, n - 1)
                    dve.tensor_tensor(part[:, n % 2], m.psum[6 + n % 2][:, :].rearrange("p (h d) -> p h d", d=HD),
                                      coef[:, :].unsqueeze(2).to_broadcast([P, HEADS, HD]),
                                      ALU.mult).then_inc(scaled, 1)

                maximum(0)
                maximum(1)
                for u in range(NU):
                    w = len(keys(u)) * P
                    dve.wait_ge(turned, 2 * u + 2)
                    dve.tensor_copy(probT[:, 1, 0:w], m.psum[5][:, 0:w]).then_inc(kept_dve, 1)
                    if u + 2 < NU:
                        maximum(u + 2)
                    if u and u % HPG == 0:
                        scale(u // HPG - 1)
                scale(NU // HPG - 1)

            @block.gpsimd
            def _(pool):
                pool.memset(zeros[:, :], 0.0).then_inc(zeroed, 1)
                for n in range(NU // HPG):
                    i, br, h = units[n * HPG]
                    out = mix[:, i, 0:HEADS * HD].rearrange("p (h d) -> p h d", h=HEADS)
                    if n:
                        pool.wait_ge(combined, n)
                    pool.wait_ge(scaled, n + 1)
                    pool.tensor_tensor(out, out, part[:, n % 2], ALU.add).then_inc(combined, 1)


def gla(m, gqk, gv, gr, al, mix):
    m.phase()
    nc, a = m.nc, m.a
    NF = GH * GDK // P
    CAP = 80.0
    with ExitStack() as t:
        alT = m.sb(t, "alT", [GRANK + 1, S])
        wa = m.sb(t, "wa2", [GRANK + 1, GH * GDK])
        tri = m.sb(t, "tri16", [P, P])
        keep = m.sb(t, "keep", [P, GCH])
        la = m.sb(t, "log_a", [P, T, GH * GDK])
        ex = m.sb(t, "ex", [P, T, GH * GDK])
        b = m.sb(t, "b", [P, NF, S])
        qb = m.sb(t, "q_decayed", [P, NF, S])
        qe = m.sb(t, "q_ref", [P, NF, S])
        kl = m.sb(t, "k_last", [P, NF, S])
        ks = m.sb(t, "k_ref", [P, NSUB, S])
        klt = m.sb(t, "k_last_tok", [P, T, NF * P])
        att = m.sb(t, "att", [P, GH, T, P])
        state = m.sb(t, "state", [P, NF, NCH, 2 * GDV])
        dec = m.sb(t, "dec", [P, NF, NCH])
        o = m.sb(t, "gla_o", [P, T, GH * GDV])
        sq = m.sb(t, "gla_sq", [P, T, GH * GDV])
        ms = m.sb(t, "gla_ms", [P, T * GH])
        root = m.sb(t, "gla_root", [P, T * GH])
        og = m.sb(t, "gla_onorm_row", [P, GDV])
        (small_in, made, dve_c, act_c, al_t, al_k, lin, lin_v, absd, exped, plus1, logged, la_done, cum, cum_k,
         d_qb, e_qb, d_qe, e_qe, d_kl, e_kl, d_ks, e_ks, ks_done, q_done, kl_done, kl_t, kl_k, atted, att_k,
         kv_done, kv_k, states, o_done, o_k, silu, mean, rooted) = (m.psem(f"gla_{s}") for s in (
            "small_in", "made", "dve", "act", "al_t", "al_k", "lin", "lin_v", "absd", "exped", "plus1", "logged",
            "la_done", "cum", "cum_k", "d_qb", "e_qb", "d_qe", "e_qe", "d_kl", "e_kl", "d_ks", "e_ks", "ks_done",
            "q_done", "kl_done", "kl_t", "kl_k", "atted", "att_k", "kv_done", "kv_k", "states", "o_done", "o_k",
            "silu", "mean", "rooted"))

        def read_scores(dve, f):
            for h in (2 * f, 2 * f + 1):
                for p in range(2):
                    half = slice(p * GCH, (p + 1) * GCH)
                    src = m.psum[h % 2][half, :].rearrange("p (i c) -> p i c", i=T)[:, :, p * GCH:(p + 1) * GCH]
                    ins = dve.tensor_tensor(att[half, h, :, p * GCH:(p + 1) * GCH], src,
                                            keep[half, :].unsqueeze(1).to_broadcast([GCH, T, GCH]), ALU.mult)
            ins.then_inc(att_k, 1)

        def sub_ref(f):
            return b[:, f, :].rearrange("p (r j) -> p r j", j=SUB)[:, :, SUB // 2:SUB // 2 + 1]

        with nc.Block() as block:
            @block.sync
            def _(sp):
                sp.dma_start(wa[0:GRANK, :], a["gla_wa2"][0]).then_inc(small_in, 16)
                sp.dma_start(wa[GRANK:GRANK + 1, :], a["gla_ba"]).then_inc(small_in, 16)
                sp.dma_start(og[:, :], a["gla_onorm"][0].partition_broadcast(P)).then_inc(small_in, 16)

            @block.gpsimd
            def _(pool):
                pool.memset(alT[:, :], 1.0).then_inc(made, 1)
                pool.memset(tri[:, :], 1.0 / GTAU).then_inc(made, 1)
                pool.memset(keep[:, :], 1.0).then_inc(made, 1)
                pool.memset(att[:, :, :, :], 0.0).then_inc(made, 1)
                pool.memset(state[:, :, :, :], 0.0).then_inc(made, 1)
                pool.wait_ge(made, 5)
                pool.affine_select(out=tri[:, :], in_=tri[:, :], compare_op=ALU.is_ge, fill=0.0, base=0,
                                   pattern=[[1, P]], channel_multiplier=-1).then_inc(made, 1)
                for p in range(2):
                    pool.wait_ge(made, 6 + p)
                    pool.affine_select(out=keep[p * GCH:(p + 1) * GCH, :], in_=keep[p * GCH:(p + 1) * GCH, :],
                                       compare_op=ALU.is_ge, fill=0.0, base=0, pattern=[[1, GCH]],
                                       channel_multiplier=-1).then_inc(made, 1)
                pool.wait_ge(made, 8)
                pool.memset(tri[0:GCH, GCH:P], 0.0).then_inc(made, 1)

            @block.tensor
            def _(pe):
                for i in range(T):
                    ins = pe.transpose(m.psum[0][0:GRANK, i * P:(i + 1) * P], al[:, i, :], m.ident[:, :])
                ins.then_inc(al_t, 1)
                pe.wait_ge(small_in, 48)
                pe.wait_ge(al_k, 1)
                for i in range(T):
                    ins = pe.matmul(m.psum[1 + i // 2][:, (i % 2) * 256:(i % 2 + 1) * 256],
                                    alT[:, i * P:(i + 1) * P], wa[:, :], start=True, stop=True)
                ins.then_inc(lin, 1)
                pe.wait_ge(made, 9)
                pe.wait_ge(la_done, 1)
                for f in range(NF):
                    for i in range(T):
                        ins = pe.matmul(m.psum[3 + f][:, i * P:(i + 1) * P], la[:, i, f * P:(f + 1) * P], tri[:, :],
                                        start=True, stop=True)
                ins.then_inc(cum, 1)
                pe.wait_ge(q_done, 2 * NF)
                for f in range(NF):
                    pe.wait_ge(ks_done, f + 1)
                    for h in (2 * f, 2 * f + 1):
                        half = slice((h % 2) * GDK, (h % 2 + 1) * GDK)
                        for c in range(NCH):
                            for s in range(NSUB):
                                q0 = c * GCH + s * SUB
                                col = (c // 2) * P + (c % 2) * GCH + s * SUB
                                ins = pe.matmul(m.psum[h % 2][(c % 2) * GCH:(c % 2 + 1) * GCH, col:col + SUB],
                                                ks[half, s, c * GCH:(c + 1) * GCH], qe[half, f, q0:q0 + SUB],
                                                start=True, stop=True)
                    ins.then_inc(atted, 1)
                    if f == 0:
                        pe.wait_ge(kl_done, NF)
                        for i in range(T):
                            for f2 in range(NF):
                                ins = pe.transpose(m.psum[2 + i // 2][:, (i % 2) * 256 + f2 * P:(i % 2) * 256 + (f2 + 1) * P],
                                                   kl[:, f2, i * P:(i + 1) * P], m.ident[:, :])
                        ins.then_inc(kl_t, 1)
                        pe.wait_ge(att_k, 1)
                pe.wait_ge(kl_k, 1)
                for c in range(NCH - 1):
                    i, half = c // 2, slice((c % 2) * GCH, (c % 2 + 1) * GCH)
                    for f in range(NF):
                        if c >= 2:
                            pe.wait_ge(states, NF * (c - 1))
                        ins = pe.matmul(m.psum[2 + c % 2][:, f * 256:(f + 1) * 256], klt[half, i, f * P:(f + 1) * P],
                                        gv[half, i, f * 2 * GDV:(f + 1) * 2 * GDV], start=True, stop=True)
                    ins.then_inc(kv_done, 1)
                pe.wait_ge(att_k, NF)
                pe.wait_ge(states, NF * (NCH - 1))
                for i in range(T):
                    out = m.psum[4 + i]
                    for h in range(GH):
                        pe.matmul(out[:, h * GDV:(h + 1) * GDV], att[:, h, i, :], gv[:, i, h * GDV:(h + 1) * GDV],
                                  start=h == 0, stop=False, skip_group_check=True)
                    for c in (2 * i, 2 * i + 1):
                        if c:
                            for f in range(NF):
                                half = slice((c % 2) * GCH, (c % 2 + 1) * GCH)
                                ins = pe.matmul(out[half, f * 256:(f + 1) * 256], qb[:, f, c * GCH:(c + 1) * GCH],
                                                state[:, f, c, :], start=False, stop=True, skip_group_check=True)
                    ins.then_inc(o_done, 1)

            @block.scalar
            def _(act):
                act.wait_ge(absd, 1)
                act.activation(ex[:, :, :], ex[:, :, :], ACT.Exp).then_inc(exped, 1)
                act.wait_ge(plus1, 1)
                act.activation(ex[:, :, :], ex[:, :, :], ACT.Ln).then_inc(logged, 1)
                for f in range(NF):
                    act.wait_ge(cum_k, f + 1)
                    act.activation(qb[:, f, :], b[:, f, :], ACT.Exp).then_inc(e_qb, 1)
                    act.activation(dec[:, f, :], b[:, f, :].rearrange("p (c j) -> p c j", j=GCH)[:, :, GCH - 1], ACT.Exp)
                    act.wait_ge(d_qe, f + 1)
                    act.activation(qe[:, f, :], qe[:, f, :], ACT.Exp).then_inc(e_qe, 1)
                    act.wait_ge(d_kl, f + 1)
                    act.activation(kl[:, f, :], kl[:, f, :], ACT.Exp).then_inc(e_kl, 1)
                for f in range(NF):
                    act.wait_ge(d_ks, f + 1)
                    act.activation(ks[:, :, :], ks[:, :, :], ACT.Exp).then_inc(e_ks, 1)
                    if f == 0:
                        act.wait_ge(kl_t, 1)
                        for i2 in range(2):
                            ins = act.activation(klt[:, 2 * i2:2 * i2 + 2, :], m.psum[2 + i2][:, :].rearrange("p (i f) -> p i f", i=2), ACT.Copy)
                        ins.then_inc(kl_k, 1)
                act.activation(gr[:, :, :], gr[:, :, :], ACT.Silu).then_inc(silu, 1)
                for i in range(T):
                    act.wait_ge(o_done, i + 1)
                    act.activation(o[:, i, :], m.psum[4 + i][:, :], ACT.Copy).then_inc(o_k, 1)
                act.wait_ge(mean, 1)
                act.activation(root[:, :], ms[:, :], ACT.Sqrt).then_inc(rooted, 1)

            @block.vector
            def _(dve):
                link = Chain(dve, dve_c).link
                dve.wait_ge(made, 5)
                dve.wait_ge(al_t, 1)
                dve.tensor_copy(alT[0:GRANK, :], m.psum[0][0:GRANK, :]).then_inc(al_k, 1)
                dve.wait_ge(lin, 1)
                for i2 in range(2):
                    ins = dve.tensor_copy(la[:, 2 * i2:2 * i2 + 2, :], m.psum[1 + i2][:, :].rearrange("p (i f) -> p i f", i=2))
                link(ins)
                dve.scalar_tensor_tensor(out=ex[:, :, :], in0=la[:, :, :], scalar=-1.0, in1=la[:, :, :],
                                         op0=ALU.mult, op1=ALU.min).then_inc(absd, 1)
                dve.wait_ge(exped, 1)
                dve.tensor_scalar(ex[:, :, :], ex[:, :, :], 1.0, None, ALU.add).then_inc(plus1, 1)
                dve.wait_ge(logged, 1)
                dve.scalar_tensor_tensor(out=la[:, :, :], in0=la[:, :, :], scalar=0.0, in1=ex[:, :, :],
                                         op0=ALU.min, op1=ALU.subtract).then_inc(la_done, 1)
                dve.wait_ge(cum, 1)
                for f in range(NF):
                    dve.tensor_copy(b[:, f, :], m.psum[3 + f][:, :]).then_inc(cum_k, 1)
                    dve.wait_ge(cum_k, f + 1)
                    link(dve.tensor_tensor(qe[:, f, :].rearrange("p (r j) -> p r j", j=SUB),
                                           b[:, f, :].rearrange("p (r j) -> p r j", j=SUB),
                                           sub_ref(f).to_broadcast([P, S // SUB, SUB]), ALU.subtract))
                    dve.tensor_scalar(qe[:, f, :], qe[:, f, :], CAP, None, ALU.min).then_inc(d_qe, 1)
                    bc = b[:, f, :].rearrange("p (c j) -> p c j", j=GCH)
                    dve.tensor_tensor(kl[:, f, :].rearrange("p (c j) -> p c j", j=GCH),
                                      bc[:, :, GCH - 1:GCH].to_broadcast([P, NCH, GCH]), bc, ALU.subtract).then_inc(d_kl, 1)
                for f in range(NF):
                    dve.wait_ge(e_qb, f + 1)
                    dve.tensor_tensor(qb[:, f, :], qb[:, f, :], gqk[:, f, :], ALU.mult).then_inc(q_done, 1)
                    dve.wait_ge(e_qe, f + 1)
                    dve.tensor_tensor(qe[:, f, :], qe[:, f, :], gqk[:, f, :], ALU.mult).then_inc(q_done, 1)
                    dve.wait_ge(e_kl, f + 1)
                    dve.tensor_tensor(kl[:, f, :], kl[:, f, :], gqk[:, NF + f, :], ALU.mult).then_inc(kl_done, 1)
                for f in range(NF):
                    if f:
                        dve.wait_ge(atted, f)
                    bc = b[:, f, :].rearrange("p (c j) -> p c j", j=GCH)
                    for s in range(NSUB):
                        at = s * SUB + SUB // 2
                        ins = dve.tensor_tensor(ks[:, s, :].rearrange("p (c j) -> p c j", j=GCH),
                                                bc[:, :, at:at + 1].to_broadcast([P, NCH, GCH]), bc, ALU.subtract)
                    link(ins)
                    dve.tensor_scalar(ks[:, :, :], ks[:, :, :], CAP, None, ALU.min).then_inc(d_ks, 1)
                    if f:
                        dve.wait_ge(made, 8)
                        read_scores(dve, f - 1)
                    dve.wait_ge(e_ks, f + 1)
                    dve.tensor_tensor(ks[:, :, :], ks[:, :, :], gqk[:, NF + f, :].unsqueeze(1).to_broadcast([P, NSUB, S]),
                                      ALU.mult).then_inc(ks_done, 1)
                dve.wait_ge(atted, NF)
                read_scores(dve, NF - 1)
                for c in range(NCH - 1):
                    dve.wait_ge(kv_done, c + 1)
                    for f in range(NF):
                        for h in range(2):
                            half, cols = slice(h * GDK, (h + 1) * GDK), slice(h * GDV, (h + 1) * GDV)
                            ins = dve.scalar_tensor_tensor(
                                out=state[half, f, c + 1, cols], in0=state[half, f, c, cols], scalar=dec[half, f, c:c + 1],
                                in1=m.psum[2 + c % 2][half, f * 256 + h * GDV:f * 256 + (h + 1) * GDV],
                                op0=ALU.mult, op1=ALU.add)
                        ins.then_inc(states, 1)
                    dve.wait_ge(states, NF * (c + 1))
                dve.wait_ge(o_k, T)
                link(dve.tensor_tensor(sq[:, :, :], o[:, :, :], o[:, :, :], ALU.mult))
                link(dve.tensor_reduce(ms[:, :], sq[:, :, :].rearrange("p t (h d) -> p (t h) d", d=GDV), AX.X, ALU.add))
                dve.tensor_scalar(ms[:, :], ms[:, :], 1.0 / GDV, EPS, ALU.mult, ALU.add).then_inc(mean, 1)
                dve.wait_ge(silu, 1)
                link(dve.tensor_tensor(gr[:, :, :], gr[:, :, :], o[:, :, :], ALU.mult))
                link(dve.tensor_tensor(gr[:, :, :].rearrange("p t (h d) -> p (t h) d", d=GDV),
                                       gr[:, :, :].rearrange("p t (h d) -> p (t h) d", d=GDV),
                                       og[:, :].unsqueeze(1).to_broadcast([P, T * GH, GDV]), ALU.mult))
                dve.wait_ge(rooted, 1)
                link(dve.reciprocal(ms[:, :], root[:, :]))
                for i in range(T):
                    ins = dve.tensor_tensor(mix[:, i, HEADS * HD:].rearrange("p (h d) -> p h d", d=GDV),
                                            gr[:, i, :].rearrange("p (h d) -> p h d", d=GDV),
                                            ms[:, i * GH:(i + 1) * GH].unsqueeze(2).to_broadcast([P, GH, GDV]), ALU.mult)
                link(ins)



def split_transpose(m, name, src, hi, lo):
    m.phase()
    turned, hi_out, lo_out = (m.psem(f"{name}_{s}") for s in ("turned", "hi_out", "lo_out"))
    with m.nc.Block() as block:
        @block.tensor
        def _(pe):
            for k in range(KD):
                for t in range(T):
                    ins = pe.transpose(m.psum[k][:, t * P:(t + 1) * P], src[:, t, k * P:(k + 1) * P], m.ident[:, :])
                ins.then_inc(turned, 1)

        @block.scalar
        def _(act):
            for k in range(KD):
                act.wait_ge(turned, k + 1)
                act.activation(hi[:, k, :], m.psum[k][:, :], ACT.Copy).then_inc(hi_out, 1)

        @block.vector
        def _(dve):
            for k in range(KD):
                dve.wait_ge(hi_out, k + 1)
                dve.tensor_tensor(lo[:, k, :], m.psum[k][:, :], hi[:, k, :], ALU.subtract).then_inc(lo_out, 1)


def linear_residual(m, name, first, n_cols, parts):
    m.phase()
    added = m.psem(f"{name}_added")
    total = n_cols * len(parts)

    def add(dve, j):
        n = j // len(parts)
        m.done(dve, first + j)
        for t in range(T):
            cols = slice(n * GC, (n + 1) * GC)
            dve.tensor_tensor(m.x[:, t, cols], m.x[:, t, cols], m.psum[4 * (n % 2) + t][:, :], ALU.add).then_inc(added, 1)

    with m.nc.Block() as block:
        @block.sync
        def _(sp):
            m.load(sp, first + total + 1)

        @block.scalar
        def _(act):
            for j in range(total):
                m.split_hi(act, first + j)

        @block.tensor
        def _(pe):
            for n in range(n_cols):
                if n >= 2:
                    pe.wait_ge(added, T * (n - 1))
                for q, (hi, lo) in enumerate(parts):
                    m.product(pe, first + n * len(parts) + q, False, m.psum[4 * (n % 2):4 * (n % 2) + 4], hi, lo,
                              first=q == 0, last=q == len(parts) - 1)

        @block.vector
        def _(dve):
            for j in range(total):
                m.split_lo(dve, first + j)
                done = j - 1
                if done >= 0 and done % len(parts) == len(parts) - 1:
                    add(dve, done)
            add(dve, total - 1)


def hybrid_layer(m, first, mix_out=None):
    a = m.a
    with ExitStack() as c:
        mix = m.sb(c, "mix", [P, T, D])
        with ExitStack() as c2:
            outputs = qk, v_sw, kvc, gqk, gv, gr, ga, al = projection_outputs(m, c2)
            with ExitStack() as c3:
                hi, lo = m.split_pair(c3, "h_mix0")
                norm_transpose(m, "mix0", m.x, a["norm_mix"][0], T, hi, lo)
                hybrid_projection(m, outputs, first, hi, lo)
            with ExitStack() as c3:
                qkT, kcT, vbd = nsa_prepare(m, c3, qk, kvc)
                nsa_attention(m, qkT, kcT, vbd, v_sw, ga, mix)
            gla(m, gqk, gv, gr, al, mix)
        if mix_out is not None:
            m.phase(); s = m.psem("mixdbg")
            with m.nc.Block() as block:
                @block.sync
                def _(sp):
                    for t in range(T):
                        sp.dma_start(mix_out[t * P:(t + 1) * P, :], mix[:, t, :]).then_inc(s, 16)
                    sp.wait_ge(s, 64)
        hi, lo = m.split_pair(c, "mixT")
        split_transpose(m, "mix0o", mix, hi, lo)
        linear_residual(m, "hyb_out", first + 8, 2, [(hi, lo)])


def project_heads(m, name, first, n_groups, normed, tiles, hi, lo, out, ms):
    m.phase()
    nc = m.nc
    out_act, out_dve = m.psem(f"{name}_out_act"), m.psem(f"{name}_out_dve")
    hpg = GC // XHD
    n_normed = normed // GC
    with ExitStack() as t:
        junk = m.sb(t, f"{name}_junk", [P, GC])
        with nc.Block() as block:
            @block.sync
            def _(sp):
                m.load(sp, first + n_groups + 1)

            @block.tensor
            def _(pe):
                for n in range(n_groups):
                    if n >= 2:
                        pe.wait_ge(out_act, tiles * min(n - 1, n_normed))
                        if n - 1 > n_normed:
                            pe.wait_ge(out_dve, tiles * (n - 1))
                        else:
                            pe.wait_ge(out_dve, tiles * (n - 1))
                    m.product(pe, first + n, False, m.psum[4 * (n % 2):4 * (n % 2) + 4], hi, lo, tiles=tiles)

            @block.scalar
            def _(act):
                m.split_hi(act, first)
                for n in range(n_groups):
                    if n + 1 < n_groups:
                        m.split_hi(act, first + n + 1)
                    if n >= n_normed:
                        continue
                    m.done(act, first + n)
                    for i in range(tiles):
                        for h in range(hpg):
                            ins = act.activation(junk[:, h * XHD:(h + 1) * XHD],
                                                 m.psum[4 * (n % 2) + i][:, h * XHD:(h + 1) * XHD], ACT.Square,
                                                 accum_out=ms[:, i, n * hpg + h:n * hpg + h + 1])
                        ins.then_inc(out_act, 1)
                        act.wait_ge(out_act, n * tiles + i + 1)

            @block.vector
            def _(dve):
                m.split_lo(dve, first)
                for n in range(n_groups):
                    if n + 1 < n_groups:
                        m.split_lo(dve, first + n + 1)
                    m.done(dve, first + n)
                    for i in range(tiles):
                        if n < n_normed:
                            dve.wait_ge(out_act, n * tiles + i + 1)
                        dve.tensor_copy(out[:, i, n * GC:(n + 1) * GC], m.psum[4 * (n % 2) + i][:, :]).then_inc(out_dve, 1)


def norm_heads(m, name, src, tiles, gain, scale, ms, dst):
    m.phase()
    nc = m.nc
    g_in, mean, rooted, normed, turned, out_act, out_dve, dve_c = (
        m.psem(f"{name}_{s}") for s in ("g_in", "mean", "rooted", "normed", "turned", "out_act", "out_dve", "dve"))
    with ExitStack() as t:
        g = m.sb(t, f"{name}_g", [P, XHD])
        root = m.sb(t, f"{name}_root", [P, tiles * XH])
        with nc.Block() as block:
            @block.sync
            def _(sp):
                sp.dma_start(g[:, :], gain.partition_broadcast(P)).then_inc(g_in, 16)

            @block.scalar
            def _(act):
                act.wait_ge(mean, 1)
                act.activation(root[:, :], ms[:, :, :].rearrange("p t h -> p (t h)"), ACT.Sqrt).then_inc(rooted, 1)
                for k in range(0, KD, 2):
                    act.wait_ge(turned, k + 1)
                    act.activation(dst[:, k, :], m.psum[k][:, 0:tiles * P], ACT.Copy).then_inc(out_act, 1)

            @block.vector
            def _(dve):
                link = Chain(dve, dve_c).link
                dve.tensor_scalar(ms[:, :, :], ms[:, :, :], 1.0 / XHD, EPS, ALU.mult, ALU.add).then_inc(mean, 1)
                dve.wait_ge(g_in, 16)
                link(dve.tensor_scalar(g[:, :], g[:, :], scale, None, ALU.mult))
                dve.wait_ge(rooted, 1)
                link(dve.reciprocal(ms[:, :, :].rearrange("p t h -> p (t h)"), root[:, :]))
                for i in range(tiles):
                    for h in range(XH):
                        cols = slice(h * XHD, (h + 1) * XHD)
                        ins = dve.scalar_tensor_tensor(out=src[:, i, cols], in0=src[:, i, cols], scalar=ms[:, i, h:h + 1],
                                                       in1=g[:, :], op0=ALU.mult, op1=ALU.mult)
                    ins.then_inc(normed, 1)
                for k in range(1, KD, 2):
                    dve.wait_ge(turned, k + 1)
                    dve.tensor_copy(dst[:, k, :], m.psum[k][:, 0:tiles * P]).then_inc(out_dve, 1)

            @block.tensor
            def _(pe):
                pe.wait_ge(normed, tiles)
                for k in range(KD):
                    for i in range(tiles):
                        ins = pe.transpose(m.psum[k][:, i * P:(i + 1) * P], src[:, i, k * P:(k + 1) * P], m.ident[:, :])
                    ins.then_inc(turned, 1)


def cross_attend(m, name, qT, kT, v, o_hi, o_lo):
    m.phase()
    nc = m.nc
    HH = XHD // P
    units = [(h, i) for h in range(XH) for i in range(T)]
    (scored, maxed, exped, normed, turned, kept, summed, o_hi_out, o_lo_out, dve_c) = (m.psem(f"{name}_{s}") for s in (
        "scored", "maxed", "exped", "normed", "turned", "kept", "summed", "o_hi_out", "o_lo_out", "dve"))
    with ExitStack() as t:
        prob = m.sb(t, f"{name}_prob", [P, 2, N_MEM])
        pT = m.sb(t, f"{name}_pT", [P, 2, MT, S])
        nmax = m.sb(t, f"{name}_nmax", [P, len(units)])
        sums = m.sb(t, f"{name}_sums", [P, len(units)])
        with nc.Block() as block:
            @block.tensor
            def _(pe):
                def score(u):
                    h, i = units[u]
                    if u >= 2:
                        pe.wait_ge(exped, u - 1)
                    for d in range(HH):
                        ins = pe.matmul(m.psum[u % 2][:, 0:N_MEM], qT[:, HH * h + d, i * P:(i + 1) * P], kT[:, HH * h + d, :],
                                        start=d == 0, stop=d == HH - 1)
                    ins.then_inc(scored, 1)

                score(0)
                for u, (h, i) in enumerate(units):
                    if u + 1 < len(units):
                        score(u + 1)
                    pe.wait_ge(normed, u + 1)
                    if u >= 2:
                        pe.wait_ge(kept, u - 1)
                    for j in range(MT):
                        ins = pe.transpose(m.psum[2 + u % 2][:, j * P:(j + 1) * P], prob[:, u % 2, j * P:(j + 1) * P], m.ident[:, :])
                    ins.then_inc(turned, 1)
                    if i == T - 1:
                        pe.wait_ge(kept, u + 1)
                        if h >= 2:
                            pe.wait_ge(o_lo_out, HH * (h - 1))
                        for d in range(HH):
                            for j in range(MT):
                                ins = pe.matmul(m.psum[4 + 2 * (h % 2) + d][:, :], v[:, j, h * XHD + d * P:h * XHD + (d + 1) * P],
                                                pT[:, h % 2, j, :], start=j == 0, stop=j == MT - 1)
                            ins.then_inc(summed, 1)

            @block.scalar
            def _(act):
                def keep(u):
                    h, i = units[u]
                    act.wait_ge(turned, u + 1)
                    if h >= 2 and i == 0:
                        act.wait_ge(summed, HH * (h - 1))
                    act.activation(pT[:, h % 2, :, i * P:(i + 1) * P],
                                   m.psum[2 + u % 2][:, 0:MT * P].rearrange("p (j t) -> p j t", j=MT), ACT.Copy).then_inc(kept, 1)

                def output(h):
                    for d in range(HH):
                        act.wait_ge(summed, HH * h + d + 1)
                        act.activation(o_hi[:, HH * h + d, :], m.psum[4 + 2 * (h % 2) + d][:, :], ACT.Copy).then_inc(o_hi_out, 1)

                for u, (h, i) in enumerate(units):
                    act.wait_ge(maxed, u + 1)
                    if u >= 2:
                        act.wait_ge(turned, u - 1)
                    act.activation(prob[:, u % 2, :], m.psum[u % 2][:, 0:N_MEM], ACT.Exp, bias=nmax[:, u:u + 1],
                                   accum_out=sums[:, u:u + 1]).then_inc(exped, 1)
                    if u:
                        keep(u - 1)
                    if h and i == 1:
                        output(h - 1)
                keep(len(units) - 1)
                output(XH - 1)

            @block.vector
            def _(dve):
                link = Chain(dve, dve_c).link

                def maximum(u):
                    dve.wait_ge(scored, u + 1)
                    dve.tensor_reduce(nmax[:, u:u + 1], m.psum[u % 2][:, 0:N_MEM], AX.X, ALU.max, negate=True).then_inc(maxed, 1)

                def rest(h):
                    for d in range(HH):
                        dve.wait_ge(o_hi_out, HH * h + d + 1)
                        dve.tensor_tensor(o_lo[:, HH * h + d, :], m.psum[4 + 2 * (h % 2) + d][:, :], o_hi[:, HH * h + d, :],
                                          ALU.subtract).then_inc(o_lo_out, 1)

                maximum(0)
                for u, (h, i) in enumerate(units):
                    if u + 1 < len(units):
                        maximum(u + 1)
                    dve.wait_ge(exped, u + 1)
                    link(dve.reciprocal(sums[:, u:u + 1], sums[:, u:u + 1]))
                    dve.tensor_scalar(prob[:, u % 2, :], prob[:, u % 2, :], sums[:, u:u + 1], None, ALU.mult).then_inc(normed, 1)
                    if h and i == 2:
                        rest(h - 1)
                rest(XH - 1)


def cross_attention(m, layer, first):
    a, nm = m.a, f"x{layer}"
    with ExitStack() as c:
        kT = m.sb(c, f"{nm}_kT", [P, KD, N_MEM])
        v = m.sb(c, f"{nm}_kv", [P, MT, 2 * D])
        with ExitStack() as c2:
            mem = m.sb(c2, f"{nm}_mem", [P, MT, D])
            ms = m.sb(c2, f"{nm}_kms", [P, MT, XH])
            m.phase()
            loaded = m.psem(f"{nm}_mem_in")
            with m.nc.Block() as block:
                @block.sync
                def _(sp):
                    for i in range(MT):
                        sp.dma_start(mem[:, i, :], a["mem"][0, i * P:(i + 1) * P, :]).then_inc(loaded, 16)
                    sp.wait_ge(loaded, 16 * MT)
            hi, lo = m.split_pair(c2, f"{nm}_mem", n=N_MEM)
            norm_transpose(m, f"{nm}_nm", mem, a["norm_mem"][layer], MT, hi, lo)
            project_heads(m, f"{nm}_kv", first, 4, D, MT, hi, lo, v, ms)
            norm_heads(m, f"{nm}_kn", v, MT, a["x_knorm"][layer], 1.0, ms, kT)
        qT = m.sb(c, f"{nm}_qT", [P, KD, S])
        with ExitStack() as c2:
            q = m.sb(c2, f"{nm}_q", [P, T, D])
            ms = m.sb(c2, f"{nm}_qms", [P, T, XH])
            hi, lo = m.split_pair(c2, f"{nm}_h")
            norm_transpose(m, f"{nm}_nx", m.x, a["norm_xattn"][layer], T, hi, lo)
            project_heads(m, f"{nm}_q", first + 4, 2, D, T, hi, lo, q, ms)
            norm_heads(m, f"{nm}_qn", q, T, a["x_qnorm"][layer], XHD ** -0.5, ms, qT)
        o_hi, o_lo = m.split_pair(c, f"{nm}_o")
        cross_attend(m, f"{nm}_at", qT, kT, v[:, :, D:2 * D], o_hi, o_lo)
        linear_residual(m, f"{nm}_wo", first + 6, 2, [(o_hi, o_lo)])


def sgu_layer(m, layer, first):
    nc, a = m.nc, m.a
    NGR = SGW // GC
    KU = SGW // P
    with ExitStack() as c:
        uT = m.sb(c, "uT", [P, KU, S])
        v = m.sb(c, "sg_v", [P, T, SGW])
        wsT = m.sb(c, "sg_wsT", [P, SGG, P])
        bsr = m.sb(c, "sg_bs_row", [P, SGG, P])
        vsum = m.sb(c, "sg_vsum", [P, T, NGR])
        with ExitStack() as c2:
            hi, lo = m.split_pair(c2, "h_sg")
            norm_transpose(m, "mix1", m.x, a["norm_mix"][layer], T, hi, lo)
            m.phase()
            read = m.psem("sg_read")
            with nc.Block() as block:
                @block.sync
                def _(sp):
                    m.load(sp, first + 2 * NGR + 1)

                @block.tensor
                def _(pe):
                    for n in range(2 * NGR):
                        if n >= 2:
                            pe.wait_ge(read, 4 * (n - 1))
                        m.product(pe, first + n, n < NGR, m.psum[4 * (n % 2):4 * (n % 2) + 4], hi, lo)

                @block.scalar
                def _(act):
                    m.split_hi(act, first)
                    for n in range(2 * NGR):
                        if n + 1 < 2 * NGR:
                            m.split_hi(act, first + n + 1)
                        m.done(act, first + n)
                        for b in range(4):
                            ps = m.psum[4 * (n % 2) + b][:, :]
                            if n < NGR:
                                act.activation(uT[:, 4 * n + b, :], ps, ACT.Gelu_apprx_tanh).then_inc(read, 1)
                            else:
                                j = n - NGR
                                act.activation(v[:, b, j * GC:(j + 1) * GC], ps, ACT.Gelu_apprx_tanh,
                                               accum_out=vsum[:, b, j:j + 1]).then_inc(read, 1)

                @block.vector
                def _(dve):
                    for n in range(2 * NGR):
                        m.split_lo(dve, first + n)
        with ExitStack() as c2:
            ws = m.sb(c2, "sgu_ws", [P, SGG, P])
            g = m.sb(c2, "sgu_g", [P, SGW])
            b = m.sb(c2, "sgu_b", [P, SGW])
            nmean = m.sb(c2, "sg_nmean", [P, T])
            m.phase()
            var = m.sb(c2, "sg_var", [P, T])
            root = m.sb(c2, "sg_root", [P, T])
            (small_in, ws_in, ws_masked, mean, squared, varied, rooted, dve_c, centred, gained, turned, ws_out) = (
                m.psem(f"sg_{s}") for s in ("small_in", "ws_in", "ws_masked", "mean", "squared", "varied", "rooted", "dve",
                                           "centred", "gained", "turned", "ws_out"))
            junk = m.sb(c2, "sg_junk", [P, SGW])
            with nc.Block() as block:
                @block.sync
                def _(sp):
                    sp.dma_start(ws[:, :, :], a["sg_ws"][0].rearrange("g t s -> t g s")).then_inc(ws_in, 16)
                    sp.dma_start(g[:, :], a["sg_ln_g"][0].partition_broadcast(P)).then_inc(small_in, 16)
                    sp.dma_start(b[:, :], a["sg_ln_b"][0].partition_broadcast(P)).then_inc(small_in, 16)
                    sp.dma_start(bsr[:, :, :], a["sg_bs"][0].partition_broadcast(P)).then_inc(small_in, 16)

                @block.gpsimd
                def _(pool):
                    pool.wait_ge(ws_in, 16)
                    pool.affine_select(out=ws[:, :, :], in_=ws[:, :, :], compare_op=ALU.is_ge, fill=0.0, base=0,
                                       pattern=[[0, SGG], [-1, P]], channel_multiplier=1).then_inc(ws_masked, 1)
                    pool.wait_ge(small_in, 48)
                    for i in range(T):
                        pool.wait_ge(centred, i + 1)
                        pool.tensor_tensor(v[:, i, :], v[:, i, :], g[:, :], ALU.mult).then_inc(gained, 1)

                @block.scalar
                def _(act):
                    act.wait_ge(mean, 1)
                    for i in range(T):
                        if i:
                            act.wait_ge(squared, i)
                        act.activation(junk[:, :], v[:, i, :], ACT.Square, bias=nmean[:, i:i + 1],
                                       accum_out=var[:, i:i + 1]).then_inc(squared, 1)
                    act.wait_ge(varied, 1)
                    act.activation(root[:, :], var[:, :], ACT.Sqrt).then_inc(rooted, 1)
                    for q in range(2):
                        act.wait_ge(turned, q + 1)
                        act.activation(wsT[:, 4 * q:4 * q + 4, :], m.psum[q][:, :].rearrange("p (g t) -> p g t", g=4), ACT.Copy)

                @block.vector
                def _(dve):
                    link = Chain(dve, dve_c).link
                    link(dve.tensor_reduce(nmean[:, :], vsum[:, :, :], AX.X, ALU.add))
                    dve.tensor_scalar(nmean[:, :], nmean[:, :], -1.0 / SGW, None, ALU.mult).then_inc(mean, 1)
                    dve.wait_ge(squared, T)
                    dve.tensor_scalar(var[:, :], var[:, :], 1.0 / SGW, EPS, ALU.mult, ALU.add).then_inc(varied, 1)
                    dve.wait_ge(rooted, 1)
                    link(dve.reciprocal(var[:, :], root[:, :]))
                    for i in range(T):
                        dve.tensor_scalar(v[:, i, :], v[:, i, :], nmean[:, i:i + 1], var[:, i:i + 1], ALU.add, ALU.mult)\
                           .then_inc(centred, 1)
                    for i in range(T):
                        dve.wait_ge(gained, i + 1)
                        ins = dve.tensor_tensor(v[:, i, :], v[:, i, :], b[:, :], ALU.add)
                    link(ins)

                @block.tensor
                def _(pe):
                    pe.wait_ge(ws_masked, 1)
                    for q in range(2):
                        for j in range(4):
                            ins = pe.transpose(m.psum[q][:, j * P:(j + 1) * P], ws[:, 4 * q + j, :], m.ident[:, :])
                        ins.then_inc(turned, 1)
        um_hi, um_lo = m.split_pair(c, "um", k=KU)
        m.phase()
        mixed, biased, gated, split, lo_out = (m.psem(f"sg_{s}") for s in ("mixed", "biased", "gated", "split", "lo_out"))
        with nc.Block() as block:
            @block.tensor
            def _(pe):
                for k in range(KU):
                    if k >= 8:
                        pe.wait_ge(biased, k - 7)
                    for i in range(T):
                        ins = pe.matmul(m.psum[k % 8][:, i * P:(i + 1) * P], v[:, i, k * P:(k + 1) * P],
                                        wsT[:, k * SGG // KU, :], start=True, stop=True)
                    ins.then_inc(mixed, 1)

            @block.vector
            def _(dve):
                for k in range(KU):
                    dve.wait_ge(mixed, k + 1)
                    dve.tensor_tensor(m.psum[k % 8][:, :].rearrange("p (i t) -> p i t", i=T),
                                      m.psum[k % 8][:, :].rearrange("p (i t) -> p i t", i=T),
                                      bsr[:, k * SGG // KU, :].unsqueeze(1).to_broadcast([P, T, P]), ALU.add).then_inc(split, 1)
                    dve.wait_ge(split, k + 1)
                    dve.tensor_tensor(uT[:, k, :], uT[:, k, :], m.psum[k % 8][:, :], ALU.mult).then_inc(biased, 1)

            @block.scalar
            def _(act):
                for k in range(KU):
                    act.wait_ge(biased, k + 1)
                    act.activation(um_hi[:, k, :], uT[:, k, :], ACT.Copy).then_inc(gated, 1)

            @block.gpsimd
            def _(pool):
                for k in range(KU):
                    pool.wait_ge(gated, k + 1)
                    pool.tensor_tensor(um_lo[:, k, :], uT[:, k, :], um_hi[:, k, :], ALU.subtract).then_inc(lo_out, 1)
                pool.wait_ge(lo_out, KU)
        linear_residual(m, "sg_out", first + 2 * NGR, 2, [(um_hi[:, 0:KD], um_lo[:, 0:KD]), (um_hi[:, KD:KU], um_lo[:, KD:KU])])


def moe_route(m, layer, hT, slot_i, wgt, meta, idx_dram):
    m.phase()
    nc, a, nm = m.nc, m.a, f"r{layer}"
    NB = MAXB + 1
    with ExitStack() as t:
        def tile(name, shape, dt=F32):
            return m.sb(t, f"{nm}_{name}", shape, dt)
        rw = tile("rw", [P, KD, NE])
        rb = tile("rb", [P, NE])
        ones, before = tile("ones", [P, P]), tile("before", [P, P])
        e_row, g_row, b_row, thr = tile("e_row", [P, NE]), tile("g_row", [P, NG]), tile("b_row", [P, NB]), tile("thr", [P, T])
        lower = tile("lower", [P, NE, NE])
        zeros_i = tile("zeros_i", [P, SLOTS // P], I32)
        tok_i = tile("tok_i", [P, T], I32)
        lg, pr = tile("lg", [P, T, NE]), tile("pr", [P, T, NE])
        mx, sm = tile("mx", [P, T]), tile("sm", [P, T])
        gm, ge = tile("gm", [P, T, NG]), tile("ge", [P, T, NG])
        gb, gi = tile("gb", [P, T]), tile("gi", [P, T])
        pm, cand = tile("pm", [P, T, NE]), tile("cand", [P, T, NE])
        top, ti = tile("top", [P, 2, T]), tile("ti", [P, 2, T])
        oh = tile("oh", [P, 2, T, NE])
        both = tile("both", [P, T, NE])
        cnt, nb, nbx = tile("cnt", [P, NE]), tile("nb", [P, NE]), tile("nbx", [P, NE, T])
        low, cum, off = tile("low", [P, NE, NE]), tile("cum", [P, NE]), tile("off", [P, NE])
        rank = tile("rank", [P, T, NE])
        sl, slot_f = tile("sl", [P, 2, T, NE]), tile("slot_f", [P, 2, T])
        be, ebf = tile("be", [P, NB, NE]), tile("ebf", [P, NB + 1])
        (ins_in, made, dve_c, logits, maxed, exped, counted, counts, zeroed, slots_at) = (m.psem(f"{nm}_{s}") for s in (
            "ins_in", "made", "dve", "logits", "maxed", "exped", "counted", "counts", "zeroed", "slots_at"))
        scattered = m.sem(f"{nm}_scattered")
        with nc.Block() as block:
            @block.sync
            def _(sp):
                sp.dma_start(rw[:, :, :], a["router_w"].rearrange("(k p) e -> p k e", p=P)).then_inc(ins_in, 16)
                sp.dma_start(rb[:, :], a["router_b"].partition_broadcast(P)).then_inc(ins_in, 16)
                sp.wait_ge(made, 1)
                with nc.allow_non_contiguous_dma(reason="a small table of slots"):
                    sp.dma_start(idx_dram.rearrange("(b p) o -> p (b o)", p=P), zeros_i[:, :]).then_inc(zeroed, 16)
                sp.wait_ge(zeroed, 16)

            @block.gpsimd
            def _(pool):
                pool.memset(zeros_i[:, :], 0).then_inc(made, 1)
                pool.memset(ones[:, :], 1.0).then_inc(made, 1)
                pool.memset(before[:, :], 1.0).then_inc(made, 1)
                pool.memset(lower[:, :, :], 1.0).then_inc(made, 1)
                for row, n, base, step in ((e_row, NE, -NE, 1), (g_row, NG, -NG, 1), (b_row, NB, 0, 1), (thr, T, 0, P)):
                    pool.iota(row[:, :], pattern=[[step, n]], base=base, channel_multiplier=0,
                              allow_small_or_imprecise_dtypes=True).then_inc(made, 1)
                pool.iota(tok_i[:, :], pattern=[[P, T]], base=0, channel_multiplier=1).then_inc(made, 1)
                pool.wait_ge(made, 9)
                pool.affine_select(out=before[:, :], in_=before[:, :], compare_op=ALU.is_gt, fill=0.0, base=0,
                                   pattern=[[1, P]], channel_multiplier=-1).then_inc(made, 1)
                pool.affine_select(out=lower[:, :, :], in_=lower[:, :, :], compare_op=ALU.is_ge, fill=0.0, base=0,
                                   pattern=[[1, NE], [-1, NE]], channel_multiplier=0).then_inc(made, 1)
                pool.wait_ge(made, 11)
                pool.wait_ge(zeroed, 16)
                pool.wait_ge(slots_at, 1)
                for c in range(2):
                    for i in range(T):
                        pool.indirect_dma_start(out=idx_dram, out_offset=bass.IndirectOffsetOnAxis(ap=slot_i[:, c * T + i:c * T + i + 1], axis=0),
                                                in_=tok_i[:, i:i + 1], in_offset=None).then_inc(scattered, 16)
                pool.wait_ge(scattered, 16 * 2 * T)

            @block.tensor
            def _(pe):
                pe.wait_ge(ins_in, 32)
                for i in range(T):
                    for k in range(KD):
                        ins = pe.matmul(m.psum[0][:, i * NE:(i + 1) * NE], hT[:, k, i * P:(i + 1) * P], rw[:, k, :],
                                        start=k == 0, stop=k == KD - 1)
                ins.then_inc(logits, 1)
                pe.wait_ge(made, 11)
                pe.wait_ge(counted, 1)
                for i in range(T):
                    for j in range(i + 1):
                        pe.matmul(m.psum[1][:, i * NE:(i + 1) * NE], before[:, :] if j == i else ones[:, :], both[:, j, :],
                                  start=j == 0, stop=j == i)
                for j in range(T):
                    ins = pe.matmul(m.psum[1][:, T * NE:(T + 1) * NE], ones[:, :], both[:, j, :], start=j == 0, stop=j == T - 1)
                ins.then_inc(counts, 1)

            @block.scalar
            def _(act):
                act.wait_ge(maxed, 1)
                act.activation(pr[:, :, :], lg[:, :, :], ACT.Exp).then_inc(exped, 1)

            @block.vector
            def _(dve):
                link = Chain(dve, dve_c).link

                def wide(x, n):
                    return x.unsqueeze(2).to_broadcast([P, T, n])

                def row(x, n):
                    return x[:, :].unsqueeze(1).to_broadcast([P, T, n])

                dve.wait_ge(ins_in, 32)
                dve.wait_ge(made, 11)
                dve.wait_ge(logits, 1)
                link(dve.tensor_tensor(lg[:, :, :], m.psum[0][:, 0:T * NE].rearrange("p (t e) -> p t e", e=NE), row(rb, NE), ALU.add))
                link(dve.tensor_reduce(mx[:, :], lg[:, :, :], AX.X, ALU.max))
                dve.tensor_tensor(lg[:, :, :], lg[:, :, :], wide(mx[:, :], NE), ALU.subtract).then_inc(maxed, 1)
                dve.wait_ge(exped, 1)
                link(dve.tensor_reduce(sm[:, :], pr[:, :, :], AX.X, ALU.add))
                link(dve.reciprocal(sm[:, :], sm[:, :]))
                link(dve.tensor_tensor(pr[:, :, :], pr[:, :, :], wide(sm[:, :], NE), ALU.mult))
                link(dve.tensor_reduce(gm[:, :, :], pr[:, :, :].rearrange("p t (g e) -> p t g e", e=EPG), AX.X, ALU.max))
                link(dve.tensor_reduce(gb[:, :], gm[:, :, :], AX.X, ALU.max))
                link(dve.tensor_tensor(ge[:, :, :], gm[:, :, :], wide(gb[:, :], NG), ALU.is_equal))
                link(dve.tensor_tensor(ge[:, :, :], ge[:, :, :], row(g_row, NG), ALU.mult))
                link(dve.tensor_reduce(gi[:, :], ge[:, :, :], AX.X, ALU.min))
                link(dve.tensor_tensor(ge[:, :, :], row(g_row, NG), wide(gi[:, :], NG), ALU.is_equal))
                for e in range(EPG):
                    ins = dve.tensor_scalar(cand[:, :, e::EPG], ge[:, :, :], 2.0, -2.0, ALU.mult, ALU.add)
                link(ins)
                link(dve.tensor_tensor(pm[:, :, :], pr[:, :, :], cand[:, :, :], ALU.add))
                for c in range(2):
                    link(dve.tensor_reduce(top[:, c, :], pm[:, :, :], AX.X, ALU.max))
                    link(dve.tensor_tensor(cand[:, :, :], pm[:, :, :], wide(top[:, c, :], NE), ALU.is_equal))
                    link(dve.tensor_tensor(cand[:, :, :], cand[:, :, :], row(e_row, NE), ALU.mult))
                    link(dve.tensor_reduce(ti[:, c, :], cand[:, :, :], AX.X, ALU.min))
                    link(dve.tensor_tensor(oh[:, c], row(e_row, NE), wide(ti[:, c, :], NE), ALU.is_equal))
                    if c == 0:
                        link(dve.scalar_tensor_tensor(out=pm[:, :, :], in0=oh[:, 0], scalar=-4.0, in1=pm[:, :, :],
                                                      op0=ALU.mult, op1=ALU.add))
                link(dve.tensor_tensor(sm[:, :], top[:, 0, :], top[:, 1, :], ALU.add))
                link(dve.reciprocal(sm[:, :], sm[:, :]))
                for c in range(2):
                    dve.tensor_tensor(wgt[:, c * T:(c + 1) * T], top[:, c, :], sm[:, :], ALU.mult)
                dve.tensor_tensor(both[:, :, :], oh[:, 0], oh[:, 1], ALU.add).then_inc(counted, 1)
                dve.wait_ge(counts, 1)
                link(dve.tensor_copy(cnt[:, :], m.psum[1][:, T * NE:(T + 1) * NE]))
                link(dve.tensor_tensor(nbx[:, :, :], cnt[:, :].unsqueeze(2).to_broadcast([P, NE, T]),
                                       thr[:, :].unsqueeze(1).to_broadcast([P, NE, T]), ALU.is_gt))
                link(dve.tensor_reduce(nb[:, :], nbx[:, :, :], AX.X, ALU.add))
                link(dve.tensor_tensor(low[:, :, :], lower[:, :, :], nb[:, :].unsqueeze(1).to_broadcast([P, NE, NE]), ALU.mult))
                link(dve.tensor_reduce(cum[:, :], low[:, :, :], AX.X, ALU.add))
                link(dve.tensor_tensor(off[:, :], cum[:, :], nb[:, :], ALU.subtract))
                link(dve.scalar_tensor_tensor(out=rank[:, :, :], in0=off[:, :].unsqueeze(1).to_broadcast([P, T, NE]), scalar=float(P),
                                              in1=m.psum[1][:, 0:T * NE].rearrange("p (t e) -> p t e", e=NE),
                                              op0=ALU.mult, op1=ALU.add))
                for c in range(2):
                    ins = dve.tensor_tensor(sl[:, c], oh[:, c], rank[:, :, :], ALU.mult)
                link(ins)
                for c in range(2):
                    ins = dve.tensor_reduce(slot_f[:, c, :], sl[:, c], AX.X, ALU.add)
                link(ins)
                dve.tensor_copy(slot_i[:, :], slot_f[:, :, :].rearrange("p c t -> p (c t)")).then_inc(slots_at, 1)
                link(dve.tensor_tensor(be[:, :, :], b_row[:, :].unsqueeze(2).to_broadcast([P, NB, NE]),
                                       cum[:, :].unsqueeze(1).to_broadcast([P, NB, NE]), ALU.is_ge))
                link(dve.tensor_reduce(ebf[:, 0:NB], be[:, :, :], AX.X, ALU.add))
                dve.tensor_scalar(ebf[:, 0:NB], ebf[:, 0:NB], float(NE - 1), None, ALU.min)
                link(dve.tensor_copy(ebf[:, NB:NB + 1], cum[:, NE - 1:NE]))
                link(dve.tensor_copy(meta[:, :], ebf[0:1, :]))


def moe_experts(m, layer, meta, h_dram, idx_dram, y_dram):
    m.phase()
    nc, a, nm = m.nc, m.a, f"e{layer}"
    NB = MAXB + 1
    CI, CO = 4, DE // P
    KC = KD // CI
    w_in = a["moe_w_in"][layer].rearrange("e d n -> (e d) n")
    w_out = a["moe_w_out"][layer].rearrange("e f n -> (e f) n")
    gate_ps, up_ps, turn_ps, act_ps, y_ps = m.psum[0], m.psum[1], m.psum[2:4], m.psum[4], m.psum[5:7]
    with ExitStack() as t:
        wi = [m.sb(t, f"{nm}_wi{q}", [P, KC, 2 * DE]) for q in range(CI)]
        wi_hi, wi_lo = ([m.sb(t, f"{nm}_wi_{s}{q}", [P, KC, 2 * DE], F32R) for q in range(CI)] for s in ("hi", "lo"))
        wo = [m.sb(t, f"{nm}_wo{f}", [P, D]) for f in range(CO)]
        ix = m.sb(t, f"{nm}_ix", [P, 1], I32)
        hx = m.sb(t, f"{nm}_hx", [P, D])
        hx_hi, hx_lo = m.split_pair(t, f"{nm}_hx", n=P)
        sg = m.sb(t, f"{nm}_silu", [P, DE])
        au = m.sb(t, f"{nm}_act", [P, DE])
        auT = m.sb(t, f"{nm}_actT", [P, CO, P])
        y = m.sb(t, f"{nm}_y", [P, D])
        wi_in, wi_his, wi_los, wi_used = ([m.psem(f"{nm}_wi_{s}{q}") for q in range(CI)] for s in ("in", "hi", "lo", "used"))
        wo_in, wo_used = ([m.psem(f"{nm}_wo_{s}{f}") for f in range(CO)] for s in ("in", "used"))
        passed = m.psem(f"{nm}_passed")
        ix_in, hx_in = m.sem(f"{nm}_ix_in"), m.sem(f"{nm}_hx_in")
        (h_turned, h_hi, h_lo, silued, multiplied, a_turned, aT_out, y_act, y_dve, stored) = (
            m.psem(f"{nm}_{s}") for s in ("h_turned", "h_hi", "h_lo", "silued", "multiplied",
                                          "a_turned", "aT_out", "y_act", "y_dve", "stored"))

        def blocks(engine):
            return engine.value_load(meta[0:1, NB:NB + 1], min_val=1, max_val=MAXB)

        with nc.Block() as block:
            @block.sync
            def _(sp):
                def expert(b):
                    return sp.value_load(meta[0:1, bass.ds(b, 1)], min_val=0, max_val=NE - 1)

                def load_in(e, q):
                    sp.dma_start(wi[q][:, :, :], w_in[bass.ds(e * D + q * KC * P, KC * P), :]
                                 .rearrange("(k p) n -> p k n", p=P)).then_inc(wi_in[q], 16)

                def load_out(e, b):
                    for f in range(CO):
                        sp.wait_ge(wo_used[f], b + 1)
                        sp.dma_start(wo[f][:, :], w_out[bass.ds(e * DE + f * P, P), :]).then_inc(wo_in[f], 16)

                e0 = expert(0)
                for q in range(CI):
                    load_in(e0, q)
                last = blocks(sp) - 1
                with sp.Fori(0, last) as b:
                    e1 = expert(b + 1)
                    for q in range(CI):
                        sp.wait_ge(wi_los[q], b + 1)
                        load_in(e1, q)
                    load_out(expert(b), b)
                load_out(expert(last), last)

            @block.gpsimd
            def _(pool):
                nb = blocks(pool)
                with pool.Fori(0, nb + 1) as b:
                    pool.wait_ge(h_turned, b + 1)
                    pool.dma_start(ix[:, :], idx_dram[bass.ds(b * P, P), :]).then_inc(ix_in, 16)
                    pool.wait_ge(ix_in, b * 16 + 16)
                    pool.sem_inc(passed, 1)
                    pool.indirect_dma_start(out=hx[:, :], out_offset=None, in_=h_dram,
                                            in_offset=bass.IndirectOffsetOnAxis(ap=ix[:, 0:1], axis=0)).then_inc(hx_in, 16)
                pool.wait_ge(h_turned, nb + 2)
                pool.sem_inc(passed, 1)

            @block.tensor
            def _(pe):
                def turn_tokens(b):
                    pe.wait_ge(hx_in, b * 16 + 16)
                    for k in range(KD):
                        ins = pe.transpose(turn_ps[k // 4][:, (k % 4) * P:(k % 4 + 1) * P], hx[:, k * P:(k + 1) * P], m.ident[:, :])
                    ins.then_inc(h_turned, 1)

                for free in wo_used + [h_turned]:
                    pe.sem_inc(free, 1)
                turn_tokens(0)
                with pe.Fori(0, blocks(pe)) as b:
                    pe.wait_ge(h_lo, b + 1)
                    for q in range(CI):
                        pe.wait_ge(wi_los[q], b + 1)
                        for kk in range(KC):
                            k = q * KC + kk
                            for term, (x, w) in enumerate(((hx_hi, wi_hi), (hx_hi, wi_lo), (hx_lo, wi_hi))):
                                start, stop = k == 0 and term == 0, k == KD - 1 and term == 2
                                pe.matmul(gate_ps[:, 0:DE], x[:, k, :], w[q][:, kk, 0:DE], start=start, stop=stop)
                                ins = pe.matmul(up_ps[:, 0:DE], x[:, k, :], w[q][:, kk, DE:2 * DE], start=start, stop=stop)
                        ins.then_inc(wi_used[q], 1)
                    turn_tokens(b + 1)
                    pe.wait_ge(multiplied, b + 1)
                    for f in range(CO):
                        ins = pe.transpose(act_ps[:, f * P:(f + 1) * P], au[:, f * P:(f + 1) * P], m.ident[:, :])
                    ins.then_inc(a_turned, 1)
                    pe.wait_ge(aT_out, b + 1)
                    pe.wait_ge(y_act, b + 1)
                    pe.wait_ge(y_dve, b + 1)
                    for f in range(CO):
                        pe.wait_ge(wo_in[f], b * 16 + 16)
                        for n in range(2):
                            ins = pe.matmul(y_ps[n][:, :], auT[:, f, :], wo[f][:, n * GC:(n + 1) * GC], start=f == 0, stop=f == CO - 1)
                        ins.then_inc(wo_used[f], 1)

            @block.scalar
            def _(act):
                def keep_tokens(b):
                    act.wait_ge(h_turned, b + 2)
                    for j in range(2):
                        ins = act.activation(hx_hi[:, 4 * j:4 * j + 4, :], turn_ps[j][:, :].rearrange("p (k t) -> p k t", k=4), ACT.Copy)
                    ins.then_inc(h_hi, 1)

                def split_in(b, q):
                    act.wait_ge(wi_in[q], b * 16 + 16)
                    act.activation(wi_hi[q][:, :, :], wi[q][:, :, :], ACT.Copy).then_inc(wi_his[q], 1)

                def run_block(b, more):
                    if more:
                        for q in range(CI - 1):
                            act.wait_ge(wi_used[q], b + 1)
                            split_in(b + 1, q)
                    act.wait_ge(wi_used[CI - 1], b + 1)
                    act.activation(sg[:, :], gate_ps[:, 0:DE], ACT.Silu).then_inc(silued, 1)
                    keep_tokens(b + 1)
                    act.wait_ge(a_turned, b + 1)
                    act.activation(auT[:, :, :], act_ps[:, 0:DE].rearrange("p (f t) -> p f t", f=CO), ACT.Copy).then_inc(aT_out, 1)
                    if more:
                        split_in(b + 1, CI - 1)
                    act.wait_ge(wo_used[CO - 1], b + 2)
                    act.wait_ge(stored, b * 16 + 16)
                    act.activation(y[:, 0:GC], y_ps[0][:, :], ACT.Copy).then_inc(y_act, 1)
                    act.wait_ge(y_act, b + 2)
                    act.wait_ge(y_dve, b + 2)
                    act.dma_start(y_dram[bass.ds(b * P, P), :], y[:, :]).then_inc(stored, 16)

                act.sem_inc(y_act, 1)
                act.sem_inc(stored, 16)
                keep_tokens(0)
                for q in range(CI):
                    split_in(0, q)
                last = blocks(act) - 1
                with act.Fori(0, last) as b:
                    run_block(b, more=True)
                run_block(last, more=False)
                act.wait_ge(stored, last * 16 + 32)
                act.sem_inc(passed, 1)

            @block.vector
            def _(dve):
                def keep_tokens(b):
                    dve.wait_ge(h_hi, b + 1)
                    for j in range(2):
                        ins = dve.tensor_tensor(hx_lo[:, 4 * j:4 * j + 4, :], turn_ps[j][:, :].rearrange("p (k t) -> p k t", k=4),
                                                hx_hi[:, 4 * j:4 * j + 4, :], ALU.subtract)
                    ins.then_inc(h_lo, 1)

                def split_in(b, q):
                    dve.wait_ge(wi_his[q], b + 1)
                    dve.tensor_tensor(wi_lo[q][:, :, :], wi[q][:, :, :], wi_hi[q][:, :, :], ALU.subtract).then_inc(wi_los[q], 1)

                def run_block(b, more):
                    if more:
                        for q in range(CI // 2):
                            split_in(b + 1, q)
                    dve.wait_ge(silued, b + 1)
                    dve.tensor_tensor(au[:, :], up_ps[:, 0:DE], sg[:, :], ALU.mult).then_inc(multiplied, 1)
                    keep_tokens(b + 1)
                    if more:
                        for q in range(CI // 2, CI):
                            split_in(b + 1, q)
                    dve.wait_ge(wo_used[CO - 1], b + 2)
                    dve.wait_ge(stored, b * 16 + 16)
                    dve.tensor_copy(y[:, GC:D], y_ps[1][:, :]).then_inc(y_dve, 1)

                dve.sem_inc(y_dve, 1)
                keep_tokens(0)
                for q in range(CI):
                    split_in(0, q)
                last = blocks(dve) - 1
                with dve.Fori(0, last) as b:
                    run_block(b, more=True)
                run_block(last, more=False)


def moe_combine(m, layer, slot_i, wgt, y_dram):
    m.phase()
    nc = m.nc
    with ExitStack() as t:
        yg = m.sb(t, f"c{layer}_y", [P, 2 * T, D])
        got = [m.sem(f"c{layer}_got{j}") for j in range(2 * T)]
        added = m.psem(f"c{layer}_added")
        order = [c * T + i for i in range(T) for c in range(2)]
        with nc.Block() as block:
            @block.gpsimd
            def _(pool):
                for j in order:
                    pool.indirect_dma_start(out=yg[:, j, :], out_offset=None, in_=y_dram,
                                            in_offset=bass.IndirectOffsetOnAxis(ap=slot_i[:, j:j + 1], axis=0)).then_inc(got[j], 16)

            @block.vector
            def _(dve):
                for n, j in enumerate(order):
                    dve.wait_ge(got[j], 16)
                    if n:
                        dve.wait_ge(added, n)
                    dve.scalar_tensor_tensor(out=m.x[:, j % T, :], in0=yg[:, j, :], scalar=wgt[:, j:j + 1],
                                             in1=m.x[:, j % T, :], op0=ALU.mult, op1=ALU.add).then_inc(added, 1)


def moe(m, layer):
    nm = f"moe{layer}"
    h_dram = m.nc.dram_tensor(f"{nm}_h", [S, D], F32).ap()
    idx_dram = m.nc.dram_tensor(f"{nm}_idx", [SLOTS, 1], I32).ap()
    y_dram = m.y_dram
    with ExitStack() as c:
        slot_i = m.sb(c, f"{nm}_slot", [P, 2 * T], I32)
        wgt = m.sb(c, f"{nm}_wgt", [P, 2 * T])
        meta = m.sb(c, f"{nm}_meta", [1, MAXB + 2], I32)
        with ExitStack() as c2:
            hT = m.sb(c2, f"{nm}_hT", [P, KD, S])
            norm_transpose(m, nm, m.x, m.a["norm_ffn"][layer], T, None, None, plain=hT, h_dram=h_dram)
            moe_route(m, layer, hT, slot_i, wgt, meta, idx_dram)
        moe_experts(m, layer, meta, h_dram, idx_dram, y_dram)
        moe_combine(m, layer, slot_i, wgt, y_dram)


def build_trunk(nc, a, out, parts="all"):
    with ExitStack() as ctx:
        m = Core(nc, ctx, a)
        two = [(0, GC), (GC, 2 * GC)]
        four = [(n * GC, (n + 1) * GC) for n in range(4)]
        eight = [(n * GC, (n + 1) * GC) for n in range(8)]
        at = {}

        def add(name, w, cols):
            at[name] = len(m.groups)
            m.add_linear(w, cols)

        if parts in ("all", "hyb"):
            add("hyb", a["hyb_w_in"][0], [(O_QA, O_KC), (O_KS, O_GA), (O_KC, O_KS), (O_QB, O_VB), (O_VB, O_AL),
                                          (O_R, O_END), (O_GA, O_QB), (O_AL, O_R)])
            add("hyb_out", a["hyb_w_out"][0], two)
        for layer in range(DEPTH):
            if layer == 1 and parts in ("all", "sgu"):
                add("sgu", a["sg_w_in"][0], eight)
                add("sgu_out", a["sg_w_out"][0], two)
            if parts == "all" or parts == f"x{layer}":
                add(f"x{layer}", a["x_wkv"][layer], four)
                add(f"xq{layer}", a["x_wq"][layer], two)
                add(f"xo{layer}", a["x_wo"][layer], two)
        setup(m)
        if parts not in ("all", "hyb"):
            m.phase()
            z = m.sb(ctx, "ztest", [P, D]); zs = m.psem("ztest")
            with nc.Block() as block:
                @block.gpsimd
                def _(pool):
                    pool.memset(z[:, :], 0.0).then_inc(zs, 1)
                @block.sync
                def _(sp):
                    sp.wait_ge(zs, 1)
                    m.clear_outputs(sp, z[:, :])
        for layer in range(DEPTH):
            if layer == 0 and "hyb" in at:
                hybrid_layer(m, at["hyb"])
            elif layer == 1 and "sgu" in at:
                sgu_layer(m, layer, at["sgu"])
            if f"x{layer}" in at:
                cross_attention(m, layer, at[f"x{layer}"])
            if parts == "all" or parts == f"moe{layer}":
                moe(m, layer)
        store_x(m, out)


_INS = ["x", "mem", "positions", "norm_mix", "norm_xattn", "norm_mem", "norm_ffn", "hyb_w_in", "hyb_w_out",
        "nsa_qnorm", "nsa_knorm", "nsa_cmp_pe", "nsa_cmp_w1", "nsa_cmp_w2", "nsa_gate_b", "gla_wa2", "gla_ba",
        "gla_onorm", "sg_w_in", "sg_ln_g", "sg_ln_b", "sg_ws", "sg_bs", "sg_w_out", "x_wq", "x_wkv", "x_wo",
        "x_qnorm", "x_knorm", "router_w", "router_b", "moe_w_in", "moe_w_out"]


def kernel(**inputs):
    import concourse.bacc as _bacc
    from concourse.bass_utils import run_bass_kernel_spmd as _run

    nc = _bacc.Bacc("TRN2", target_bir_lowering=False, num_devices=1)
    arrays, args = {}, {}
    for name in _INS:
        arrays[f"in_{name}"] = np.ascontiguousarray(inputs[name])
        args[name] = nc.dram_tensor(f"in_{name}", arrays[f"in_{name}"].shape,
                                    mybir.dt.from_np(arrays[f"in_{name}"].dtype), kind="ExternalInput").ap()
    half = HD // 2
    arrays["rope_freq"] = (np.float32(10000.0) ** (-np.arange(half, dtype=np.float32) / half)).astype(np.float32)
    args["rope_freq"] = nc.dram_tensor("rope_freq", (half,), F32, kind="ExternalInput").ap()
    out = nc.dram_tensor("out_x", (1, S, D), F32, kind="ExternalOutput").ap()
    build_trunk(nc, args, out)
    r = _run(nc, [arrays], core_ids=[0])
    return r.results[0]["out_x"]
```

```python
from contextlib import ExitStack

import numpy as np
import concourse.bass as bass
from concourse import mybir

F32 = mybir.dt.float32
F32R = mybir.dt.float32r
I32 = mybir.dt.int32
ACT = mybir.ActivationFunctionType
ALU = mybir.AluOpType
AX = mybir.AxisListType

P = 128
D = 1024
S = 512
T = S // P
KD = D // P
DEPTH = 2
N_MEM = 256
MT = N_MEM // P
EPS = 1e-6
NEG = -1e30
GC = 512
KH = 4

HEADS, KVH, HD = 8, 2, 64
HPG = HEADS // KVH
CMP_LEN, CMP_STRIDE = 32, 16
N_CMP = (S - CMP_LEN) // CMP_STRIDE + 1
CP = 32
WINDOW = 256
WT = WINDOW // P

GH, GDK, GDV, GRANK, GTAU, GCH = 4, 64, 128, 16, 16.0, 64
SUB = 16
NSUB = GCH // SUB
NCH = S // GCH

SGW = 2 * D
SGG = 8
XH, XHD = 4, 256
NE, NG, EPG, DE = 16, 4, 4, 384
MAXB = (2 * S) // P + NE - 1
SLOTS = (MAXB + 1) * P

SIZES = (512, 128, 128, 128, 128, 128, 128, 24, 256, 256, 512, 16, 512)
OFF = [0]
for _s in SIZES:
    OFF.append(OFF[-1] + _s)
(O_QA, O_KC, O_VC, O_KS, O_VS, O_KW, O_VW, O_GA, O_QB, O_KB, O_VB, O_AL, O_R, O_END) = OFF


AL_AT = 32
PHASE_SEMS = 48

class Chain:

    def __init__(self, engine, sem):
        self.engine, self.sem, self.n = engine, sem, 0

    def link(self, ins):
        self.n += 1
        ins.then_inc(self.sem, 1)
        self.engine.wait_ge(self.sem, self.n)


class Core:

    def __init__(self, nc, ctx, a):
        self.nc, self.ctx, self.a = nc, ctx, a
        self.turn, self.taken = 0, 0
        self.banks = [[self.sem(f"phase{b}_{i}") for i in range(PHASE_SEMS)] for b in range(2)]
        sb, sem = self.sb, self.sem
        self.x = sb(ctx, "x_res", [P, T, D])
        self.ident = sb(ctx, "ident", [P, P])
        self.stage = [sb(ctx, f"w_stage{h}", [P, KH, GC]) for h in range(2)]
        self.w_hi = [sb(ctx, f"w_hi{h}", [P, KH, GC], F32R) for h in range(2)]
        self.w_lo = [sb(ctx, f"w_lo{h}", [P, KH, GC], F32R) for h in range(2)]
        self.psum = [ctx.enter_context(nc.psum_tensor(f"bank{b}", [P, GC], F32)) for b in range(8)]
        self.landed = [sem(f"w_landed{h}") for h in range(2)]
        self.hi_done = [sem(f"w_hi_done{h}") for h in range(2)]
        self.lo_done = [sem(f"w_lo_done{h}") for h in range(2)]
        self.used = [sem(f"w_used{h}") for h in range(2)]
        self.y_dram = nc.dram_tensor("moe_y", [SLOTS, D], F32).ap()
        self.cleared = sem("y_cleared")
        self.groups = []
        self.pieces = [0]
        self.asked, self.n_hi, self.n_lo = 0, 0, 0

    def sb(self, ctx, name, shape, dt=F32):
        return ctx.enter_context(self.nc.sbuf_tensor(name, shape, dt))

    def split_pair(self, ctx, name, k=KD, n=S):
        return (self.sb(ctx, f"{name}_hi", [P, k, n], F32R), self.sb(ctx, f"{name}_lo", [P, k, n], F32R))

    def clear_outputs(self, sp, zeros):
        for b in range(2 * S // P, SLOTS // P):
            sp.dma_start(self.y_dram[b * P:(b + 1) * P, :], zeros).then_inc(self.cleared, 16)
        sp.wait_ge(self.cleared, 16 * (SLOTS // P - 2 * S // P))

    def sem(self, name):
        return self.ctx.enter_context(self.nc.semaphore(name))

    def phase(self):
        self.turn += 1
        self.taken = 0
        if self.turn > 1:
            last = self.banks[self.turn % 2]
            self.nc.gpsimd.sem_clear(range(last[0].num, last[-1].num + 1))

    def psem(self, name):
        s = self.banks[(self.turn + 1) % 2][self.taken]
        self.taken += 1
        return s

    def add_group(self, w, ranges):
        halves = [[], []]
        at = 0
        for c0, c1 in ranges:
            for h in range(2):
                halves[h].append((at, w[h * KH * P:(h + 1) * KH * P, c0:c1].rearrange("(k p) n -> p k n", p=P)))
            at += c1 - c0
        self.groups.append((halves, at))
        self.pieces.append(self.pieces[-1] + len(ranges))

    def add_linear(self, w, cols):
        for c in cols:
            for k0 in range(0, w.shape[0], 2 * KH * P):
                self.add_group(w[k0:k0 + 2 * KH * P, :], [c])

    def load(self, sp, upto):
        while self.asked < min(upto, len(self.groups)):
            n = self.asked
            for h in range(2):
                if n:
                    sp.wait_ge(self.lo_done[h], n)
                for c0, src in self.groups[n][0][h]:
                    sp.dma_start(self.stage[h][:, :, c0:c0 + src.shape[2]], src).then_inc(self.landed[h], 16)
            self.asked += 1

    def split_hi(self, act, n):
        if n < self.n_hi:
            return
        self.n_hi = n + 1
        cols = self.groups[n][1]
        for h in range(2):
            act.wait_ge(self.landed[h], 16 * self.pieces[n + 1])
            if n:
                act.wait_ge(self.used[h], n)
            act.activation(self.w_hi[h][:, :, :cols], self.stage[h][:, :, :cols], ACT.Copy)\
               .then_inc(self.hi_done[h], 1)

    def split_lo(self, dve, n):
        if n < self.n_lo:
            return
        self.n_lo = n + 1
        cols = self.groups[n][1]
        for h in range(2):
            dve.wait_ge(self.hi_done[h], n + 1)
            dve.tensor_tensor(self.w_lo[h][:, :, :cols], self.stage[h][:, :, :cols],
                              self.w_hi[h][:, :, :cols], ALU.subtract).then_inc(self.lo_done[h], 1)

    def split_next_hi(self, act):
        if self.n_hi < self.asked:
            self.split_hi(act, self.n_hi)

    def split_next_lo(self, dve):
        if self.n_lo < self.asked:
            self.split_lo(dve, self.n_lo)

    def product(self, pe, n, feature_major, banks, hi, lo, tiles=T, first=True, last=True, k0=0):
        cols = self.groups[n][1]
        for h in range(2):
            pe.wait_ge(self.lo_done[h], n + 1)
            for b in range(-(-cols // P) if feature_major else tiles):
                for kk in range(KH):
                    k = k0 + KH * h + kk
                    for term, (x_part, w_part) in enumerate(((hi, self.w_hi[h]), (hi, self.w_lo[h]), (lo, self.w_hi[h]))):
                        start = first and h == 0 and kk == 0 and term == 0
                        stop = last and h == 1 and kk == KH - 1 and term == 2
                        if feature_major:
                            w_cols = slice(b * P, min(cols, (b + 1) * P))
                            ins = pe.matmul(banks[b][:w_cols.stop - w_cols.start, :tiles * P], w_part[:, kk, w_cols],
                                            x_part[:, k, :tiles * P], start=start, stop=stop)
                        else:
                            ins = pe.matmul(banks[b][:, :cols], x_part[:, k, b * P:(b + 1) * P],
                                            w_part[:, kk, :cols], start=start, stop=stop)
            ins.then_inc(self.used[h], 1)

    def done(self, engine, n):
        engine.wait_ge(self.used[1], n + 1)


def setup(m):
    m.phase()
    nc, ctx = m.nc, m.ctx
    made = m.psem("consts_made")
    m.causal = m.sb(ctx, "causal_neg", [P, P])
    m.beyond = m.sb(ctx, "beyond_neg", [P, P])
    with nc.Block() as block:
        @block.gpsimd
        def _(pool):
            pool.memset(m.ident[:, :], 0.0).then_inc(made, 1)
            pool.memset(m.causal[:, :], 0.0).then_inc(made, 1)
            pool.memset(m.beyond[:, :], 0.0).then_inc(made, 1)
            pool.wait_ge(made, 3)
            pool.affine_select(out=m.ident[:, :], in_=m.ident[:, :], compare_op=ALU.not_equal, fill=1.0,
                               base=0, pattern=[[-1, P]], channel_multiplier=1).then_inc(made, 1)
            pool.affine_select(out=m.causal[:, :], in_=m.causal[:, :], compare_op=ALU.is_ge, fill=NEG,
                               base=0, pattern=[[-1, P]], channel_multiplier=1).then_inc(made, 1)
            pool.affine_select(out=m.beyond[:, :], in_=m.beyond[:, :], compare_op=ALU.is_gt, fill=NEG,
                               base=0, pattern=[[1, P]], channel_multiplier=-1).then_inc(made, 1)
            pool.wait_ge(made, 6)


def norm_transpose(m, name, src, gain, tiles, hi, lo, plain=None, h_dram=None, source=None):
    m.phase()
    nc = m.nc
    loaded = [m.psem(f"{name}_loaded{t}") for t in range(tiles)]
    with ExitStack() as c:
        xn = m.sb(c, f"{name}_xn", [P, tiles, D])
        g = m.sb(c, f"{name}_gain", [P, KD])
        junk = m.sb(c, f"{name}_sq", [P, 2, D])
        ms = m.sb(c, f"{name}_ms", [P, tiles])
        root = m.sb(c, f"{name}_root", [P, tiles])
        rstd = m.sb(c, f"{name}_rstd", [P, tiles])
        gain_in, squared, mean, rooted, normed, turned, hi_out, lo_out, dve_c, stored = (
            m.psem(f"{name}_{s}") for s in ("gain_in", "squared", "mean", "rooted", "normed", "turned",
                                           "hi_out", "lo_out", "dve", "stored"))
        gb = m.sb(c, f"{name}_gain_row", [P, D]) if plain is not None else None
        with nc.Block() as block:
            @block.sync
            def _(sp):
                if source is not None:
                    for t in range(tiles):
                        sp.dma_start(src[:, t, :], source[t * P:(t + 1) * P, :]).then_inc(loaded[t], 16)
                    m.load(sp, 1)
                if plain is None:
                    with nc.allow_non_contiguous_dma(reason="one gain per partition"):
                        sp.dma_start(g[:, :], gain.rearrange("(k p) -> p k", p=P)).then_inc(gain_in, 16)
                else:
                    sp.dma_start(gb[:, :], gain.partition_broadcast(P)).then_inc(gain_in, 16)
                    for t in range(tiles):
                        sp.wait_ge(normed, t + 1)
                        sp.dma_start(h_dram[t * P:(t + 1) * P, :], xn[:, t, :]).then_inc(stored, 16)
                    sp.wait_ge(stored, 16 * tiles)

            @block.scalar
            def _(act):
                def take_root(t):
                    act.wait_ge(mean, t + 1)
                    act.activation(root[:, t:t + 1], ms[:, t:t + 1], ACT.Sqrt).then_inc(rooted, 1)

                for t in range(tiles):
                    if source is not None:
                        act.wait_ge(loaded[t], 16)
                    act.activation(junk[:, t % 2], src[:, t, :], ACT.Square, accum_out=ms[:, t:t + 1])\
                       .then_inc(squared, 1)
                    if t:
                        take_root(t - 1)
                take_root(tiles - 1)
                if plain is None:
                    m.split_next_hi(act)
                if plain is None:
                    act.wait_ge(gain_in, 16)
                for k in range(KD):
                    act.wait_ge(turned, k + 1)
                    if plain is None:
                        act.activation(hi[:, k, :tiles * P], m.psum[k][:, :tiles * P], ACT.Copy,
                                       scale=g[:, k:k + 1]).then_inc(hi_out, 1)
                    elif k % 2 == 0:
                        act.activation(plain[:, k, :tiles * P], m.psum[k][:, :tiles * P], ACT.Copy).then_inc(hi_out, 1)

            @block.vector
            def _(dve):
                link = Chain(dve, dve_c).link
                def normalize(t):
                    if source is not None:
                        dve.wait_ge(loaded[t], 16)
                    dve.wait_ge(rooted, t + 1)
                    link(dve.reciprocal(rstd[:, t:t + 1], root[:, t:t + 1]))
                    if plain is None:
                        dve.tensor_scalar(xn[:, t, :], src[:, t, :], rstd[:, t:t + 1], None, ALU.mult).then_inc(normed, 1)
                    else:
                        if t == 0:
                            dve.wait_ge(gain_in, 16)
                        dve.scalar_tensor_tensor(out=xn[:, t, :], in0=src[:, t, :], scalar=rstd[:, t:t + 1],
                                                 in1=gb[:, :], op0=ALU.mult, op1=ALU.mult).then_inc(normed, 1)

                for t in range(tiles):
                    dve.wait_ge(squared, t + 1)
                    dve.tensor_scalar(ms[:, t:t + 1], ms[:, t:t + 1], 1.0 / D, EPS, ALU.mult, ALU.add).then_inc(mean, 1)
                    if t:
                        normalize(t - 1)
                normalize(tiles - 1)
                if plain is None:
                    m.split_next_lo(dve)
                    dve.wait_ge(gain_in, 16)
                if plain is None:
                    for k in range(KD):
                        dve.wait_ge(hi_out, k + 1)
                        dve.scalar_tensor_tensor(out=lo[:, k, :tiles * P], in0=m.psum[k][:, :tiles * P],
                                                 scalar=g[:, k:k + 1], in1=hi[:, k, :tiles * P],
                                                 op0=ALU.mult, op1=ALU.subtract).then_inc(lo_out, 1)
                else:
                    for k in range(1, KD, 2):
                        dve.wait_ge(turned, k + 1)
                        dve.tensor_copy(plain[:, k, :tiles * P], m.psum[k][:, :tiles * P]).then_inc(lo_out, 1)

            @block.tensor
            def _(pe):
                for t in range(tiles):
                    pe.wait_ge(normed, t + 1)
                    for k in range(KD):
                        ins = pe.transpose(m.psum[k][:, t * P:(t + 1) * P], xn[:, t, k * P:(k + 1) * P], m.ident[:, :])
                        if t == tiles - 1:
                            ins.then_inc(turned, 1)


def store_x(m, out):
    m.phase()
    stored = m.psem("x_stored")
    with m.nc.Block() as block:
        @block.sync
        def _(sp):
            for t in range(T):
                sp.dma_start(out[0, t * P:(t + 1) * P, :], m.x[:, t, :]).then_inc(stored, 16)
            sp.wait_ge(stored, 16 * T)


def projection_outputs(m, c):
    qk = m.sb(c, "qk", [P, T, HEADS + 2 * KVH, HD])
    v_sw = m.sb(c, "v_sw", [P, T, 2, KVH * HD])
    kvc = m.sb(c, "kvc", [P, 2, S])
    gqk = m.sb(c, "gla_qk", [P, 4, S])
    gv = m.sb(c, "gla_v", [P, T, GH * GDV])
    gr = m.sb(c, "gla_r", [P, T, GH * GDV])
    gaT = m.sb(c, "gatesT", [3 * HEADS, S])
    alT = m.sb(c, "a_lowT", [GRANK + 1, S])
    return qk, v_sw, kvc, gqk, gv, gr, gaT, alT


def hybrid_projection(m, outputs, first, hi, lo):
    m.phase()
    nc = m.nc
    qk, v_sw, kvc, gqk, gv, gr, gaT, alT = outputs
    out_act, out_dve, ones = m.psem("proj_out_act"), m.psem("proj_out_dve"), m.psem("proj_ones")
    kinds = [(False, 4), (False, 4), (True, 2), (True, 4), (False, 4), (False, 4), (True, 0)]

    def bank(j, b):
        return m.psum[4 * (j % 2) + b]

    with nc.Block() as block:
        @block.sync
        def _(sp):
            m.load(sp, first + len(kinds) + 1)

        @block.tensor
        def _(pe):
            for j, (fm, _) in enumerate(kinds):
                if j >= 2:
                    pe.wait_ge(out_act, sum(k[1] // 2 for k in kinds[:j - 1]))
                    pe.wait_ge(out_dve, sum(k[1] // 2 for k in kinds[:j - 1]))
                m.product(pe, first + j, fm, [bank(j, b) for b in range(4)], hi, lo)

        def read_out(engine, copy, j, b):
            ps = bank(j, b)
            if j == 0:
                copy(qk[:, b, 0:HEADS, :].rearrange("p (i g) d -> p g i d", g=KVH),
                     ps[:, :].rearrange("p (g i d) -> p g i d", g=KVH, d=HD)).then_inc(engine, 1)
            elif j == 1:
                parts = ps[:, :].rearrange("p (w kv c) -> p w kv c", w=2, kv=2)
                copy(qk[:, b, HEADS:, :].rearrange("p (w g) d -> p w (g d)", w=2), parts[:, :, 0, :])
                copy(v_sw[:, b, :, :], parts[:, :, 1, :]).then_inc(engine, 1)
            elif j == 2:
                copy(kvc[:, b, :], ps[:, :]).then_inc(engine, 1)
            elif j == 3:
                copy(gqk[:, b, :], ps[:, :], GDK ** -0.5 if b < 2 else 1.0).then_inc(engine, 1)
            elif j == 4:
                copy(gv[:, b, :], ps[:, :]).then_inc(engine, 1)
            else:
                copy(gr[:, b, :], ps[:, :]).then_inc(engine, 1)

        @block.scalar
        def _(act):
            def copy(out, ps, scale=1.0):
                return act.activation(out, ps, ACT.Copy, scale=scale)
            m.split_hi(act, first)
            for j, (_, n_banks) in enumerate(kinds):
                if j + 1 < len(kinds):
                    m.split_hi(act, first + j + 1)
                m.done(act, first + j)
                for b in range(0, n_banks, 2):
                    read_out(out_act, copy, j, b)
            copy(gaT[:, :], bank(len(kinds) - 1, 0)[0:3 * HEADS, :])
            act.wait_ge(ones, 1)
            copy(alT[0:GRANK, :], bank(len(kinds) - 1, 0)[AL_AT:AL_AT + GRANK, :])

        @block.gpsimd
        def _(pool):
            pool.memset(alT[:, :], 1.0).then_inc(ones, 1)

        @block.vector
        def _(dve):
            def copy(out, ps, scale=1.0):
                return dve.tensor_scalar(out, ps, scale, None, ALU.mult)
            m.split_lo(dve, first)
            for j, (_, n_banks) in enumerate(kinds):
                if j + 1 < len(kinds):
                    m.split_lo(dve, first + j + 1)
                m.done(dve, first + j)
                for b in range(1, n_banks, 2):
                    read_out(out_dve, copy, j, b)


def nsa_prepare(m, c, qk, kvc):
    m.phase()
    nc, a = m.nc, m.a
    NP6 = (HEADS + 2 * KVH) // 2
    QH = HEADS + 2 * KVH
    HF = HD // 2
    MAGIC = 1.5 * 2 ** 23
    TWO_PI = 2 * np.pi
    C1 = 6.28125
    C2 = float(np.float32(np.round((TWO_PI - C1) * 2 ** 22) / 2 ** 22))
    C3 = float(TWO_PI - C1 - C2)

    qkT = m.sb(c, "qkT", [P, NP6, S])
    kcT = m.sb(c, "kcT", [P, CP])
    vbd = m.sb(c, "vc_diag", [P, KVH, HPG, HD])
    with ExitStack() as t:
        pos_i = m.sb(t, "pos_i", [P, T + 1], I32)
        pos = m.sb(t, "pos", [P, T + 1])
        freq = m.sb(t, "freq", [P, HF])
        ang = m.sb(t, "ang", [P, T + 1, HF])
        turns = m.sb(t, "turns", [P, T + 1, HF])
        sin = m.sb(t, "sin", [P, T + 1, HF])
        cos = m.sb(t, "cos", [P, T + 1, HF])
        gains = m.sb(t, "head_gains", [P, QH, HD])
        kc_gain = m.sb(t, "kc_gain", [P, HD])
        sq = m.sb(t, "head_sq", [P, QH * HD])
        rot = m.sb(t, "head_rot", [P, QH, HD])
        tmp = m.sb(t, "head_tmp", [P, 2, QH, HF])
        ss = m.sb(t, "head_ss", [P, T * QH])
        root = m.sb(t, "head_root", [P, T * QH])
        w1 = m.sb(t, "cmp_w1", [P, 2, CMP_LEN, P])
        w2 = m.sb(t, "cmp_w2", [P, 2, P])
        pe_t = m.sb(t, "cmp_pe", [P, 2, CMP_LEN])
        blk = m.sb(t, "cmp_blocks", [P, CMP_LEN, CP])
        act1 = m.sb(t, "cmp_act", [P, 2, CP])
        kc = m.sb(t, "kc", [CP, KVH, HD])
        kc_sq = m.sb(t, "kc_sq", [CP, KVH, HD])
        kc_n = m.sb(t, "kc_n", [CP, KVH, HD])
        kc_r = m.sb(t, "kc_r", [CP, KVH, HD])
        kc_ss = m.sb(t, "kc_ss", [CP, KVH])
        kc_tmp = m.sb(t, "kc_tmp", [CP, 2, KVH, HF])
        vc = m.sb(t, "vc", [CP, KVH * HD])
        (small_in, w_in, zeroed, dve_c, act_c, angles, sines, sqr, means, roots, heads_done, turned, kept,
         blocks, hidden, gelued, out2, kc_mean, kc_root, kc_done, kc_turned, v_here, v_spread) = (
            m.psem(f"prep_{s}") for s in (
                "small_in", "w_in", "zeroed", "dve", "act", "angles", "sines", "sqr", "means", "roots",
                "heads_done", "turned", "kept", "blocks", "hidden", "gelued", "out2", "kc_mean",
                "kc_root", "kc_done", "kc_turned", "v_here", "v_spread"))

        def rotate(dve, link, out, xin, cs, sn, tmp2, n):
            x1, x2 = xin[:, :, 0:HF], xin[:, :, HF:HD]
            p = xin.shape[0]
            cb = cs.unsqueeze(1).to_broadcast([p, n, HF])
            sb = sn.unsqueeze(1).to_broadcast([p, n, HF])
            dve.tensor_tensor(tmp2[:, 0], x2, sb, ALU.mult)
            dve.tensor_tensor(tmp2[:, 1], x1, sb, ALU.mult)
            dve.tensor_tensor(out[:, :, 0:HF], x1, cb, ALU.mult)
            link(dve.tensor_tensor(out[:, :, HF:HD], x2, cb, ALU.mult))
            dve.tensor_tensor(out[:, :, 0:HF], out[:, :, 0:HF], tmp2[:, 0], ALU.subtract)
            return dve.tensor_tensor(out[:, :, HF:HD], out[:, :, HF:HD], tmp2[:, 1], ALU.add)

        with nc.Block() as block:
            @block.sync
            def _(sp):
                with nc.allow_non_contiguous_dma(reason="small tables, one element per partition"):
                    sp.dma_start(pos_i[:, 0:T], a["positions"][0].rearrange("(t p) -> p t", p=P)).then_inc(small_in, 16)
                    sp.wait_ge(angles, 1)
                    sp.dma_start(pos_i[0:N_CMP, T:T + 1],
                                 a["positions"][0:1, CMP_LEN - 1:CMP_LEN - 1 + CMP_STRIDE * (N_CMP - 1) + 1:CMP_STRIDE]
                                 .rearrange("a c -> c a")).then_inc(small_in, 16)
                    sp.dma_start(freq[:, :], a["rope_freq"].partition_broadcast(P)).then_inc(small_in, 16)
                    for g0, n, src in ((0, HEADS, a["nsa_qnorm"][0]), (HEADS, KVH, a["nsa_knorm"][0, 1]),
                                       (HEADS + KVH, KVH, a["nsa_knorm"][0, 2])):
                        for i in range(n):
                            sp.dma_start(gains[:, g0 + i, :], src.partition_broadcast(P)).then_inc(small_in, 16)
                    sp.dma_start(kc_gain[:, :], a["nsa_knorm"][0, 0].partition_broadcast(P)).then_inc(small_in, 16)
                    sp.wait_ge(zeroed, 4)
                    for kv in range(2):
                        for g in range(KVH):
                            half = slice(g * HD, (g + 1) * HD)
                            sp.dma_start(w1[half, kv, :, half], a["nsa_cmp_w1"][0, kv].rearrange("(l d) e -> d l e", d=HD)).then_inc(w_in, 16)
                            sp.dma_start(w2[half, kv, half], a["nsa_cmp_w2"][0, kv]).then_inc(w_in, 16)
                            sp.dma_start(pe_t[half, kv, :], a["nsa_cmp_pe"][0, kv].rearrange("l d -> d l")).then_inc(w_in, 16)
                    sp.wait_ge(v_here, 1)
                    for g in range(KVH):
                        for i in range(HPG):
                            sp.dma_start(vbd[i * CP:i * CP + N_CMP, g, i, :], vc[0:N_CMP, g * HD:(g + 1) * HD]).then_inc(v_spread, 16)
                    sp.wait_ge(v_spread, 16 * KVH * HPG)

            @block.gpsimd
            def _(pool):
                pool.memset(w1[:, :, :, :], 0.0).then_inc(zeroed, 1)
                pool.memset(w2[:, :, :], 0.0).then_inc(zeroed, 1)
                pool.memset(vbd[:, :, :, :], 0.0).then_inc(zeroed, 1)
                pool.memset(kcT[:, :], 0.0).then_inc(zeroed, 1)

            @block.vector
            def _(dve):
                link = Chain(dve, dve_c).link
                dve.memset(pos_i[:, T:T + 1], 0).then_inc(angles, 1)
                for i in range(T):
                    link(dve.tensor_tensor(sq[:, :], qk[:, i].rearrange("p h d -> p (h d)"),
                                           qk[:, i].rearrange("p h d -> p (h d)"), ALU.mult))
                    link(dve.tensor_reduce(ss[:, i * QH:(i + 1) * QH], sq[:, :].rearrange("p (h d) -> p h d", d=HD), AX.X, ALU.add))
                dve.tensor_scalar(ss[:, :], ss[:, :], 1.0 / HD, EPS, ALU.mult, ALU.add).then_inc(means, 1)
                dve.wait_ge(small_in, 16 * (3 + QH + 1))
                link(dve.tensor_copy(pos[:, :], pos_i[:, :]))
                for i in range(T + 1):
                    ins = dve.tensor_scalar(ang[:, i, :], freq[:, :], pos[:, i:i + 1], None, ALU.mult)
                link(ins)
                link(dve.tensor_scalar(turns[:, :, :], ang[:, :, :], 1 / TWO_PI, MAGIC, ALU.mult, ALU.add))
                link(dve.tensor_scalar(turns[:, :, :], turns[:, :, :], MAGIC, None, ALU.subtract))
                for part in (C1, C2, C3):
                    link(dve.scalar_tensor_tensor(out=ang[:, :, :], in0=turns[:, :, :], scalar=-part,
                                                  in1=ang[:, :, :], op0=ALU.mult, op1=ALU.add))
                dve.tensor_scalar(ang[:, :, :], ang[:, :, :], 3.1415925, -3.1415925, ALU.min, ALU.max).then_inc(angles, 1)

                def blocks_of(kv):
                    dve.wait_ge(w_in, 16 * 12)
                    if kv:
                        dve.wait_ge(hidden, 1)
                    for lh in range(2):
                        src = kvc[:, kv, lh * 16:lh * 16 + 16 * N_CMP].rearrange("p (c l) -> p l c", l=16)
                        dve.tensor_tensor(blk[:, lh * 16:lh * 16 + 16, 0:N_CMP], src,
                                          pe_t[:, kv, lh * 16:lh * 16 + 16].unsqueeze(2).to_broadcast([P, 16, N_CMP]),
                                          ALU.add).then_inc(blocks, 1)
                dve.wait_ge(sines, 2)
                link(dve.tensor_tensor(cos[:, :, :], cos[:, :, :], cos[:, :, :], ALU.mult))
                link(dve.tensor_scalar(cos[:, :, :], cos[:, :, :], -2.0, 1.0, ALU.mult, ALU.add))
                dve.wait_ge(roots, 1)
                link(dve.reciprocal(ss[:, :], root[:, :]))
                link(dve.tensor_scalar(gains[:, 0:HEADS, :], gains[:, 0:HEADS, :], HD ** -0.5, None, ALU.mult))

                def heads(i):
                    r = ss[:, i * QH:(i + 1) * QH].unsqueeze(2).to_broadcast([P, QH, HD])
                    link(dve.tensor_tensor(rot[:, :, :], qk[:, i], r, ALU.mult))
                    link(dve.tensor_tensor(rot[:, :, :], rot[:, :, :], gains[:, :, :], ALU.mult))
                    rotate(dve, link, qk[:, i], rot[:, :, :], cos[:, i], sin[:, i], tmp, QH).then_inc(heads_done, 1)
                    dve.wait_ge(heads_done, i + 1)

                heads(0)
                blocks_of(0)
                heads(1)
                blocks_of(1)
                heads(2)
                heads(3)
                dve.wait_ge(out2, 1)
                link(dve.tensor_copy(kc[0:N_CMP], m.psum[6][0:N_CMP, 0:P].rearrange("p (g d) -> p g d", g=KVH)))
                link(dve.tensor_tensor(kc_sq[0:N_CMP], kc[0:N_CMP], kc[0:N_CMP], ALU.mult))
                link(dve.tensor_reduce(kc_ss[0:N_CMP], kc_sq[0:N_CMP], AX.X, ALU.add))
                dve.tensor_scalar(kc_ss[0:N_CMP], kc_ss[0:N_CMP], 1.0 / HD, EPS, ALU.mult, ALU.add).then_inc(kc_mean, 1)
                dve.wait_ge(kc_root, 1)
                link(dve.reciprocal(kc_ss[0:N_CMP], kc_sq[0:N_CMP, 0, 0:KVH]))
                link(dve.tensor_tensor(kc_n[0:N_CMP], kc[0:N_CMP], kc_ss[0:N_CMP].unsqueeze(2).to_broadcast([N_CMP, KVH, HD]), ALU.mult))
                link(dve.tensor_tensor(kc_n[0:N_CMP], kc_n[0:N_CMP], kc_gain[0:N_CMP].unsqueeze(1).to_broadcast([N_CMP, KVH, HD]), ALU.mult))
                rotate(dve, link, kc_r[0:N_CMP], kc_n[0:N_CMP], cos[0:N_CMP, T], sin[0:N_CMP, T], kc_tmp[0:N_CMP], KVH).then_inc(kc_done, 1)
                dve.wait_ge(zeroed, 4)
                dve.wait_ge(kc_turned, 1)
                dve.tensor_copy(kcT[:, 0:N_CMP], m.psum[7][:, 0:N_CMP])

            @block.scalar
            def _(act):
                act.wait_ge(angles, 2)
                act.activation(sin[:, :, :], ang[:, :, :], ACT.Sin).then_inc(sines, 1)
                act.activation(cos[:, :, :], ang[:, :, :], ACT.Sin, scale=0.5).then_inc(sines, 1)
                act.wait_ge(means, 1)
                act.activation(root[:, :], ss[:, :], ACT.Sqrt).then_inc(roots, 1)
                for kv in range(2):
                    act.wait_ge(hidden, kv + 1)
                    act.activation(act1[:, kv, 0:N_CMP], m.psum[kv][:, 0:N_CMP], ACT.Gelu_apprx_tanh).then_inc(gelued, 1)
                act.wait_ge(out2, 2)
                act.activation(vc[0:N_CMP], m.psum[7][0:N_CMP, 0:P], ACT.Copy).then_inc(v_here, 1)
                act.wait_ge(kc_mean, 1)
                act.activation(kc_sq[0:N_CMP, 0, 0:KVH], kc_ss[0:N_CMP], ACT.Sqrt).then_inc(kc_root, 1)
                for i in range(T):
                    act.wait_ge(turned, i + 1)
                    act.activation(qkT[:, 0:4, i * P:(i + 1) * P],
                                   m.psum[2 + 2 * (i % 2)][:, :].rearrange("p (k t) -> p k t", k=4), ACT.Copy)
                    act.activation(qkT[:, 4:6, i * P:(i + 1) * P],
                                   m.psum[3 + 2 * (i % 2)][:, 0:2 * P].rearrange("p (k t) -> p k t", k=2), ACT.Copy).then_inc(kept, 1)

            @block.tensor
            def _(pe):
                for kv in range(2):
                    pe.wait_ge(blocks, 2 * kv + 2)
                    for l in range(CMP_LEN):
                        ins = pe.matmul(m.psum[kv][:, 0:N_CMP], w1[:, kv, l, :], blk[:, l, 0:N_CMP],
                                        start=l == 0, stop=l == CMP_LEN - 1)
                    ins.then_inc(hidden, 1)
                for kv in range(2):
                    pe.wait_ge(gelued, kv + 1)
                    pe.matmul(m.psum[6 + kv][0:N_CMP, 0:P], act1[:, kv, 0:N_CMP], w2[:, kv, :],
                              start=True, stop=True).then_inc(out2, 1)
                for i in range(T):
                    pe.wait_ge(heads_done, i + 1)
                    if i >= 2:
                        pe.wait_ge(kept, i - 1)
                    for pair in range(NP6):
                        ins = pe.transpose(m.psum[2 + 2 * (i % 2) + pair // 4][:, (pair % 4) * P:(pair % 4 + 1) * P],
                                           qk[:, i, 2 * pair:2 * pair + 2, :].rearrange("p h d -> p (h d)"), m.ident[:, :])
                    ins.then_inc(turned, 1)
                pe.wait_ge(kc_done, 1)
                pe.wait_ge(v_here, 1)
                pe.transpose(m.psum[7][:, 0:N_CMP], kc_r[0:N_CMP].rearrange("p g d -> p (g d)"),
                             m.ident[0:N_CMP, 0:N_CMP]).then_inc(kc_turned, 1)
    return qkT, kcT, vbd


def compressed_branch(m, qkT, kcT, vbd, gaT, mix, gate):
    m.phase()
    nc, a = m.nc, m.a
    with ExitStack() as t:
        cmask = m.sb(t, "cmp_neg", [P, T, CP])
        cone = m.sb(t, "cmp_one", [P, T, CP])
        gate_b = m.sb(t, "gate_b", [P, 3 * HEADS])
        ga = m.sb(t, "gates", [P, T, 3 * HEADS])
        cs = m.sb(t, "cmp_s", [P, KVH, T, HPG, CP])
        cp = m.sb(t, "cmp_p", [P, KVH, T, HPG, CP])
        cpT = m.sb(t, "cmp_pT", [P, KVH, T, P])
        cmax = m.sb(t, "cmp_max", [P, KVH, T, HPG])
        csum = m.sb(t, "cmp_sum", [P, KVH, T, HPG])
        ga_t = m.psem("cmp_ga_t")
        (gb_in, masks, gated, g_lin, dve_c, subbed, exped, normed, turned, kept, out_ps) = (
            m.psem(f"cmp_{s}") for s in ("gb_in", "masks", "gated", "g_lin", "dve", "subbed",
                                         "exped", "normed", "turned", "kept", "out_ps"))
        scored = [m.psem(f"cmp_scored{g}") for g in range(KVH)]
        with nc.Block() as block:
            @block.sync
            def _(sp):
                sp.dma_start(gate_b[:, :], a["nsa_gate_b"][0].partition_broadcast(P)).then_inc(gb_in, 16)

            @block.gpsimd
            def _(pool):
                pool.memset(cmask[:, :, :], 0.0).then_inc(masks, 1)
                pool.memset(cone[:, :, :], 1.0).then_inc(masks, 1)
                pool.wait_ge(masks, 2)
                for tile_, fill in ((cmask, NEG), (cone, 0.0)):
                    pool.affine_select(out=tile_[:, :, :], in_=tile_[:, :, :], compare_op=ALU.is_ge, fill=fill,
                                       base=-(CMP_LEN - 1), pattern=[[P, T], [-CMP_STRIDE, CP]],
                                       channel_multiplier=1).then_inc(masks, 1)

            @block.tensor
            def _(pe):
                for i in range(T):
                    ins = pe.transpose(m.psum[0][:, i * 3 * HEADS:(i + 1) * 3 * HEADS], gaT[:, i * P:(i + 1) * P],
                                       m.ident[0:3 * HEADS, 0:3 * HEADS])
                ins.then_inc(ga_t, 1)
                for i in range(T):
                    for h in range(HPG):
                        for g in range(KVH):
                            c0 = (i * HPG + h) * CP
                            ins = pe.matmul(m.psum[4 + g][:, c0:c0 + CP], qkT[g * HD:(g + 1) * HD, h, i * P:(i + 1) * P],
                                            kcT[g * HD:(g + 1) * HD, :], start=True, stop=True)
                            if i == T - 1 and h == HPG - 1:
                                ins.then_inc(scored[g], 1)
                pe.wait_ge(normed, 1)
                for g in range(KVH):
                    for i in range(T):
                        ins = pe.transpose(m.psum[6 + g][:, i * P:(i + 1) * P],
                                           cp[:, g, i].rearrange("p h c -> p (h c)"), m.ident[:, :])
                    ins.then_inc(turned, 1)
                pe.wait_ge(kept, KVH)
                for i in range(T):
                    for g in range(KVH):
                        ins = pe.matmul(m.psum[i][:, g * HPG * HD:(g + 1) * HPG * HD], cpT[:, g, i, :],
                                        vbd[:, g].rearrange("p h d -> p (h d)"), start=True, stop=True)
                    ins.then_inc(out_ps, 1)

            @block.scalar
            def _(act):
                act.wait_ge(subbed, 1)
                act.activation(cp[:, :, :, :, :], cs[:, :, :, :, :], ACT.Exp).then_inc(exped, 1)
                act.wait_ge(g_lin, 1)
                act.activation(gate[:, :, :, :].rearrange("p t h b -> p (t h b)"),
                               ga[:, :, :].rearrange("p t c -> p (t c)"), ACT.Sigmoid).then_inc(gated, 1)
                for g in range(KVH):
                    act.wait_ge(turned, g + 1)
                    act.activation(cpT[:, g], m.psum[6 + g][:, :].rearrange("p (i t) -> p i t", i=T), ACT.Copy).then_inc(kept, 1)

            @block.vector
            def _(dve):
                link = Chain(dve, dve_c).link
                dve.wait_ge(gb_in, 16)
                dve.wait_ge(ga_t, 1)
                dve.tensor_tensor(ga[:, :, :], m.psum[0][:, 0:T * 3 * HEADS].rearrange("p (t c) -> p t c", t=T), gate_b[:, :].unsqueeze(1).to_broadcast([P, T, 3 * HEADS]),
                                  ALU.add).then_inc(g_lin, 1)
                dve.wait_ge(masks, 4)
                for g in range(KVH):
                    dve.wait_ge(scored[g], 1)
                    for i in range(T):
                        ins = dve.tensor_tensor(cs[:, g, i], m.psum[4 + g][:, i * P:(i + 1) * P].rearrange("p (h c) -> p h c", c=CP),
                                                cmask[:, i].unsqueeze(1).to_broadcast([P, HPG, CP]), ALU.add)
                link(ins)
                link(dve.tensor_reduce(cmax[:, :, :, :], cs[:, :, :, :, :], AX.X, ALU.max))
                for g in range(KVH):
                    ins = dve.tensor_tensor(cs[:, g], cs[:, g], cmax[:, g].unsqueeze(3).to_broadcast([P, T, HPG, CP]),
                                            ALU.subtract)
                ins.then_inc(subbed, 1)
                dve.wait_ge(exped, 1)
                for g in range(KVH):
                    for i in range(T):
                        ins = dve.tensor_tensor(cp[:, g, i], cp[:, g, i], cone[:, i].unsqueeze(1).to_broadcast([P, HPG, CP]), ALU.mult)
                ins.then_inc(normed, 1)
                dve.wait_ge(normed, 1)
                link(dve.tensor_reduce(csum[:, :, :, :], cp[:, :, :, :, :], AX.X, ALU.add))
                link(dve.tensor_scalar(csum[:, :, :, :], csum[:, :, :, :], 1e-30, None, ALU.max))
                link(dve.reciprocal(csum[:, :, :, :], csum[:, :, :, :]))
                dve.wait_ge(gated, 1)
                for g in range(KVH):
                    ins = dve.tensor_tensor(csum[:, g], csum[:, g], gate[:, :, g * HPG:(g + 1) * HPG, 0], ALU.mult)
                link(ins)
                for i in range(T):
                    dve.wait_ge(out_ps, i + 1)
                    for g in range(KVH):
                        cols = slice(g * HPG * HD, (g + 1) * HPG * HD)
                        dve.tensor_tensor(mix[:, i, cols].rearrange("p (h d) -> p h d", d=HD),
                                          m.psum[i][:, cols].rearrange("p (h d) -> p h d", d=HD),
                                          csum[:, g, i].unsqueeze(2).to_broadcast([P, HPG, HD]), ALU.mult)


def nsa_attention(m, qkT, kcT, vbd, v_sw, gaT, mix):
    nc = m.nc
    units = [(i, br, h) for i in range(T) for br in range(2) for h in range(HPG)]
    NU = len(units)

    def keys(u):
        i, br, h = units[u]
        return list(range(0 if br == 0 else max(0, i - WT), i + 1))

    with ExitStack() as t:
        gate = m.sb(t, "gate", [P, T, HEADS, 3])
        compressed_branch(m, qkT, kcT, vbd, gaT, mix, gate)
        m.phase()
        prob = m.sb(t, "prob", [P, 2, 2, S])
        probT = m.sb(t, "probT", [P, 2, S])
        nmax = m.sb(t, "nmax", [P, 2, 2])
        sums = m.sb(t, "sums", [P, 2, KVH, HPG])
        coef = m.sb(t, "coef", [P, HEADS])
        part = m.sb(t, "part", [P, 2, HEADS, HD])
        zeros = m.sb(t, "zeros", [P, D])
        (zeroed, dve_c, maxed, exped, turned, kept_act, kept_dve, summed, scaled, combined) = (
            m.psem(f"attn_{s}") for s in ("zeroed", "dve", "maxed", "exped", "turned", "kept_act",
                                          "kept_dve", "summed", "scaled", "combined"))
        scored = [m.psem(f"attn_scored{g}") for g in range(KVH)]
        with nc.Block() as block:
            @block.sync
            def _(sp):
                sp.wait_ge(zeroed, 1)
                m.clear_outputs(sp, zeros[:, :])

            @block.tensor
            def _(pe):
                def score(u):
                    i, br, h = units[u]
                    kt = keys(u)
                    for g in range(KVH):
                        half = slice(g * HD, (g + 1) * HD)
                        ins = pe.matmul(m.psum[2 * (u % 2) + g][:, 0:len(kt) * P], qkT[half, h, i * P:(i + 1) * P],
                                        qkT[half, 4 + br, kt[0] * P:(kt[-1] + 1) * P], start=True, stop=True)
                        ins.then_inc(scored[g], 1)

                score(0)
                score(1)
                for u, (i, br, h) in enumerate(units):
                    kt = keys(u)
                    for e in range(2):
                        pe.wait_ge(exped, 2 * u + e + 1)
                        for j in range(len(kt)):
                            ins = pe.transpose(m.psum[4 + e][:, j * P:(j + 1) * P],
                                               prob[:, u % 2, e, j * P:(j + 1) * P], m.ident[:, :])
                        ins.then_inc(turned, 1)
                    if u + 2 < NU:
                        score(u + 2)
                    n = u // HPG
                    if u % HPG == 0 and n >= 2:
                        pe.wait_ge(scaled, n - 1)
                    for e, kept in enumerate((kept_act, kept_dve)):
                        pe.wait_ge(kept, u + 1)
                        c0 = (e * HPG + h) * HD
                        for j, k in enumerate(kt):
                            ins = pe.matmul(m.psum[6 + n % 2][:, c0:c0 + HD], probT[:, e, j * P:(j + 1) * P],
                                            v_sw[:, k, br, e * HD:(e + 1) * HD], start=j == 0, stop=j == len(kt) - 1)
                    if u % HPG == HPG - 1:
                        ins.then_inc(summed, 1)

            @block.scalar
            def _(act):
                def exp(u):
                    i, br, h = units[u]
                    w = len(keys(u)) * P
                    act.wait_ge(maxed, u + 1)
                    if u >= 2:
                        act.wait_ge(turned, 2 * (u - 1))
                    if u % HPG == 0 and u >= 2 * HPG:
                        act.wait_ge(scaled, u // HPG - 1)
                    for e in range(2):
                        act.activation(prob[:, u % 2, e, 0:w], m.psum[2 * (u % 2) + e][:, 0:w], ACT.Exp,
                                       bias=nmax[:, u % 2, e:e + 1],
                                       accum_out=sums[:, br, e, h:h + 1]).then_inc(exped, 1)

                exp(0)
                for u in range(NU):
                    if u + 1 < NU:
                        exp(u + 1)
                    w = len(keys(u)) * P
                    act.wait_ge(turned, 2 * u + 1)
                    act.activation(probT[:, 0, 0:w], m.psum[4][:, 0:w], ACT.Copy).then_inc(kept_act, 1)

            @block.vector
            def _(dve):
                link = Chain(dve, dve_c).link

                def maximum(u):
                    i, br, h = units[u]
                    w = len(keys(u)) * P
                    for e in range(2):
                        dve.wait_ge(scored[e], u + 1)
                        s = m.psum[2 * (u % 2) + e]
                        ins = dve.tensor_tensor(s[:, w - P:w], s[:, w - P:w], m.causal[:, :], ALU.add)
                        if br and i >= WT:
                            ins = dve.tensor_tensor(s[:, 0:P], s[:, 0:P], m.beyond[:, :], ALU.add)
                    link(ins)
                    for e in range(2):
                        ins = dve.tensor_reduce(nmax[:, u % 2, e:e + 1], m.psum[2 * (u % 2) + e][:, 0:w], AX.X, ALU.max, negate=True)
                    ins.then_inc(maxed, 1)

                def scale(n):
                    i, br, h = units[n * HPG]
                    dve.wait_ge(exped, 2 * HPG * (n + 1))
                    link(dve.reciprocal(coef[:, :], sums[:, br].rearrange("p g h -> p (g h)")))
                    link(dve.tensor_tensor(coef[:, :], coef[:, :], gate[:, i, :, 1 + br], ALU.mult))
                    dve.wait_ge(summed, n + 1)
                    if n >= 2:
                        dve.wait_ge(combined, n - 1)
                    dve.tensor_tensor(part[:, n % 2], m.psum[6 + n % 2][:, :].rearrange("p (h d) -> p h d", d=HD),
                                      coef[:, :].unsqueeze(2).to_broadcast([P, HEADS, HD]),
                                      ALU.mult).then_inc(scaled, 1)

                maximum(0)
                maximum(1)
                for u in range(NU):
                    w = len(keys(u)) * P
                    dve.wait_ge(turned, 2 * u + 2)
                    dve.tensor_copy(probT[:, 1, 0:w], m.psum[5][:, 0:w]).then_inc(kept_dve, 1)
                    if u + 2 < NU:
                        maximum(u + 2)
                    if u and u % HPG == 0:
                        scale(u // HPG - 1)
                scale(NU // HPG - 1)

            @block.gpsimd
            def _(pool):
                pool.memset(zeros[:, :], 0.0).then_inc(zeroed, 1)
                for n in range(NU // HPG):
                    i, br, h = units[n * HPG]
                    out = mix[:, i, 0:HEADS * HD].rearrange("p (h d) -> p h d", h=HEADS)
                    if n:
                        pool.wait_ge(combined, n)
                    pool.wait_ge(scaled, n + 1)
                    pool.tensor_tensor(out, out, part[:, n % 2], ALU.add).then_inc(combined, 1)


def gla(m, gqk, gv, gr, alT, mix):
    m.phase()
    nc, a = m.nc, m.a
    NF = GH * GDK // P
    CAP = 80.0
    with ExitStack() as t:
        wa = m.sb(t, "wa2", [GRANK + 1, GH * GDK])
        tri = m.sb(t, "tri16", [P, P])
        keep = m.sb(t, "keep", [P, GCH])
        la = m.sb(t, "log_a", [P, T, GH * GDK])
        ex = m.sb(t, "ex", [P, T, GH * GDK])
        b = m.sb(t, "b", [P, NF, S])
        qb = m.sb(t, "q_decayed", [P, NF, S])
        qe = m.sb(t, "q_ref", [P, NF, S])
        kl = m.sb(t, "k_last", [P, NF, S])
        ks = m.sb(t, "k_ref", [P, NSUB, S])
        klt = m.sb(t, "k_last_tok", [P, T, NF * P])
        att = m.sb(t, "att", [P, GH, T, P])
        state = m.sb(t, "state", [P, NF, NCH, 2 * GDV])
        dec = m.sb(t, "dec", [P, NF, NCH])
        o = m.sb(t, "gla_o", [P, T, GH * GDV])
        ms = m.sb(t, "gla_ms", [P, T * GH])
        root = m.sb(t, "gla_root", [P, T * GH])
        og = m.sb(t, "gla_onorm_row", [P, GDV])
        (small_in, made, dve_c, lin, absd, exped, plus1, logged, la_done, cum, cum_k,
         d_qb, e_qb, d_qe, e_qe, d_kl, e_kl, d_ks, e_ks, ks_done, q_done, kl_done, kl_t, kl_k, atted, att_k,
         kv_done, kv_k, states, o_done, o_k, silu, mean, rooted) = (m.psem(f"gla_{s}") for s in (
            "small_in", "made", "dve", "lin", "absd", "exped", "plus1", "logged",
            "la_done", "cum", "cum_k", "d_qb", "e_qb", "d_qe", "e_qe", "d_kl", "e_kl", "d_ks", "e_ks", "ks_done",
            "q_done", "kl_done", "kl_t", "kl_k", "atted", "att_k", "kv_done", "kv_k", "states", "o_done", "o_k",
            "silu", "mean", "rooted"))

        def read_scores(dve, f):
            for h in (2 * f, 2 * f + 1):
                for p in range(2):
                    half = slice(p * GCH, (p + 1) * GCH)
                    src = m.psum[h % 2][half, :].rearrange("p (i c) -> p i c", i=T)[:, :, p * GCH:(p + 1) * GCH]
                    ins = dve.tensor_tensor(att[half, h, :, p * GCH:(p + 1) * GCH], src,
                                            keep[half, :].unsqueeze(1).to_broadcast([GCH, T, GCH]), ALU.mult)
            ins.then_inc(att_k, 1)

        def sub_ref(f):
            return b[:, f, :].rearrange("p (r j) -> p r j", j=SUB)[:, :, SUB // 2:SUB // 2 + 1]

        with nc.Block() as block:
            @block.sync
            def _(sp):
                sp.dma_start(wa[0:GRANK, :], a["gla_wa2"][0]).then_inc(small_in, 16)
                sp.dma_start(wa[GRANK:GRANK + 1, :], a["gla_ba"]).then_inc(small_in, 16)
                sp.dma_start(og[:, :], a["gla_onorm"][0].partition_broadcast(P)).then_inc(small_in, 16)

            @block.gpsimd
            def _(pool):
                pool.memset(tri[:, :], 1.0 / GTAU).then_inc(made, 1)
                pool.memset(keep[:, :], 1.0).then_inc(made, 1)
                pool.memset(att[:, :, :, :], 0.0).then_inc(made, 1)
                pool.memset(state[:, :, :, :], 0.0).then_inc(made, 1)
                pool.wait_ge(made, 4)
                pool.affine_select(out=tri[:, :], in_=tri[:, :], compare_op=ALU.is_ge, fill=0.0, base=0,
                                   pattern=[[1, P]], channel_multiplier=-1).then_inc(made, 1)
                for p in range(2):
                    pool.wait_ge(made, 5 + p)
                    pool.affine_select(out=keep[p * GCH:(p + 1) * GCH, :], in_=keep[p * GCH:(p + 1) * GCH, :],
                                       compare_op=ALU.is_ge, fill=0.0, base=0, pattern=[[1, GCH]],
                                       channel_multiplier=-1).then_inc(made, 1)
                pool.wait_ge(made, 7)
                pool.memset(tri[0:GCH, GCH:P], 0.0).then_inc(made, 1)

            @block.tensor
            def _(pe):
                pe.wait_ge(small_in, 48)
                for i in range(T):
                    ins = pe.matmul(m.psum[1 + i // 2][:, (i % 2) * 256:(i % 2 + 1) * 256],
                                    alT[:, i * P:(i + 1) * P], wa[:, :], start=True, stop=True)
                ins.then_inc(lin, 1)
                pe.wait_ge(made, 8)
                pe.wait_ge(la_done, 1)
                for f in range(NF):
                    for i in range(T):
                        ins = pe.matmul(m.psum[3 + f][:, i * P:(i + 1) * P], la[:, i, f * P:(f + 1) * P], tri[:, :],
                                        start=True, stop=True)
                ins.then_inc(cum, 1)
                pe.wait_ge(q_done, 2 * NF)
                for f in range(NF):
                    pe.wait_ge(ks_done, f + 1)
                    for h in (2 * f, 2 * f + 1):
                        half = slice((h % 2) * GDK, (h % 2 + 1) * GDK)
                        for c in range(NCH):
                            for s in range(NSUB):
                                q0 = c * GCH + s * SUB
                                col = (c // 2) * P + (c % 2) * GCH + s * SUB
                                ins = pe.matmul(m.psum[h % 2][(c % 2) * GCH:(c % 2 + 1) * GCH, col:col + SUB],
                                                ks[half, s, c * GCH:(c + 1) * GCH], qe[half, f, q0:q0 + SUB],
                                                start=True, stop=True)
                    ins.then_inc(atted, 1)
                    if f == 0:
                        pe.wait_ge(kl_done, NF)
                        for i in range(T):
                            for f2 in range(NF):
                                ins = pe.transpose(m.psum[2 + i // 2][:, (i % 2) * 256 + f2 * P:(i % 2) * 256 + (f2 + 1) * P],
                                                   kl[:, f2, i * P:(i + 1) * P], m.ident[:, :])
                        ins.then_inc(kl_t, 1)
                        pe.wait_ge(att_k, 1)
                pe.wait_ge(kl_k, 1)
                for c in range(NCH - 1):
                    i, half = c // 2, slice((c % 2) * GCH, (c % 2 + 1) * GCH)
                    for f in range(NF):
                        if c >= 2:
                            pe.wait_ge(states, NF * (c - 1))
                        ins = pe.matmul(m.psum[2 + c % 2][:, f * 256:(f + 1) * 256], klt[half, i, f * P:(f + 1) * P],
                                        gv[half, i, f * 2 * GDV:(f + 1) * 2 * GDV], start=True, stop=True)
                    ins.then_inc(kv_done, 1)
                pe.wait_ge(att_k, NF)
                pe.wait_ge(states, NF * (NCH - 1))
                for i in range(T):
                    out = m.psum[4 + i]
                    for h in range(GH):
                        pe.matmul(out[:, h * GDV:(h + 1) * GDV], att[:, h, i, :], gv[:, i, h * GDV:(h + 1) * GDV],
                                  start=h == 0, stop=False, skip_group_check=True)
                    for c in (2 * i, 2 * i + 1):
                        if c:
                            for f in range(NF):
                                half = slice((c % 2) * GCH, (c % 2 + 1) * GCH)
                                ins = pe.matmul(out[half, f * 256:(f + 1) * 256], qb[:, f, c * GCH:(c + 1) * GCH],
                                                state[:, f, c, :], start=False, stop=True, skip_group_check=True)
                    ins.then_inc(o_done, 1)

            @block.scalar
            def _(act):
                act.wait_ge(absd, 1)
                act.activation(ex[:, :, :], ex[:, :, :], ACT.Exp).then_inc(exped, 1)
                act.wait_ge(plus1, 1)
                act.activation(ex[:, :, :], ex[:, :, :], ACT.Ln).then_inc(logged, 1)
                for f in range(NF):
                    act.wait_ge(cum_k, f + 1)
                    act.activation(qb[:, f, :], b[:, f, :], ACT.Exp).then_inc(e_qb, 1)
                    act.activation(dec[:, f, :], b[:, f, :].rearrange("p (c j) -> p c j", j=GCH)[:, :, GCH - 1], ACT.Exp)
                    act.wait_ge(d_qe, f + 1)
                    act.activation(qe[:, f, :], qe[:, f, :], ACT.Exp).then_inc(e_qe, 1)
                    act.wait_ge(d_kl, f + 1)
                    act.activation(kl[:, f, :], kl[:, f, :], ACT.Exp).then_inc(e_kl, 1)
                for f in range(NF):
                    act.wait_ge(d_ks, f + 1)
                    act.activation(ks[:, :, :], ks[:, :, :], ACT.Exp).then_inc(e_ks, 1)
                    if f == 0:
                        act.wait_ge(kl_t, 1)
                        for i2 in range(2):
                            ins = act.activation(klt[:, 2 * i2:2 * i2 + 2, :], m.psum[2 + i2][:, :].rearrange("p (i f) -> p i f", i=2), ACT.Copy)
                        ins.then_inc(kl_k, 1)
                act.activation(gr[:, :, :], gr[:, :, :], ACT.Silu).then_inc(silu, 1)
                for i in range(T):
                    act.wait_ge(o_done, i + 1)
                    act.activation(o[:, i, :], m.psum[4 + i][:, :], ACT.Copy).then_inc(o_k, 1)
                act.wait_ge(mean, 1)
                act.activation(root[:, :], ms[:, :], ACT.Sqrt).then_inc(rooted, 1)

            @block.vector
            def _(dve):
                link = Chain(dve, dve_c).link
                dve.wait_ge(made, 4)
                dve.wait_ge(lin, 1)
                for i2 in range(2):
                    ins = dve.tensor_copy(la[:, 2 * i2:2 * i2 + 2, :], m.psum[1 + i2][:, :].rearrange("p (i f) -> p i f", i=2))
                link(ins)
                dve.scalar_tensor_tensor(out=ex[:, :, :], in0=la[:, :, :], scalar=-1.0, in1=la[:, :, :],
                                         op0=ALU.mult, op1=ALU.min).then_inc(absd, 1)
                dve.wait_ge(exped, 1)
                dve.tensor_scalar(ex[:, :, :], ex[:, :, :], 1.0, None, ALU.add).then_inc(plus1, 1)
                dve.wait_ge(logged, 1)
                dve.scalar_tensor_tensor(out=la[:, :, :], in0=la[:, :, :], scalar=0.0, in1=ex[:, :, :],
                                         op0=ALU.min, op1=ALU.subtract).then_inc(la_done, 1)
                dve.wait_ge(cum, 1)
                for f in range(NF):
                    dve.tensor_copy(b[:, f, :], m.psum[3 + f][:, :]).then_inc(cum_k, 1)
                    dve.wait_ge(cum_k, f + 1)
                    link(dve.tensor_tensor(qe[:, f, :].rearrange("p (r j) -> p r j", j=SUB),
                                           b[:, f, :].rearrange("p (r j) -> p r j", j=SUB),
                                           sub_ref(f).to_broadcast([P, S // SUB, SUB]), ALU.subtract))
                    dve.tensor_scalar(qe[:, f, :], qe[:, f, :], CAP, None, ALU.min).then_inc(d_qe, 1)
                    bc = b[:, f, :].rearrange("p (c j) -> p c j", j=GCH)
                    dve.tensor_tensor(kl[:, f, :].rearrange("p (c j) -> p c j", j=GCH),
                                      bc[:, :, GCH - 1:GCH].to_broadcast([P, NCH, GCH]), bc, ALU.subtract).then_inc(d_kl, 1)
                for f in range(NF):
                    dve.wait_ge(e_qb, f + 1)
                    dve.tensor_tensor(qb[:, f, :], qb[:, f, :], gqk[:, f, :], ALU.mult).then_inc(q_done, 1)
                    dve.wait_ge(e_qe, f + 1)
                    dve.tensor_tensor(qe[:, f, :], qe[:, f, :], gqk[:, f, :], ALU.mult).then_inc(q_done, 1)
                    dve.wait_ge(e_kl, f + 1)
                    dve.tensor_tensor(kl[:, f, :], kl[:, f, :], gqk[:, NF + f, :], ALU.mult).then_inc(kl_done, 1)
                for f in range(NF):
                    if f:
                        dve.wait_ge(atted, f)
                    bc = b[:, f, :].rearrange("p (c j) -> p c j", j=GCH)
                    for s in range(NSUB):
                        at = s * SUB + SUB // 2
                        ins = dve.tensor_tensor(ks[:, s, :].rearrange("p (c j) -> p c j", j=GCH),
                                                bc[:, :, at:at + 1].to_broadcast([P, NCH, GCH]), bc, ALU.subtract)
                    link(ins)
                    dve.tensor_scalar(ks[:, :, :], ks[:, :, :], CAP, None, ALU.min).then_inc(d_ks, 1)
                    if f:
                        dve.wait_ge(made, 7)
                        read_scores(dve, f - 1)
                    dve.wait_ge(e_ks, f + 1)
                    dve.tensor_tensor(ks[:, :, :], ks[:, :, :], gqk[:, NF + f, :].unsqueeze(1).to_broadcast([P, NSUB, S]),
                                      ALU.mult).then_inc(ks_done, 1)
                dve.wait_ge(atted, NF)
                read_scores(dve, NF - 1)
                for c in range(NCH - 1):
                    dve.wait_ge(kv_done, c + 1)
                    for f in range(NF):
                        for h in range(2):
                            half, cols = slice(h * GDK, (h + 1) * GDK), slice(h * GDV, (h + 1) * GDV)
                            ins = dve.scalar_tensor_tensor(
                                out=state[half, f, c + 1, cols], in0=state[half, f, c, cols], scalar=dec[half, f, c:c + 1],
                                in1=m.psum[2 + c % 2][half, f * 256 + h * GDV:f * 256 + (h + 1) * GDV],
                                op0=ALU.mult, op1=ALU.add)
                        ins.then_inc(states, 1)
                    dve.wait_ge(states, NF * (c + 1))
                dve.wait_ge(o_k, T)
                link(dve.tensor_tensor(ks[:, :, :], o[:, :, :], o[:, :, :], ALU.mult))
                link(dve.tensor_reduce(ms[:, :], ks[:, :, :].rearrange("p t (h d) -> p (t h) d", d=GDV), AX.X, ALU.add))
                dve.tensor_scalar(ms[:, :], ms[:, :], 1.0 / GDV, EPS, ALU.mult, ALU.add).then_inc(mean, 1)
                dve.wait_ge(silu, 1)
                link(dve.tensor_tensor(gr[:, :, :], gr[:, :, :], o[:, :, :], ALU.mult))
                link(dve.tensor_tensor(gr[:, :, :].rearrange("p t (h d) -> p (t h) d", d=GDV),
                                       gr[:, :, :].rearrange("p t (h d) -> p (t h) d", d=GDV),
                                       og[:, :].unsqueeze(1).to_broadcast([P, T * GH, GDV]), ALU.mult))
                dve.wait_ge(rooted, 1)
                link(dve.reciprocal(ms[:, :], root[:, :]))
                for i in range(T):
                    ins = dve.tensor_tensor(mix[:, i, HEADS * HD:].rearrange("p (h d) -> p h d", d=GDV),
                                            gr[:, i, :].rearrange("p (h d) -> p h d", d=GDV),
                                            ms[:, i * GH:(i + 1) * GH].unsqueeze(2).to_broadcast([P, GH, GDV]), ALU.mult)
                link(ins)



def split_transpose(m, name, src, hi, lo):
    m.phase()
    turned, hi_out, lo_out = (m.psem(f"{name}_{s}") for s in ("turned", "hi_out", "lo_out"))
    with m.nc.Block() as block:
        @block.tensor
        def _(pe):
            for k in range(KD):
                for t in range(T):
                    ins = pe.transpose(m.psum[k][:, t * P:(t + 1) * P], src[:, t, k * P:(k + 1) * P], m.ident[:, :])
                ins.then_inc(turned, 1)

        @block.scalar
        def _(act):
            m.split_next_hi(act)
            for k in range(KD):
                act.wait_ge(turned, k + 1)
                act.activation(hi[:, k, :], m.psum[k][:, :], ACT.Copy).then_inc(hi_out, 1)

        @block.vector
        def _(dve):
            m.split_next_lo(dve)
            for k in range(KD):
                dve.wait_ge(hi_out, k + 1)
                dve.tensor_tensor(lo[:, k, :], m.psum[k][:, :], hi[:, k, :], ALU.subtract).then_inc(lo_out, 1)


def linear_residual(m, name, first, n_cols, parts):
    m.phase()
    added = m.psem(f"{name}_added")
    total = n_cols * len(parts)

    def add(dve, j):
        n = j // len(parts)
        m.done(dve, first + j)
        for t in range(T):
            cols = slice(n * GC, (n + 1) * GC)
            dve.tensor_tensor(m.x[:, t, cols], m.x[:, t, cols], m.psum[4 * (n % 2) + t][:, :], ALU.add).then_inc(added, 1)

    with m.nc.Block() as block:
        @block.sync
        def _(sp):
            m.load(sp, first + total + 1)

        @block.scalar
        def _(act):
            for j in range(total):
                m.split_hi(act, first + j)

        @block.tensor
        def _(pe):
            for n in range(n_cols):
                if n >= 2:
                    pe.wait_ge(added, T * (n - 1))
                for q, (hi, lo) in enumerate(parts):
                    m.product(pe, first + n * len(parts) + q, False, m.psum[4 * (n % 2):4 * (n % 2) + 4], hi, lo,
                              first=q == 0, last=q == len(parts) - 1)

        @block.vector
        def _(dve):
            for j in range(total):
                m.split_lo(dve, first + j)
                done = j - 1
                if done >= 0 and done % len(parts) == len(parts) - 1:
                    add(dve, done)
            add(dve, total - 1)


def hybrid_layer(m, first):
    a = m.a
    with ExitStack() as c:
        mix = m.sb(c, "mix", [P, T, D])
        with ExitStack() as c2:
            outputs = qk, v_sw, kvc, gqk, gv, gr, gaT, alT = projection_outputs(m, c2)
            with ExitStack() as c3:
                hi, lo = m.split_pair(c3, "h_mix0")
                norm_transpose(m, "mix0", m.x, a["norm_mix"][0], T, hi, lo, source=a["x"][0])
                hybrid_projection(m, outputs, first, hi, lo)
            with ExitStack() as c3:
                qkT, kcT, vbd = nsa_prepare(m, c3, qk, kvc)
                nsa_attention(m, qkT, kcT, vbd, v_sw, gaT, mix)
            gla(m, gqk, gv, gr, alT, mix)
        hi, lo = m.split_pair(c, "mixT")
        split_transpose(m, "mix0o", mix, hi, lo)
        linear_residual(m, "hyb_out", first + 7, 2, [(hi, lo)])


def project_heads(m, name, first, n_groups, n_normed, tiles, hi, lo, out, gain, scale, dst):
    m.phase()
    nc = m.nc
    g_in, squares, out_dve, mean, rooted, normed, turned, dve_c, kept_act, kept_dve = (
        m.psem(f"{name}_{s}") for s in ("g_in", "squares", "out_dve", "mean", "rooted", "normed", "turned", "dve",
                                        "kept_act", "kept_dve"))
    HG = GC // XHD
    KG = GC // P

    def place(k):
        j, kk = k // KG, k % KG
        if tiles == T:
            return KG * j + kk, 0, kk % 2 == 0
        return KG * j + 2 + kk // 2, kk % 2 * tiles * P, kk // 2 == 0

    def turns_after(n):
        return [j for j in range(n_normed) if min(j + 2, n_groups - 1) == n]

    with ExitStack() as t:
        junk = m.sb(t, f"{name}_junk", [P, GC])
        g = m.sb(t, f"{name}_g", [P, XHD])
        ms = m.sb(t, f"{name}_ms", [P, n_normed, tiles, HG])
        root = m.sb(t, f"{name}_root", [P, n_normed, tiles, HG])
        with nc.Block() as block:
            @block.sync
            def _(sp):
                sp.dma_start(g[:, :], gain.partition_broadcast(P)).then_inc(g_in, 16)
                m.load(sp, first + n_groups + 1)

            @block.tensor
            def _(pe):
                for n in range(n_groups):
                    if n >= 2:
                        pe.wait_ge(out_dve, tiles * (n - 1))
                    m.product(pe, first + n, False, m.psum[KG * (n % 2):KG * (n % 2) + KG], hi, lo, tiles=tiles)
                    for j in turns_after(n):
                        pe.wait_ge(normed, tiles * (j + 1))
                        for k in range(KG * j, KG * (j + 1)):
                            bank, c0, _ = place(k)
                            for i in range(tiles):
                                ins = pe.transpose(m.psum[bank][:, c0 + i * P:c0 + (i + 1) * P],
                                                   out[:, i, k * P:(k + 1) * P], m.ident[:, :])
                            ins.then_inc(turned, 1)

            def keep(engine, copy, n, on_act, kept):
                for j in turns_after(n):
                    for k in range(KG * j, KG * (j + 1)):
                        bank, c0, mine = place(k)
                        if mine == on_act:
                            engine.wait_ge(turned, KG * j + KG)
                            copy(dst[:, k, :], m.psum[bank][:, c0:c0 + tiles * P]).then_inc(kept, 1)

            @block.scalar
            def _(act):
                def copy(o, i):
                    return act.activation(o, i, ACT.Copy)

                m.split_hi(act, first)
                for n in range(n_groups):
                    if n + 1 < n_groups:
                        m.split_hi(act, first + n + 1)
                    if n:
                        keep(act, copy, n - 1, True, kept_act)
                    if n >= n_normed:
                        continue
                    m.done(act, first + n)
                    for i in range(tiles):
                        for h in range(HG):
                            cols = slice(h * XHD, (h + 1) * XHD)
                            ins = act.activation(junk[:, cols], m.psum[KG * (n % 2) + i][:, cols], ACT.Square,
                                                 accum_out=ms[:, n, i, h:h + 1])
                        ins.then_inc(squares, 1)
                        act.wait_ge(squares, n * tiles + i + 1)
                    act.wait_ge(mean, n + 1)
                    act.activation(root[:, n], ms[:, n], ACT.Sqrt).then_inc(rooted, 1)
                keep(act, copy, n_groups - 1, True, kept_act)

            @block.vector
            def _(dve):
                link = Chain(dve, dve_c).link
                m.split_lo(dve, first)
                dve.wait_ge(g_in, 16)
                link(dve.tensor_scalar(g[:, :], g[:, :], scale, None, ALU.mult))
                for n in range(n_groups):
                    if n + 1 < n_groups:
                        m.split_lo(dve, first + n + 1)
                    if n:
                        keep(dve, dve.tensor_copy, n - 1, False, kept_dve)
                    m.done(dve, first + n)
                    for i in range(tiles):
                        if n < n_normed:
                            dve.wait_ge(squares, n * tiles + i + 1)
                        dve.tensor_copy(out[:, i, n * GC:(n + 1) * GC], m.psum[KG * (n % 2) + i][:, :]).then_inc(out_dve, 1)
                    if n >= n_normed:
                        continue
                    dve.tensor_scalar(ms[:, n], ms[:, n], 1.0 / XHD, EPS, ALU.mult, ALU.add).then_inc(mean, 1)
                    dve.wait_ge(rooted, n + 1)
                    link(dve.reciprocal(ms[:, n], root[:, n]))
                    dve.wait_ge(out_dve, (n + 1) * tiles)
                    for i in range(tiles):
                        for h in range(HG):
                            cols = slice((n * HG + h) * XHD, (n * HG + h + 1) * XHD)
                            ins = dve.scalar_tensor_tensor(out=out[:, i, cols], in0=out[:, i, cols], scalar=ms[:, n, i, h:h + 1],
                                                           in1=g[:, :], op0=ALU.mult, op1=ALU.mult)
                        ins.then_inc(normed, 1)
                keep(dve, dve.tensor_copy, n_groups - 1, False, kept_dve)


def cross_attend(m, name, qT, kT, v, o_hi, o_lo):
    m.phase()
    nc = m.nc
    HH = XHD // P
    units = [(h, i) for h in range(XH) for i in range(T)]
    NU = len(units)
    RING, AHEAD = 4, 3
    score_ps, turn_ps, out_ps = m.psum[0:4], m.psum[4:6], m.psum[6:8]
    (scored, maxed, exped, normed, turned, kept, summed, o_hi_out, o_lo_out, dve_c) = (m.psem(f"{name}_{s}") for s in (
        "scored", "maxed", "exped", "normed", "turned", "kept", "summed", "o_hi_out", "o_lo_out", "dve"))
    with ExitStack() as t:
        prob = m.sb(t, f"{name}_prob", [P, RING, N_MEM])
        pT = m.sb(t, f"{name}_pT", [P, 2, MT, S])
        nmax = m.sb(t, f"{name}_nmax", [P, len(units)])
        sums = m.sb(t, f"{name}_sums", [P, len(units)])
        with nc.Block() as block:
            @block.tensor
            def _(pe):
                def score(u):
                    h, i = units[u]
                    if u >= RING:
                        pe.wait_ge(exped, u - RING + 1)
                    for d in range(HH):
                        ins = pe.matmul(score_ps[u % RING][:, 0:N_MEM], qT[:, HH * h + d, i * P:(i + 1) * P],
                                        kT[:, HH * h + d, :], start=d == 0, stop=d == HH - 1)
                    ins.then_inc(scored, 1)

                for u in range(AHEAD):
                    score(u)
                for u, (h, i) in enumerate(units):
                    pe.wait_ge(normed, u + 1)
                    if u >= 2:
                        pe.wait_ge(kept, u - 1)
                    for j in range(MT):
                        ins = pe.transpose(turn_ps[u % 2][:, j * P:(j + 1) * P], prob[:, u % RING, j * P:(j + 1) * P], m.ident[:, :])
                    ins.then_inc(turned, 1)
                    if u + AHEAD < NU:
                        score(u + AHEAD)
                    if i == T - 1:
                        pe.wait_ge(kept, u + 1)
                        for d in range(HH):
                            if h:
                                pe.wait_ge(o_lo_out, HH * (h - 1) + d + 1)
                            for j in range(MT):
                                ins = pe.matmul(out_ps[d][:, :], v[:, j, h * XHD + d * P:h * XHD + (d + 1) * P],
                                                pT[:, h % 2, j, :], start=j == 0, stop=j == MT - 1)
                            ins.then_inc(summed, 1)

            @block.scalar
            def _(act):
                def exp(u):
                    act.wait_ge(maxed, u + 1)
                    if u >= RING:
                        act.wait_ge(turned, u - RING + 1)
                    act.activation(prob[:, u % RING, :], score_ps[u % RING][:, 0:N_MEM], ACT.Exp, bias=nmax[:, u:u + 1],
                                   accum_out=sums[:, u:u + 1]).then_inc(exped, 1)

                def output(h):
                    for d in range(HH):
                        act.wait_ge(summed, HH * h + d + 1)
                        act.activation(o_hi[:, HH * h + d, :], out_ps[d][:, :], ACT.Copy).then_inc(o_hi_out, 1)

                for u in range(AHEAD - 1):
                    exp(u)
                for u, (h, i) in enumerate(units):
                    if u + AHEAD - 1 < NU:
                        exp(u + AHEAD - 1)
                    act.wait_ge(turned, u + 1)
                    if h >= 2 and i == 0:
                        act.wait_ge(summed, HH * (h - 1))
                    act.activation(pT[:, h % 2, :, i * P:(i + 1) * P],
                                   turn_ps[u % 2][:, 0:MT * P].rearrange("p (j t) -> p j t", j=MT), ACT.Copy).then_inc(kept, 1)
                    if h and i == 0:
                        output(h - 1)
                    if u == T + 1:
                        m.split_next_hi(act)
                output(XH - 1)

            @block.vector
            def _(dve):
                link = Chain(dve, dve_c).link

                def maximum(u):
                    dve.wait_ge(scored, u + 1)
                    dve.tensor_reduce(nmax[:, u:u + 1], score_ps[u % RING][:, 0:N_MEM], AX.X, ALU.max, negate=True).then_inc(maxed, 1)

                def normalize(u):
                    dve.wait_ge(exped, u + 1)
                    link(dve.reciprocal(sums[:, u:u + 1], sums[:, u:u + 1]))
                    dve.tensor_scalar(prob[:, u % RING, :], prob[:, u % RING, :], sums[:, u:u + 1], None, ALU.mult).then_inc(normed, 1)

                def rest(h):
                    for d in range(HH):
                        dve.wait_ge(o_hi_out, HH * h + d + 1)
                        dve.tensor_tensor(o_lo[:, HH * h + d, :], out_ps[d][:, :], o_hi[:, HH * h + d, :],
                                          ALU.subtract).then_inc(o_lo_out, 1)

                for u in range(AHEAD):
                    maximum(u)
                normalize(0)
                for u, (h, i) in enumerate(units):
                    if u + 1 < NU:
                        normalize(u + 1)
                    if u + AHEAD < NU:
                        maximum(u + AHEAD)
                    if h and i == 1:
                        rest(h - 1)
                    if u == T + 3:
                        m.split_next_lo(dve)
                rest(XH - 1)


def cross_attention(m, layer, first):
    a, nm = m.a, f"x{layer}"
    with ExitStack() as c:
        kT = m.sb(c, f"{nm}_kT", [P, KD, N_MEM])
        v = m.sb(c, f"{nm}_kv", [P, MT, 2 * D])
        with ExitStack() as c2:
            mem = m.sb(c2, f"{nm}_mem", [P, MT, D])
            hi, lo = m.split_pair(c2, f"{nm}_mem", n=N_MEM)
            norm_transpose(m, f"{nm}_nm", mem, a["norm_mem"][layer], MT, hi, lo, source=a["mem"][0])
            project_heads(m, f"{nm}_kv", first, 4, 2, MT, hi, lo, v, a["x_knorm"][layer], 1.0, kT)
        qT = m.sb(c, f"{nm}_qT", [P, KD, S])
        with ExitStack() as c2:
            q = m.sb(c2, f"{nm}_q", [P, T, D])
            hi, lo = m.split_pair(c2, f"{nm}_h")
            norm_transpose(m, f"{nm}_nx", m.x, a["norm_xattn"][layer], T, hi, lo)
            project_heads(m, f"{nm}_q", first + 4, 2, 2, T, hi, lo, q, a["x_qnorm"][layer], XHD ** -0.5, qT)
        o_hi, o_lo = m.split_pair(c, f"{nm}_o")
        cross_attend(m, f"{nm}_at", qT, kT, v[:, :, D:2 * D], o_hi, o_lo)
        linear_residual(m, f"{nm}_wo", first + 6, 2, [(o_hi, o_lo)])


def sgu_layer(m, layer, first):
    nc, a = m.nc, m.a
    NGR = SGW // GC
    KU = SGW // P
    with ExitStack() as c:
        uT = m.sb(c, "uT", [P, KU, S])
        v = m.sb(c, "sg_v", [P, T, SGW])
        wsT = m.sb(c, "sg_wsT", [P, SGG, P])
        bsr = m.sb(c, "sg_bs_row", [P, SGG, P])
        with ExitStack() as c2:
            hi, lo = m.split_pair(c2, "h_sg")
            norm_transpose(m, "mix1", m.x, a["norm_mix"][layer], T, hi, lo)
            m.phase()
            ws = m.sb(c2, "sgu_ws", [P, SGG, P])
            g = m.sb(c2, "sgu_g", [P, SGW])
            b = m.sb(c2, "sgu_b", [P, SGW])
            vsum = m.sb(c2, "sg_vsum", [P, T, NGR])
            nmean, var, root = (m.sb(c2, f"sg_{s}", [P, T]) for s in ("nmean", "var", "root"))
            junk = m.sb(c2, "sg_junk", [P, SGW])
            (read, small_in, ws_in, ws_masked, mean, squared, varied, rooted, dve_c, centred, gained, turned) = (
                m.psem(f"sg_{s}") for s in ("read", "small_in", "ws_in", "ws_masked", "mean", "squared", "varied",
                                           "rooted", "dve", "centred", "gained", "turned"))
            with nc.Block() as block:
                @block.sync
                def _(sp):
                    sp.dma_start(ws[:, :, :], a["sg_ws"][0].rearrange("g t s -> t g s")).then_inc(ws_in, 16)
                    m.load(sp, first + NGR)
                    sp.dma_start(g[:, :], a["sg_ln_g"][0].partition_broadcast(P)).then_inc(small_in, 16)
                    sp.dma_start(b[:, :], a["sg_ln_b"][0].partition_broadcast(P)).then_inc(small_in, 16)
                    sp.dma_start(bsr[:, :, :], a["sg_bs"][0].partition_broadcast(P)).then_inc(small_in, 16)
                    m.load(sp, first + 2 * NGR + 1)
                    sp.wait_ge(small_in, 48)

                @block.gpsimd
                def _(pool):
                    pool.wait_ge(ws_in, 16)
                    pool.affine_select(out=ws[:, :, :], in_=ws[:, :, :], compare_op=ALU.is_ge, fill=0.0, base=0,
                                       pattern=[[0, SGG], [-1, P]], channel_multiplier=1).then_inc(ws_masked, 1)
                    pool.wait_ge(small_in, 48)
                    for i in range(T):
                        pool.wait_ge(centred, i + 1)
                        pool.tensor_tensor(v[:, i, :], v[:, i, :], g[:, :], ALU.mult).then_inc(gained, 1)

                @block.tensor
                def _(pe):
                    for n in range(2 * NGR):
                        if n >= 2:
                            pe.wait_ge(read, 4 * (n - 1))
                        m.product(pe, first + n, n >= NGR, m.psum[4 * (n % 2):4 * (n % 2) + 4], hi, lo)
                    pe.wait_ge(read, 4 * (2 * NGR - 1))
                    pe.wait_ge(ws_masked, 1)
                    for q in range(2):
                        for j in range(4):
                            ins = pe.transpose(m.psum[q][:, j * P:(j + 1) * P], ws[:, 4 * q + j, :], m.ident[:, :])
                        ins.then_inc(turned, 1)

                @block.scalar
                def _(act):
                    m.split_hi(act, first)
                    for n in range(2 * NGR):
                        m.split_hi(act, first + n + 1)
                        if n == NGR:
                            act.wait_ge(mean, 1)
                            for i in range(T):
                                if i:
                                    act.wait_ge(squared, i)
                                act.activation(junk[:, :], v[:, i, :], ACT.Square, bias=nmean[:, i:i + 1],
                                               accum_out=var[:, i:i + 1]).then_inc(squared, 1)
                            act.wait_ge(varied, 1)
                            act.activation(root[:, :], var[:, :], ACT.Sqrt).then_inc(rooted, 1)
                        m.done(act, first + n)
                        for t in range(4):
                            ps = m.psum[4 * (n % 2) + t][:, :]
                            if n < NGR:
                                act.activation(v[:, t, n * GC:(n + 1) * GC], ps, ACT.Gelu_apprx_tanh,
                                               accum_out=vsum[:, t, n:n + 1]).then_inc(read, 1)
                            else:
                                act.activation(uT[:, 4 * (n - NGR) + t, :], ps, ACT.Gelu_apprx_tanh).then_inc(read, 1)
                    for q in range(2):
                        act.wait_ge(turned, q + 1)
                        act.activation(wsT[:, 4 * q:4 * q + 4, :], m.psum[q][:, :].rearrange("p (g t) -> p g t", g=4), ACT.Copy)

                @block.vector
                def _(dve):
                    link = Chain(dve, dve_c).link
                    for n in range(NGR + 1):
                        m.split_lo(dve, first + n)
                    dve.wait_ge(read, 4 * NGR)
                    link(dve.tensor_reduce(nmean[:, :], vsum[:, :, :], AX.X, ALU.add))
                    dve.tensor_scalar(nmean[:, :], nmean[:, :], -1.0 / SGW, None, ALU.mult).then_inc(mean, 1)
                    m.split_lo(dve, first + NGR + 1)
                    dve.wait_ge(squared, T)
                    dve.tensor_scalar(var[:, :], var[:, :], 1.0 / SGW, EPS, ALU.mult, ALU.add).then_inc(varied, 1)
                    dve.wait_ge(rooted, 1)
                    link(dve.reciprocal(var[:, :], root[:, :]))
                    for i in range(T):
                        dve.tensor_scalar(v[:, i, :], v[:, i, :], nmean[:, i:i + 1], var[:, i:i + 1], ALU.add, ALU.mult)\
                           .then_inc(centred, 1)
                    m.split_lo(dve, first + NGR + 2)
                    for i in range(2):
                        dve.wait_ge(gained, i + 1)
                        dve.tensor_tensor(v[:, i, :], v[:, i, :], b[:, :], ALU.add)
                    m.split_lo(dve, first + NGR + 3)
                    for i in range(2, T):
                        dve.wait_ge(gained, i + 1)
                        dve.tensor_tensor(v[:, i, :], v[:, i, :], b[:, :], ALU.add)
                    m.split_lo(dve, first + 2 * NGR)
        um_hi, um_lo = m.split_pair(c, "um", k=KU)
        m.phase()
        mixed, biased, gated, split, lo_out = (m.psem(f"sg_{s}") for s in ("mixed", "biased", "gated", "split", "lo_out"))
        with nc.Block() as block:
            @block.tensor
            def _(pe):
                for k in range(KU):
                    if k >= 8:
                        pe.wait_ge(biased, k - 7)
                    for i in range(T):
                        ins = pe.matmul(m.psum[k % 8][:, i * P:(i + 1) * P], v[:, i, k * P:(k + 1) * P],
                                        wsT[:, k * SGG // KU, :], start=True, stop=True)
                    ins.then_inc(mixed, 1)

            @block.vector
            def _(dve):
                for k in range(KU):
                    dve.wait_ge(mixed, k + 1)
                    dve.tensor_tensor(m.psum[k % 8][:, :].rearrange("p (i t) -> p i t", i=T),
                                      m.psum[k % 8][:, :].rearrange("p (i t) -> p i t", i=T),
                                      bsr[:, k * SGG // KU, :].unsqueeze(1).to_broadcast([P, T, P]), ALU.add).then_inc(split, 1)
                    dve.wait_ge(split, k + 1)
                    dve.tensor_tensor(uT[:, k, :], uT[:, k, :], m.psum[k % 8][:, :], ALU.mult).then_inc(biased, 1)

            @block.scalar
            def _(act):
                for k in range(KU):
                    act.wait_ge(biased, k + 1)
                    act.activation(um_hi[:, k, :], uT[:, k, :], ACT.Copy).then_inc(gated, 1)

            @block.gpsimd
            def _(pool):
                for k in range(KU):
                    pool.wait_ge(gated, k + 1)
                    pool.tensor_tensor(um_lo[:, k, :], uT[:, k, :], um_hi[:, k, :], ALU.subtract).then_inc(lo_out, 1)
                pool.wait_ge(lo_out, KU)
        linear_residual(m, "sg_out", first + 2 * NGR, 2, [(um_hi[:, 0:KD], um_lo[:, 0:KD]), (um_hi[:, KD:KU], um_lo[:, KD:KU])])


def moe_route(m, layer, hT, slot_i, tok_i, wgt, meta, idx_dram):
    m.phase()
    nc, a, nm = m.nc, m.a, f"r{layer}"
    NB = MAXB + 1
    with ExitStack() as t:
        def tile(name, shape, dt=F32):
            return m.sb(t, f"{nm}_{name}", shape, dt)
        rw = tile("rw", [P, KD, NE])
        rb = tile("rb", [P, NE])
        ones, before = tile("ones", [P, P]), tile("before", [P, P])
        e_row, g_row, b_row, thr = tile("e_row", [P, NE]), tile("g_row", [P, NG]), tile("b_row", [P, NB]), tile("thr", [P, T])
        lower = tile("lower", [P, NE, NE])
        zeros_i = tile("zeros_i", [P, SLOTS // P], I32)
        lg, pr = tile("lg", [P, T, NE]), tile("pr", [P, T, NE])
        mx, sm = tile("mx", [P, T]), tile("sm", [P, T])
        gm, ge = tile("gm", [P, T, NG]), tile("ge", [P, T, NG])
        gb, gi = tile("gb", [P, T]), tile("gi", [P, T])
        pm, cand = tile("pm", [P, T, NE]), tile("cand", [P, T, NE])
        top, ti = tile("top", [P, 2, T]), tile("ti", [P, 2, T])
        oh = tile("oh", [P, 2, T, NE])
        both = tile("both", [P, T, NE])
        cnt, nb, nbx = tile("cnt", [P, NE]), tile("nb", [P, NE]), tile("nbx", [P, NE, T])
        low, cum, off = tile("low", [P, NE, NE]), tile("cum", [P, NE]), tile("off", [P, NE])
        rank = tile("rank", [P, T, NE])
        sl, slot_f = tile("sl", [P, 2, T, NE]), tile("slot_f", [P, 2, T])
        be, ebf = tile("be", [P, NB, NE]), tile("ebf", [P, NB + 2])
        (ins_in, made, dve_c, logits, maxed, exped, counted, counts, zeroed) = (m.psem(f"{nm}_{s}") for s in (
            "ins_in", "made", "dve", "logits", "maxed", "exped", "counted", "counts", "zeroed"))
        with nc.Block() as block:
            @block.sync
            def _(sp):
                sp.dma_start(rw[:, :, :], a["router_w"].rearrange("(k p) e -> p k e", p=P)).then_inc(ins_in, 16)
                sp.dma_start(rb[:, :], a["router_b"].partition_broadcast(P)).then_inc(ins_in, 16)
                sp.wait_ge(made, 1)
                with nc.allow_non_contiguous_dma(reason="a small table of slots"):
                    sp.dma_start(idx_dram.rearrange("(b p) o -> p (b o)", p=P), zeros_i[:, :]).then_inc(zeroed, 16)
                sp.wait_ge(zeroed, 16)

            @block.gpsimd
            def _(pool):
                pool.memset(zeros_i[:, :], 0).then_inc(made, 1)
                pool.memset(ones[:, :], 1.0).then_inc(made, 1)
                pool.memset(before[:, :], 1.0).then_inc(made, 1)
                pool.memset(lower[:, :, :], 1.0).then_inc(made, 1)
                for row, n, base, step in ((e_row, NE, -NE, 1), (g_row, NG, -NG, 1), (b_row, NB, 0, 1), (thr, T, 0, P)):
                    pool.iota(row[:, :], pattern=[[step, n]], base=base, channel_multiplier=0,
                              allow_small_or_imprecise_dtypes=True).then_inc(made, 1)
                pool.iota(tok_i[:, :], pattern=[[P, T]], base=0, channel_multiplier=1).then_inc(made, 1)
                pool.wait_ge(made, 9)
                pool.affine_select(out=before[:, :], in_=before[:, :], compare_op=ALU.is_gt, fill=0.0, base=0,
                                   pattern=[[1, P]], channel_multiplier=-1).then_inc(made, 1)
                pool.affine_select(out=lower[:, :, :], in_=lower[:, :, :], compare_op=ALU.is_ge, fill=0.0, base=0,
                                   pattern=[[1, NE], [-1, NE]], channel_multiplier=0).then_inc(made, 1)
                pool.wait_ge(made, 11)

            @block.tensor
            def _(pe):
                pe.wait_ge(ins_in, 32)
                for i in range(T):
                    for k in range(KD):
                        ins = pe.matmul(m.psum[0][:, i * NE:(i + 1) * NE], hT[:, k, i * P:(i + 1) * P], rw[:, k, :],
                                        start=k == 0, stop=k == KD - 1)
                ins.then_inc(logits, 1)
                pe.wait_ge(made, 11)
                pe.wait_ge(counted, 1)
                for i in range(T):
                    for j in range(i + 1):
                        pe.matmul(m.psum[1][:, i * NE:(i + 1) * NE], before[:, :] if j == i else ones[:, :], both[:, j, :],
                                  start=j == 0, stop=j == i)
                for j in range(T):
                    ins = pe.matmul(m.psum[1][:, T * NE:(T + 1) * NE], ones[:, :], both[:, j, :], start=j == 0, stop=j == T - 1)
                ins.then_inc(counts, 1)

            @block.scalar
            def _(act):
                act.wait_ge(maxed, 1)
                act.activation(pr[:, :, :], lg[:, :, :], ACT.Exp).then_inc(exped, 1)

            @block.vector
            def _(dve):
                link = Chain(dve, dve_c).link

                def wide(x, n):
                    return x.unsqueeze(2).to_broadcast([P, T, n])

                def row(x, n):
                    return x[:, :].unsqueeze(1).to_broadcast([P, T, n])

                dve.wait_ge(ins_in, 32)
                dve.wait_ge(made, 11)
                dve.wait_ge(logits, 1)
                link(dve.tensor_tensor(lg[:, :, :], m.psum[0][:, 0:T * NE].rearrange("p (t e) -> p t e", e=NE), row(rb, NE), ALU.add))
                link(dve.tensor_reduce(mx[:, :], lg[:, :, :], AX.X, ALU.max))
                dve.tensor_tensor(lg[:, :, :], lg[:, :, :], wide(mx[:, :], NE), ALU.subtract).then_inc(maxed, 1)
                dve.wait_ge(exped, 1)
                link(dve.tensor_reduce(sm[:, :], pr[:, :, :], AX.X, ALU.add))
                link(dve.reciprocal(sm[:, :], sm[:, :]))
                link(dve.tensor_tensor(pr[:, :, :], pr[:, :, :], wide(sm[:, :], NE), ALU.mult))
                link(dve.tensor_reduce(gm[:, :, :], pr[:, :, :].rearrange("p t (g e) -> p t g e", e=EPG), AX.X, ALU.max))
                link(dve.tensor_reduce(gb[:, :], gm[:, :, :], AX.X, ALU.max))
                link(dve.tensor_tensor(ge[:, :, :], gm[:, :, :], wide(gb[:, :], NG), ALU.is_equal))
                link(dve.tensor_tensor(ge[:, :, :], ge[:, :, :], row(g_row, NG), ALU.mult))
                link(dve.tensor_reduce(gi[:, :], ge[:, :, :], AX.X, ALU.min))
                link(dve.tensor_tensor(ge[:, :, :], row(g_row, NG), wide(gi[:, :], NG), ALU.is_equal))
                for e in range(EPG):
                    ins = dve.tensor_scalar(cand[:, :, e::EPG], ge[:, :, :], 2.0, -2.0, ALU.mult, ALU.add)
                link(ins)
                link(dve.tensor_tensor(pm[:, :, :], pr[:, :, :], cand[:, :, :], ALU.add))
                for c in range(2):
                    link(dve.tensor_reduce(top[:, c, :], pm[:, :, :], AX.X, ALU.max))
                    link(dve.tensor_tensor(cand[:, :, :], pm[:, :, :], wide(top[:, c, :], NE), ALU.is_equal))
                    link(dve.tensor_tensor(cand[:, :, :], cand[:, :, :], row(e_row, NE), ALU.mult))
                    link(dve.tensor_reduce(ti[:, c, :], cand[:, :, :], AX.X, ALU.min))
                    link(dve.tensor_tensor(oh[:, c], row(e_row, NE), wide(ti[:, c, :], NE), ALU.is_equal))
                    if c == 0:
                        link(dve.scalar_tensor_tensor(out=pm[:, :, :], in0=oh[:, 0], scalar=-4.0, in1=pm[:, :, :],
                                                      op0=ALU.mult, op1=ALU.add))
                link(dve.tensor_tensor(sm[:, :], top[:, 0, :], top[:, 1, :], ALU.add))
                link(dve.reciprocal(sm[:, :], sm[:, :]))
                for c in range(2):
                    dve.tensor_tensor(wgt[:, c * T:(c + 1) * T], top[:, c, :], sm[:, :], ALU.mult)
                dve.tensor_tensor(both[:, :, :], oh[:, 0], oh[:, 1], ALU.add).then_inc(counted, 1)
                dve.wait_ge(counts, 1)
                link(dve.tensor_copy(cnt[:, :], m.psum[1][:, T * NE:(T + 1) * NE]))
                link(dve.tensor_tensor(nbx[:, :, :], cnt[:, :].unsqueeze(2).to_broadcast([P, NE, T]),
                                       thr[:, :].unsqueeze(1).to_broadcast([P, NE, T]), ALU.is_gt))
                link(dve.tensor_reduce(nb[:, :], nbx[:, :, :], AX.X, ALU.add))
                link(dve.tensor_tensor(low[:, :, :], lower[:, :, :], nb[:, :].unsqueeze(1).to_broadcast([P, NE, NE]), ALU.mult))
                link(dve.tensor_reduce(cum[:, :], low[:, :, :], AX.X, ALU.add))
                link(dve.tensor_tensor(off[:, :], cum[:, :], nb[:, :], ALU.subtract))
                link(dve.scalar_tensor_tensor(out=rank[:, :, :], in0=off[:, :].unsqueeze(1).to_broadcast([P, T, NE]), scalar=float(P),
                                              in1=m.psum[1][:, 0:T * NE].rearrange("p (t e) -> p t e", e=NE),
                                              op0=ALU.mult, op1=ALU.add))
                for c in range(2):
                    ins = dve.tensor_tensor(sl[:, c], oh[:, c], rank[:, :, :], ALU.mult)
                link(ins)
                for c in range(2):
                    ins = dve.tensor_reduce(slot_f[:, c, :], sl[:, c], AX.X, ALU.add)
                link(ins)
                dve.tensor_copy(slot_i[:, :], slot_f[:, :, :].rearrange("p c t -> p (c t)"))
                link(dve.tensor_tensor(be[:, :, :], b_row[:, :].unsqueeze(2).to_broadcast([P, NB, NE]),
                                       cum[:, :].unsqueeze(1).to_broadcast([P, NB, NE]), ALU.is_ge))
                link(dve.tensor_reduce(ebf[:, 0:NB], be[:, :, :], AX.X, ALU.add))
                dve.tensor_scalar(ebf[:, 0:NB], ebf[:, 0:NB], float(NE - 1), None, ALU.min)
                dve.tensor_copy(ebf[:, NB:NB + 1], cum[:, NE - 1:NE])
                link(dve.tensor_scalar(ebf[:, NB + 1:NB + 2], cum[:, NE - 1:NE], 2.0, None, ALU.subtract))
                link(dve.tensor_copy(meta[:, :], ebf[0:1, :]))


def moe_experts(m, layer, slot_i, tok_i, meta, h_dram, idx_dram, y_dram):
    m.phase()
    nc, a, nm = m.nc, m.a, f"e{layer}"
    NB = MAXB + 1
    CI, CO = 4, DE // P
    KC = KD // CI
    w_in = a["moe_w_in"][layer].rearrange("e d n -> (e d) n")
    w_out = a["moe_w_out"][layer].rearrange("e f n -> (e f) n")
    gate_ps, up_ps, turn_ps, act_ps, y_ps = m.psum[0], m.psum[1], m.psum[2:4], m.psum[4], m.psum[5:7]
    with ExitStack() as t:
        wi = [m.sb(t, f"{nm}_wi{q}", [P, KC, 2 * DE]) for q in range(CI)]
        wi_hi, wi_lo = ([m.sb(t, f"{nm}_wi_{s}{q}", [P, KC, 2 * DE], F32R) for q in range(CI)] for s in ("hi", "lo"))
        wo = [m.sb(t, f"{nm}_wo{f}", [P, D]) for f in range(CO)]
        wo_last = [m.sb(t, f"{nm}_wo_last{f}", [P, D]) for f in range(CO)]
        ix = m.sb(t, f"{nm}_ix", [P, 1], I32)
        hx = m.sb(t, f"{nm}_hx", [P, D])
        hx_hi, hx_lo = m.split_pair(t, f"{nm}_hx", n=P)
        sg = m.sb(t, f"{nm}_silu", [P, DE])
        au = m.sb(t, f"{nm}_act", [P, DE])
        auT = m.sb(t, f"{nm}_actT", [P, CO, P])
        y = m.sb(t, f"{nm}_y", [P, D])
        wi_in, wi_his, wi_los, wi_used = ([m.psem(f"{nm}_wi_{s}{q}") for q in range(CI)] for s in ("in", "hi", "lo", "used"))
        wo_in, wo_used = ([m.psem(f"{nm}_wo_{s}{f}") for f in range(CO)] for s in ("in", "used"))
        wo_last_in = [m.psem(f"{nm}_wo_last_in{f}") for f in range(CO)]
        passed = m.psem(f"{nm}_passed")
        scattered, ix_in, hx_in = (m.sem(f"{nm}_{s}") for s in ("scattered", "ix_in", "hx_in"))
        (h_turned, h_hi, h_lo, silued, multiplied, a_turned, aT_out, y_act, y_dve, stored) = (
            m.psem(f"{nm}_{s}") for s in ("h_turned", "h_hi", "h_lo", "silued", "multiplied",
                                          "a_turned", "aT_out", "y_act", "y_dve", "stored"))

        def blocks(engine):
            return engine.value_load(meta[0:1, NB:NB + 1], min_val=2 * S // P, max_val=MAXB)

        def before_last(engine):
            return engine.value_load(meta[0:1, NB + 1:NB + 2], min_val=2 * S // P - 2, max_val=MAXB - 2)

        with nc.Block() as block:
            @block.sync
            def _(sp):
                def expert(b):
                    return sp.value_load(meta[0:1, bass.ds(b, 1)], min_val=0, max_val=NE - 1)

                def load_in(e, q):
                    sp.dma_start(wi[q][:, :, :], w_in[bass.ds(e * D + q * KC * P, KC * P), :]
                                 .rearrange("(k p) n -> p k n", p=P)).then_inc(wi_in[q], 16)

                e0 = expert(0)
                for q in range(CI):
                    load_in(e0, q)
                last = blocks(sp) - 1
                with sp.Fori(0, last) as b:
                    e1 = expert(b + 1)
                    for q in range(CI):
                        sp.wait_ge(wi_los[q], b + 1)
                        load_in(e1, q)

            @block.gpsimd
            def _(pool):
                for c in range(2):
                    for i in range(T):
                        pool.indirect_dma_start(out=idx_dram, out_offset=bass.IndirectOffsetOnAxis(ap=slot_i[:, c * T + i:c * T + i + 1], axis=0),
                                                in_=tok_i[:, i:i + 1], in_offset=None).then_inc(scattered, 16)
                pool.wait_ge(scattered, 16 * 2 * T)
                nb = blocks(pool)
                with pool.Fori(0, nb + 1) as b:
                    pool.wait_ge(h_turned, b + 1)
                    pool.dma_start(ix[:, :], idx_dram[bass.ds(b * P, P), :]).then_inc(ix_in, 16)
                    pool.wait_ge(ix_in, b * 16 + 16)
                    pool.sem_inc(passed, 1)
                    pool.indirect_dma_start(out=hx[:, :], out_offset=None, in_=h_dram,
                                            in_offset=bass.IndirectOffsetOnAxis(ap=ix[:, 0:1], axis=0)).then_inc(hx_in, 16)
                pool.wait_ge(h_turned, nb + 2)
                pool.sem_inc(passed, 1)

            @block.tensor
            def _(pe):
                def turn_tokens(b):
                    pe.wait_ge(hx_in, b * 16 + 16)
                    for k in range(KD):
                        ins = pe.transpose(turn_ps[k // 4][:, (k % 4) * P:(k % 4 + 1) * P], hx[:, k * P:(k + 1) * P], m.ident[:, :])
                    ins.then_inc(h_turned, 1)

                def products(b):
                    pe.wait_ge(h_lo, b + 1)
                    for q in range(CI):
                        pe.wait_ge(wi_los[q], b + 1)
                        for kk in range(KC):
                            k = q * KC + kk
                            for term, (x, w) in enumerate(((hx_hi, wi_hi), (hx_hi, wi_lo), (hx_lo, wi_hi))):
                                start, stop = k == 0 and term == 0, k == KD - 1 and term == 2
                                pe.matmul(gate_ps[:, 0:DE], x[:, k, :], w[q][:, kk, 0:DE], start=start, stop=stop)
                                ins = pe.matmul(up_ps[:, 0:DE], x[:, k, :], w[q][:, kk, DE:2 * DE], start=start, stop=stop)
                        ins.then_inc(wi_used[q], 1)

                def turn_activations(b):
                    pe.wait_ge(multiplied, b + 1)
                    for f in range(CO):
                        ins = pe.transpose(act_ps[:, f * P:(f + 1) * P], au[:, f * P:(f + 1) * P], m.ident[:, :])
                    ins.then_inc(a_turned, 1)

                def outputs(b, last=False):
                    pe.wait_ge(aT_out, b + 1)
                    pe.wait_ge(y_act, b + 1)
                    pe.wait_ge(y_dve, b + 1)
                    for f in range(CO):
                        if last:
                            pe.wait_ge(wo_last_in[f], 16)
                        else:
                            pe.wait_ge(wo_in[f], b * 16 + 16)
                        w = wo_last[f] if last else wo[f]
                        for n in range(2):
                            ins = pe.matmul(y_ps[n][:, :], auT[:, f, :], w[:, n * GC:(n + 1) * GC], start=f == 0, stop=f == CO - 1)
                        ins.then_inc(wo_used[f], 1)

                pe.sem_inc(h_turned, 1)
                turn_tokens(0)
                products(0)
                turn_tokens(1)
                turn_activations(0)
                nb = blocks(pe)
                with pe.Fori(0, nb - 1) as b:
                    products(b + 1)
                    turn_tokens(b + 2)
                    outputs(b)
                    turn_activations(b + 1)
                outputs(nb - 1, last=True)

            @block.scalar
            def _(act):
                def keep_tokens(b):
                    act.wait_ge(h_turned, b + 2)
                    for j in range(2):
                        ins = act.activation(hx_hi[:, 4 * j:4 * j + 4, :], turn_ps[j][:, :].rearrange("p (k t) -> p k t", k=4), ACT.Copy)
                    ins.then_inc(h_hi, 1)

                def split_in(b, q):
                    act.wait_ge(wi_in[q], b * 16 + 16)
                    act.activation(wi_hi[q][:, :, :], wi[q][:, :, :], ACT.Copy).then_inc(wi_his[q], 1)

                def activate(b, more):
                    if more:
                        for q in range(CI - 1):
                            act.wait_ge(wi_used[q], b + 1)
                            split_in(b + 1, q)
                    act.wait_ge(wi_used[CI - 1], b + 1)
                    act.activation(sg[:, :], gate_ps[:, 0:DE], ACT.Silu).then_inc(silued, 1)
                    keep_tokens(b + 1)
                    if more:
                        split_in(b + 1, CI - 1)

                def copy_activations(b):
                    act.wait_ge(a_turned, b + 1)
                    act.activation(auT[:, :, :], act_ps[:, 0:DE].rearrange("p (f t) -> p f t", f=CO), ACT.Copy).then_inc(aT_out, 1)

                def load_out(b, to, landed):
                    e = act.value_load(meta[0:1, bass.ds(b, 1)], min_val=0, max_val=NE - 1)
                    for f in range(CO):
                        act.dma_start(to[f][:, :], w_out[bass.ds(e * DE + f * P, P), :]).then_inc(landed[f], 16)

                def finish(b):
                    act.wait_ge(wo_used[CO - 1], b + 1)
                    act.wait_ge(stored, b * 16 + 16)
                    act.activation(y[:, 0:GC], y_ps[0][:, :], ACT.Copy).then_inc(y_act, 1)
                    act.wait_ge(y_act, b + 2)
                    act.wait_ge(y_dve, b + 2)
                    act.dma_start(y_dram[bass.ds(b * P, P), :], y[:, :]).then_inc(stored, 16)

                act.sem_inc(y_act, 1)
                act.sem_inc(stored, 16)
                keep_tokens(0)
                for q in range(CI):
                    split_in(0, q)
                load_out(0, wo, wo_in)
                activate(0, more=True)
                n = before_last(act)
                with act.Fori(0, n) as b:
                    copy_activations(b)
                    activate(b + 1, more=True)
                    finish(b)
                    load_out(b + 1, wo, wo_in)
                load_out(n + 1, wo_last, wo_last_in)
                copy_activations(n)
                activate(n + 1, more=False)
                finish(n)
                copy_activations(n + 1)
                finish(n + 1)
                act.wait_ge(stored, n * 16 + 48)
                act.sem_inc(passed, 1)

            @block.vector
            def _(dve):
                def keep_tokens(b):
                    dve.wait_ge(h_hi, b + 1)
                    for j in range(2):
                        ins = dve.tensor_tensor(hx_lo[:, 4 * j:4 * j + 4, :], turn_ps[j][:, :].rearrange("p (k t) -> p k t", k=4),
                                                hx_hi[:, 4 * j:4 * j + 4, :], ALU.subtract)
                    ins.then_inc(h_lo, 1)

                def split_in(b, q):
                    dve.wait_ge(wi_his[q], b + 1)
                    dve.tensor_tensor(wi_lo[q][:, :, :], wi[q][:, :, :], wi_hi[q][:, :, :], ALU.subtract).then_inc(wi_los[q], 1)

                def multiply(b, more):
                    if more:
                        for q in range(CI // 2):
                            split_in(b + 1, q)
                    dve.wait_ge(silued, b + 1)
                    dve.tensor_tensor(au[:, :], up_ps[:, 0:DE], sg[:, :], ALU.mult).then_inc(multiplied, 1)
                    keep_tokens(b + 1)
                    if more:
                        for q in range(CI // 2, CI):
                            split_in(b + 1, q)

                def finish(b):
                    dve.wait_ge(wo_used[CO - 1], b + 1)
                    dve.wait_ge(stored, b * 16 + 16)
                    dve.tensor_copy(y[:, GC:D], y_ps[1][:, :]).then_inc(y_dve, 1)

                dve.sem_inc(y_dve, 1)
                keep_tokens(0)
                for q in range(CI):
                    split_in(0, q)
                multiply(0, more=True)
                n = before_last(dve)
                with dve.Fori(0, n) as b:
                    multiply(b + 1, more=True)
                    finish(b)
                multiply(n + 1, more=False)
                finish(n)
                finish(n + 1)


def moe_combine(m, layer, slot_i, wgt, y_dram):
    m.phase()
    nc = m.nc
    with ExitStack() as t:
        yg = m.sb(t, f"c{layer}_y", [P, 2 * T, D])
        got = [m.sem(f"c{layer}_got{j}") for j in range(2 * T)]
        added = m.psem(f"c{layer}_added")
        order = [c * T + i for i in range(T) for c in range(2)]
        with nc.Block() as block:
            @block.gpsimd
            def _(pool):
                for j in order:
                    pool.indirect_dma_start(out=yg[:, j, :], out_offset=None, in_=y_dram,
                                            in_offset=bass.IndirectOffsetOnAxis(ap=slot_i[:, j:j + 1], axis=0)).then_inc(got[j], 16)

            @block.vector
            def _(dve):
                for n, j in enumerate(order):
                    dve.wait_ge(got[j], 16)
                    if n:
                        dve.wait_ge(added, n)
                    dve.scalar_tensor_tensor(out=m.x[:, j % T, :], in0=yg[:, j, :], scalar=wgt[:, j:j + 1],
                                             in1=m.x[:, j % T, :], op0=ALU.mult, op1=ALU.add).then_inc(added, 1)


def moe(m, layer):
    nm = f"moe{layer}"
    h_dram = m.nc.dram_tensor(f"{nm}_h", [S, D], F32).ap()
    idx_dram = m.nc.dram_tensor(f"{nm}_idx", [SLOTS, 1], I32).ap()
    y_dram = m.y_dram
    with ExitStack() as c:
        slot_i = m.sb(c, f"{nm}_slot", [P, 2 * T], I32)
        tok_i = m.sb(c, f"{nm}_tok", [P, T], I32)
        wgt = m.sb(c, f"{nm}_wgt", [P, 2 * T])
        meta = m.sb(c, f"{nm}_meta", [1, MAXB + 3], I32)
        with ExitStack() as c2:
            hT = m.sb(c2, f"{nm}_hT", [P, KD, S])
            norm_transpose(m, nm, m.x, m.a["norm_ffn"][layer], T, None, None, plain=hT, h_dram=h_dram)
            moe_route(m, layer, hT, slot_i, tok_i, wgt, meta, idx_dram)
        moe_experts(m, layer, slot_i, tok_i, meta, h_dram, idx_dram, y_dram)
        moe_combine(m, layer, slot_i, wgt, y_dram)


def build_trunk(nc, a, out):
    with ExitStack() as ctx:
        m = Core(nc, ctx, a)
        two = [(0, GC), (GC, 2 * GC)]
        four = [(n * GC, (n + 1) * GC) for n in range(4)]
        eight = [(n * GC, (n + 1) * GC) for n in range(8)]
        at = {}

        def add(name, w, cols):
            at[name] = len(m.groups)
            m.add_linear(w, cols)

        add("hyb", a["hyb_w_in"][0], [(O_QA, O_KC), (O_KS, O_GA), (O_KC, O_KS), (O_QB, O_VB), (O_VB, O_AL),
                                      (O_R, O_END)])
        m.add_group(a["hyb_w_in"][0], [(O_GA, O_GA + AL_AT), (O_AL, O_R)])
        add("hyb_out", a["hyb_w_out"][0], two)
        for layer in range(DEPTH):
            if layer == 1:
                add("sgu", a["sg_w_in"][0], eight[4:] + eight[:4])
                add("sgu_out", a["sg_w_out"][0], two)
            add(f"x{layer}", a["x_wkv"][layer], four)
            add(f"xq{layer}", a["x_wq"][layer], two)
            add(f"xo{layer}", a["x_wo"][layer], two)
        setup(m)
        for layer in range(DEPTH):
            if layer == 0:
                hybrid_layer(m, at["hyb"])
            else:
                sgu_layer(m, layer, at["sgu"])
            cross_attention(m, layer, at[f"x{layer}"])
            moe(m, layer)
        store_x(m, out)


_INS = ["x", "mem", "positions", "norm_mix", "norm_xattn", "norm_mem", "norm_ffn", "hyb_w_in", "hyb_w_out",
        "nsa_qnorm", "nsa_knorm", "nsa_cmp_pe", "nsa_cmp_w1", "nsa_cmp_w2", "nsa_gate_b", "gla_wa2", "gla_ba",
        "gla_onorm", "sg_w_in", "sg_ln_g", "sg_ln_b", "sg_ws", "sg_bs", "sg_w_out", "x_wq", "x_wkv", "x_wo",
        "x_qnorm", "x_knorm", "router_w", "router_b", "moe_w_in", "moe_w_out"]


def kernel(**inputs):
    import concourse.bacc as _bacc
    from concourse.bass_utils import run_bass_kernel_spmd as _run

    nc = _bacc.Bacc("TRN2", target_bir_lowering=False, num_devices=1)
    arrays, args = {}, {}
    for name in _INS:
        arrays[f"in_{name}"] = np.ascontiguousarray(inputs[name])
        args[name] = nc.dram_tensor(f"in_{name}", arrays[f"in_{name}"].shape,
                                    mybir.dt.from_np(arrays[f"in_{name}"].dtype), kind="ExternalInput").ap()
    half = HD // 2
    arrays["rope_freq"] = (np.float32(10000.0) ** (-np.arange(half, dtype=np.float32) / half)).astype(np.float32)
    args["rope_freq"] = nc.dram_tensor("rope_freq", (half,), F32, kind="ExternalInput").ap()
    out = nc.dram_tensor("out_x", (1, S, D), F32, kind="ExternalOutput").ap()
    build_trunk(nc, args, out)
    r = _run(nc, [arrays], core_ids=[0])
    return r.results[0]["out_x"]
```
